# Optimizing a Trainium2 kernel written in Bass

```python
import jax, jax.numpy as jnp
from jax import lax
import numpy as np
import math

D_MODEL = 1024
BATCH = 1
SEQ = 256
DEPTH = 1

POOL_WINDOWS = (2, 4, 8, 16)
POOL_GROUPS = 4
POOL_GC = 64
POOL_W = POOL_GROUPS * POOL_GC
M_HEADS = 4
M_DH = 64
M_W = M_HEADS * M_DH
M_CONV = 4
M_CHUNK = 128
A_HEADS = 8
A_DH = 64
A_W = A_HEADS * A_DH
MOBA_BLOCK = 256
MOBA_TOPK = 3
Q_BLOCK = 128
MIX_W = POOL_W + M_W + A_W
OFF_MQK = POOL_W
OFF_MV = OFF_MQK + 2 * M_W
OFF_MO = OFF_MV + M_W
OFF_MI = OFF_MO + M_W
OFF_MF = OFF_MI + M_HEADS
OFF_A = OFF_MF + M_HEADS
IN_W = OFF_A + 3 * A_W
D_FF = 2816
FFN_CONV = 3
EPS = 1e-6


def rmsnorm(x, g):
    xf = x.astype(jnp.float32)
    y = xf * lax.rsqrt(jnp.mean(xf * xf, axis=-1, keepdims=True) + EPS) * g.astype(jnp.float32)
    return y.astype(x.dtype)

def causal_dwconv(x, w):
    K = w.shape[0]
    S = x.shape[1]
    xp = jnp.pad(x, ((0, 0), (K - 1, 0), (0, 0)))
    y = xp[:, 0:S] * w[0]
    for j in range(1, K):
        y = y + xp[:, j:j + S] * w[j]
    return y

def pool_mixer(xp, w_pool, scale):
    B, S, _ = xp.shape
    xg = xp.astype(jnp.float32).reshape(B, S, POOL_GROUPS, POOL_GC)
    cs = jnp.concatenate([jnp.zeros((B, 1, POOL_GROUPS, POOL_GC), jnp.float32), jnp.cumsum(xg, axis=1)], axis=1)
    t = jnp.arange(S)
    outs = []
    for g, w in enumerate(POOL_WINDOWS):
        lo = jnp.maximum(t + 1 - w, 0)
        cnt = (t + 1 - lo).astype(jnp.float32)
        win_sum = cs[:, 1:, g] - cs[:, lo, g]
        outs.append(win_sum / cnt[None, :, None] - xg[:, :, g])
    d = jnp.stack(outs, axis=2)
    y = jnp.einsum('bsgc,gcd->bsgd', d, w_pool.astype(jnp.float32)).reshape(B, S, POOL_W)
    return y * scale.astype(jnp.float32)

def mlstm_chunkwise(q, k, v, i_pre, f_pre):
    B, S, H, Dh = q.shape
    L = M_CHUNK
    NC = S // L
    def ch5(t):
        return t.reshape(B, NC, L, H, Dh).transpose(1, 0, 3, 2, 4)
    def ch4(t):
        return t.reshape(B, NC, L, H).transpose(1, 0, 3, 2)
    logf = jax.nn.log_sigmoid(f_pre)
    causal = jnp.tril(jnp.ones((L, L), dtype=bool))

    def step(carry, inp):
        C, n, m = carry
        qc, kc, vc, ic, lf = inp
        g = jnp.cumsum(lf, axis=-1)
        logd = jnp.where(causal, g[..., :, None] - g[..., None, :] + ic[..., None, :], -jnp.inf)
        inter = g + m[..., None]
        mt = jnp.maximum(inter, jnp.max(logd, axis=-1))
        w = jnp.einsum('bhtd,bhsd->bhts', qc, kc) * jnp.exp(logd - mt[..., None])
        a = jnp.exp(inter - mt)
        num = jnp.einsum('bhts,bhse->bhte', w, vc) + a[..., None] * jnp.einsum('bhtd,bhde->bhte', qc, C)
        den = jnp.sum(w, axis=-1) + a * jnp.einsum('bhtd,bhd->bht', qc, n)
        hc = num / jnp.maximum(jnp.abs(den), jnp.exp(-mt))[..., None]
        gl = g[..., -1]
        wl = gl[..., None] - g + ic
        m_new = jnp.maximum(gl + m, jnp.max(wl, axis=-1))
        wk = jnp.exp(wl - m_new[..., None])
        dec = jnp.exp(gl + m - m_new)
        C = dec[..., None, None] * C + jnp.einsum('bhs,bhsd,bhse->bhde', wk, kc, vc)
        n = dec[..., None] * n + jnp.einsum('bhs,bhsd->bhd', wk, kc)
        return (C, n, m_new), hc

    init = (jnp.zeros((B, H, Dh, Dh), jnp.float32), jnp.zeros((B, H, Dh), jnp.float32), jnp.zeros((B, H), jnp.float32))
    _, hs = lax.scan(step, init, (ch5(q), ch5(k), ch5(v), ch4(i_pre), ch4(logf)))
    return hs.transpose(1, 0, 3, 2, 4).reshape(B, S, H, Dh)

def moba_attention(q, k, v):
    q = q.astype(jnp.float32).transpose(0, 2, 1, 3)
    k = k.astype(jnp.float32).transpose(0, 2, 1, 3)
    v = v.astype(jnp.float32).transpose(0, 2, 1, 3)
    B, H, S, Dh = q.shape
    NB = -(-S // MOBA_BLOCK)
    pad = NB * MOBA_BLOCK - S
    kp = jnp.pad(k, ((0, 0), (0, 0), (0, pad), (0, 0)))
    vp = jnp.pad(v, ((0, 0), (0, 0), (0, pad), (0, 0)))
    kb = kp.reshape(B, H, NB, MOBA_BLOCK, Dh)
    vb = vp.reshape(B, H, NB, MOBA_BLOCK, Dh)
    kmean = jnp.mean(kb, axis=3)
    topk = min(MOBA_TOPK, NB)
    NQ = S // Q_BLOCK
    scale = A_DH ** -0.5
    qs = q.reshape(B, H, NQ, Q_BLOCK, Dh).transpose(2, 0, 1, 3, 4)
    bi = jnp.arange(B)[:, None, None, None]
    hi = jnp.arange(H)[None, :, None, None]
    blk_ids = jnp.arange(NB)

    def one(args):
        qi, ci = args
        q0 = ci * Q_BLOCK
        own = q0 // MOBA_BLOCK
        gate = jnp.einsum('bhqd,bhnd->bhqn', qi, kmean)
        gate = jnp.where((blk_ids < own)[None, None, None, :], gate, -jnp.inf)
        gval, gidx = lax.top_k(gate, topk)
        valid = jnp.isfinite(gval)
        ksel = kb[bi, hi, gidx]
        vsel = vb[bi, hi, gidx]
        s_sel = jnp.einsum('bhqd,bhqjkd->bhqjk', qi, ksel) * scale
        s_sel = jnp.where(valid[..., None], s_sel, -jnp.inf).reshape(B, H, Q_BLOCK, topk * MOBA_BLOCK)
        k_own = lax.dynamic_slice_in_dim(kp, own * MOBA_BLOCK, MOBA_BLOCK, axis=2)
        v_own = lax.dynamic_slice_in_dim(vp, own * MOBA_BLOCK, MOBA_BLOCK, axis=2)
        s_own = jnp.einsum('bhqd,bhkd->bhqk', qi, k_own) * scale
        kpos = own * MOBA_BLOCK + jnp.arange(MOBA_BLOCK)
        qpos = q0 + jnp.arange(Q_BLOCK)
        s_own = jnp.where((kpos[None, :] <= qpos[:, None])[None, None], s_own, -jnp.inf)
        p = jax.nn.softmax(jnp.concatenate([s_sel, s_own], axis=-1), axis=-1)
        p_sel = p[..., :topk * MOBA_BLOCK].reshape(B, H, Q_BLOCK, topk, MOBA_BLOCK)
        p_own = p[..., topk * MOBA_BLOCK:]
        return jnp.einsum('bhqjk,bhqjkd->bhqd', p_sel, vsel) + jnp.einsum('bhqk,bhkd->bhqd', p_own, v_own)

    outs = lax.map(one, (qs, jnp.arange(NQ)))
    return outs.transpose(1, 0, 3, 2, 4).reshape(B, S, H, Dh)

def first_inputs(seed: int = 0) -> dict:
    key = jax.random.key(seed)
    ks = jax.random.split(key, 18)
    nrm = jax.random.normal
    f32 = jnp.float32
    return {
        'x': nrm(ks[0], (BATCH, SEQ, D_MODEL), f32),
        'ln1_g': 1.0 + 0.02 * nrm(ks[1], (DEPTH, D_MODEL), f32),
        'w_in': nrm(ks[2], (DEPTH, D_MODEL, IN_W), f32) * D_MODEL ** -0.5,
        'pool_w': nrm(ks[3], (DEPTH, POOL_GROUPS, POOL_GC, POOL_GC), f32) * POOL_GC ** -0.5,
        'pool_scale': 1.0 + 0.1 * nrm(ks[4], (DEPTH, POOL_W), f32),
        'm_conv': nrm(ks[5], (DEPTH, M_CONV, 2 * M_W), f32) * M_CONV ** -0.5,
        'm_b_i': 0.1 * nrm(ks[6], (DEPTH, M_HEADS), f32),
        'm_b_f': jnp.linspace(3.0, 6.0, M_HEADS, dtype=f32)[None, :] + 0.01 * nrm(ks[7], (DEPTH, M_HEADS), f32),
        'm_norm_g': 1.0 + 0.02 * nrm(ks[8], (DEPTH, M_W), f32),
        'a_q_g': 1.0 + 0.02 * nrm(ks[9], (DEPTH, A_DH), f32),
        'a_k_g': 1.0 + 0.02 * nrm(ks[10], (DEPTH, A_DH), f32),
        'w_out': nrm(ks[11], (DEPTH, MIX_W, D_MODEL), f32) * MIX_W ** -0.5,
        'ln2_g': 1.0 + 0.02 * nrm(ks[12], (DEPTH, D_MODEL), f32),
        'w_up': nrm(ks[13], (DEPTH, D_MODEL, 2 * D_FF), f32) * D_MODEL ** -0.5,
        'ffn_conv': nrm(ks[14], (DEPTH, FFN_CONV, 2 * D_FF), f32) * FFN_CONV ** -0.5,
        'w_down': nrm(ks[15], (DEPTH, D_FF, D_MODEL), f32) * D_FF ** -0.5,
    }

def first_block(x, ln1_g, w_in, pool_w, pool_scale, m_conv, m_b_i, m_b_f, m_norm_g,
              a_q_g, a_k_g, w_out, ln2_g, w_up, ffn_conv, w_down):
    B, S, _ = x.shape
    for l in range(DEPTH):
        h = rmsnorm(x, ln1_g[l])
        z = h @ w_in[l]
        po = pool_mixer(z[..., :OFF_MQK], pool_w[l], pool_scale[l])
        qk = jax.nn.silu(causal_dwconv(z[..., OFF_MQK:OFF_MV], m_conv[l])).astype(jnp.float32)
        mq = qk[..., :M_W].reshape(B, S, M_HEADS, M_DH)
        mk = qk[..., M_W:].reshape(B, S, M_HEADS, M_DH) * (M_DH ** -0.5)
        mv = z[..., OFF_MV:OFF_MO].astype(jnp.float32).reshape(B, S, M_HEADS, M_DH)
        mo = jax.nn.sigmoid(z[..., OFF_MO:OFF_MI])
        mi = (z[..., OFF_MI:OFF_MF] + m_b_i[l]).astype(jnp.float32)
        mf = (z[..., OFF_MF:OFF_A] + m_b_f[l]).astype(jnp.float32)
        hm = mlstm_chunkwise(mq, mk, mv, mi, mf)
        hm = rmsnorm(hm, m_norm_g[l].reshape(M_HEADS, M_DH)).reshape(B, S, M_W).astype(x.dtype) * mo
        aq = rmsnorm(z[..., OFF_A:OFF_A + A_W].reshape(B, S, A_HEADS, A_DH), a_q_g[l])
        ak = rmsnorm(z[..., OFF_A + A_W:OFF_A + 2 * A_W].reshape(B, S, A_HEADS, A_DH), a_k_g[l])
        av = z[..., OFF_A + 2 * A_W:].reshape(B, S, A_HEADS, A_DH)
        ao = moba_attention(aq, ak, av).reshape(B, S, A_W)
        mix = jnp.concatenate([po.astype(x.dtype), hm, ao.astype(x.dtype)], axis=-1)
        x = x + mix @ w_out[l]
        h2 = rmsnorm(x, ln2_g[l])
        u = causal_dwconv(h2 @ w_up[l], ffn_conv[l])
        x = x + (jax.nn.silu(u[..., :D_FF]) * u[..., D_FF:]) @ w_down[l]
    return x


DEPTH_2 = 2

N_MIXERS = 3
REL_BUCKETS = 32
REL_EXACT = REL_BUCKETS // 2
REL_MAX_DIST = 128
ATTN_HEADS = 16
HEAD_DIM = D_MODEL // ATTN_HEADS
NSA_KV_HEADS = 4
NSA_QPG = ATTN_HEADS // NSA_KV_HEADS
CMP_STRIDE = 16
CMP_LEN = 2 * CMP_STRIDE
CMP_HIDDEN = 2 * HEAD_DIM
SEL_BLOCK = 64
SEL_COUNT = 16
NSA_WINDOW = 512
NSA_QBLOCK = 64
NSA_IN = ATTN_HEADS * HEAD_DIM + 6 * NSA_KV_HEADS * HEAD_DIM + 3 * ATTN_HEADS
HGRN_HEADS = 8
HGRN_KDIM = D_MODEL // HGRN_HEADS
HGRN_VDIM = D_MODEL // HGRN_HEADS
HGRN_CHUNK = 64
SWA_KV_HEADS = 2
SWA_QPG = ATTN_HEADS // SWA_KV_HEADS
SWA_WINDOW = 128
SWA_BLOCK = SWA_WINDOW
SWA_IN = ATTN_HEADS * HEAD_DIM + 2 * SWA_KV_HEADS * HEAD_DIM
LN_EPS = 1e-5
RMS_EPS = 1e-6
NEG_INF = -1e30
N_NSA = len(range(0, DEPTH_2, N_MIXERS))
N_HGRN = len(range(1, DEPTH_2, N_MIXERS))
N_SWA = len(range(2, DEPTH_2, N_MIXERS))


F32 = jnp.float32

def _layer_norm(x, g, b):
    xf = x.astype(F32)
    mu = jnp.mean(xf, axis=-1, keepdims=True)
    xc = xf - mu
    var = jnp.mean(xc * xc, axis=-1, keepdims=True)
    return (xc * lax.rsqrt(var + LN_EPS) * g.astype(F32) + b.astype(F32)).astype(x.dtype)

def _swiglu(x, w_gate, w_up, w_down):
    return (jax.nn.silu(x @ w_gate) * (x @ w_up)) @ w_down

def _t5_bucket(dist):
    n = jnp.maximum(dist, 0)
    nf = jnp.maximum(n, 1).astype(F32)
    large = REL_EXACT + (jnp.log(nf / REL_EXACT) / math.log(REL_MAX_DIST / REL_EXACT)
                         * (REL_BUCKETS - REL_EXACT)).astype(jnp.int32)
    return jnp.where(n < REL_EXACT, n, jnp.minimum(large, REL_BUCKETS - 1))

def _rel_bias(table, dist):
    return jnp.moveaxis(table[_t5_bucket(dist)], -1, 0).astype(F32)

def _masked_softmax(logits, valid):
    p = jax.nn.softmax(jnp.where(valid, logits.astype(F32), NEG_INF), axis=-1)
    return jnp.where(valid, p, 0.0)

def _lower_bounds(lb_param):
    sm = jax.nn.softmax(lb_param.astype(F32), axis=0)
    return jnp.cumsum(sm, axis=0) - sm[0]

def _nsa(x, w_in, w_out, cmp_pos, cmp_w1, cmp_w2, rel_bias):
    B, T, _ = x.shape
    dt = x.dtype
    G, Q, Dh = NSA_KV_HEADS, NSA_QPG, HEAD_DIM
    n_cmp = T // CMP_STRIDE - 1
    n_blk = T // SEL_BLOCK
    n_sel = min(SEL_COUNT, n_blk)
    n_qb = T // NSA_QBLOCK
    scale = Dh ** -0.5
    kvw = G * Dh
    h = x @ w_in
    sizes = [ATTN_HEADS * Dh] + [kvw] * 6
    q, k_c, v_c, k_s, v_s, k_w, v_w, gate = jnp.split(h, np.cumsum(sizes).tolist(), axis=-1)

    def heads(z):
        return z.reshape(B, T, G, Dh)

    def compress(z, pos, w1, w2):
        ch = heads(z).reshape(B, T // CMP_STRIDE, CMP_STRIDE, G, Dh)
        blk = jnp.concatenate([ch[:, :-1], ch[:, 1:]], axis=2) + pos[:, None, :]
        hid = jax.nn.gelu(jnp.einsum('bnlgd,lde->bnge', blk, w1))
        return jnp.einsum('bnge,ed->bgnd', hid, w2)

    kc = compress(k_c, cmp_pos[0], cmp_w1[0], cmp_w2[0])
    vc = compress(v_c, cmp_pos[1], cmp_w1[1], cmp_w2[1])
    cmp_end = CMP_STRIDE * jnp.arange(n_cmp, dtype=jnp.int32) + CMP_LEN - 1
    ci = np.arange(n_cmp)[:, None]
    bj = np.arange(n_blk)[None, :]
    overlap = jnp.asarray(((CMP_STRIDE * ci < SEL_BLOCK * (bj + 1)) &
                           (CMP_STRIDE * ci + CMP_LEN > SEL_BLOCK * bj)).astype(np.float32))

    def sel_blocks(z):
        return heads(z).reshape(B, n_blk, SEL_BLOCK, G, Dh).transpose(0, 3, 1, 2, 4)

    ks, vs = sel_blocks(k_s), sel_blocks(v_s)

    def win_keys(z):
        return jnp.pad(heads(z).transpose(0, 2, 1, 3), ((0, 0), (0, 0), (NSA_WINDOW, 0), (0, 0)))

    kw, vw = win_keys(k_w), win_keys(v_w)
    q_blocks = q.reshape(B, n_qb, NSA_QBLOCK, G, Q, Dh).transpose(1, 0, 3, 4, 2, 5)
    g_blocks = jax.nn.sigmoid(gate.astype(F32)).reshape(B, n_qb, NSA_QBLOCK, G, Q, 3).transpose(1, 0, 3, 4, 2, 5)
    bi = jnp.arange(B)[:, None, None, None]
    gi = jnp.arange(G)[None, :, None, None]
    tab_g = rel_bias.reshape(REL_BUCKETS, G, Q).transpose(1, 0, 2)
    blk_ids = jnp.arange(n_blk, dtype=jnp.int32)
    tok_in_blk = jnp.arange(SEL_BLOCK, dtype=jnp.int32)
    win_off = jnp.arange(NSA_WINDOW + NSA_QBLOCK, dtype=jnp.int32)

    def block(args):
        qb, gb, qi = args
        t = qi * NSA_QBLOCK + jnp.arange(NSA_QBLOCK, dtype=jnp.int32)
        d_c = t[:, None] - cmp_end[None, :]
        l_c = (jnp.einsum('bgqtd,bgnd->bgqtn', qb, kc).astype(F32) * scale
               + _rel_bias(rel_bias, d_c).reshape(G, Q, NSA_QBLOCK, n_cmp))
        p_c = _masked_softmax(l_c, d_c >= 0)
        o_c = jnp.einsum('bgqtn,bgnd->bgqtd', p_c.astype(dt), vc)
        imp = jnp.einsum('bgqtn,nj->bgtj', p_c, overlap)
        cur = (t // SEL_BLOCK)[:, None]
        forced = (blk_ids == 0) | (blk_ids == cur) | (blk_ids == cur - 1)
        imp = jnp.where(blk_ids > cur, -1e9, jnp.where(forced, 1e9, imp))
        _, idx = lax.top_k(imp, n_sel)
        k_g = ks[bi, gi, idx].reshape(B, G, NSA_QBLOCK, n_sel * SEL_BLOCK, Dh)
        v_g = vs[bi, gi, idx].reshape(B, G, NSA_QBLOCK, n_sel * SEL_BLOCK, Dh)
        pos = (idx[..., None] * SEL_BLOCK + tok_in_blk).reshape(B, G, NSA_QBLOCK, n_sel * SEL_BLOCK)
        d_s = t[:, None] - pos
        b_s = tab_g[gi, _t5_bucket(d_s)].transpose(0, 1, 4, 2, 3).astype(F32)
        l_s = jnp.einsum('bgqtd,bgtsd->bgqts', qb, k_g).astype(F32) * scale + b_s
        p_s = _masked_softmax(l_s, (d_s >= 0)[:, :, None])
        o_s = jnp.einsum('bgqts,bgtsd->bgqtd', p_s.astype(dt), v_g)
        start = qi * NSA_QBLOCK
        k_wb = lax.dynamic_slice_in_dim(kw, start, NSA_WINDOW + NSA_QBLOCK, axis=2)
        v_wb = lax.dynamic_slice_in_dim(vw, start, NSA_WINDOW + NSA_QBLOCK, axis=2)
        s_abs = start - NSA_WINDOW + win_off
        d_w = t[:, None] - s_abs[None, :]
        valid_w = (d_w >= 0) & (d_w < NSA_WINDOW) & (s_abs >= 0)[None, :]
        l_w = (jnp.einsum('bgqtd,bgsd->bgqts', qb, k_wb).astype(F32) * scale
               + _rel_bias(rel_bias, d_w).reshape(G, Q, NSA_QBLOCK, NSA_WINDOW + NSA_QBLOCK))
        p_w = _masked_softmax(l_w, valid_w)
        o_w = jnp.einsum('bgqts,bgsd->bgqtd', p_w.astype(dt), v_wb)
        return (gb[..., 0:1] * o_c + gb[..., 1:2] * o_s + gb[..., 2:3] * o_w).astype(dt)

    o = lax.map(block, (q_blocks, g_blocks, jnp.arange(n_qb, dtype=jnp.int32)))
    o = o.transpose(1, 0, 4, 2, 3, 5).reshape(B, T, D_MODEL)
    return o @ w_out

def _hgrn2(x, w_in, w_out, norm_gain, lb):
    B, T, _ = x.shape
    H, K, V, C = HGRN_HEADS, HGRN_KDIM, HGRN_VDIM, HGRN_CHUNK
    n_ch = T // C
    h = (x @ w_in).astype(F32)
    zq, zf, zi, zg = jnp.split(h, 4, axis=-1)
    lbf = lb.astype(F32)
    q = jax.nn.silu(zq)
    log_f = jnp.logaddexp(jnp.log(lbf), jnp.log1p(-lbf) + jax.nn.log_sigmoid(zf))
    k = (1.0 - lbf) * jax.nn.sigmoid(-zf)

    def chunks(z, d):
        return z.reshape(B, n_ch, C, H, d).transpose(1, 0, 3, 2, 4)

    causal = jnp.tril(jnp.ones((C, C), dtype=bool))[None, None, :, :, None]

    def step(S, inp):
        qc, kc, vc, gc = inp
        bcum = jnp.cumsum(gc, axis=2)
        o_inter = jnp.einsum('bhck,bhkv->bhcv', qc * jnp.exp(bcum), S)
        diff = jnp.where(causal, bcum[:, :, :, None, :] - bcum[:, :, None, :, :], -jnp.inf)
        a = jnp.einsum('bhtk,bhsk,bhtsk->bhts', qc, kc, jnp.exp(diff))
        o_intra = jnp.einsum('bhts,bhsv->bhtv', a, vc)
        b_last = bcum[:, :, -1]
        S_new = (jnp.exp(b_last)[..., None] * S
                 + jnp.einsum('bhsk,bhsv->bhkv', kc * jnp.exp(b_last[:, :, None] - bcum), vc))
        return S_new, o_inter + o_intra

    S0 = jnp.zeros((B, H, K, V), F32)
    _, o = lax.scan(step, S0, (chunks(q, K), chunks(k, K), chunks(zi, V), chunks(log_f, K)))
    o = o.transpose(1, 0, 3, 2, 4).reshape(B, T, H, V)
    o = o * lax.rsqrt(jnp.mean(o * o, axis=-1, keepdims=True) + RMS_EPS) * norm_gain.astype(F32)
    o = o * jax.nn.silu(zg.reshape(B, T, H, V))
    return o.reshape(B, T, D_MODEL).astype(x.dtype) @ w_out

def _swa(x, w_in, w_out, sinks, rel_bias):
    B, T, _ = x.shape
    nb = T // SWA_BLOCK
    Kv, Q, Dh, L = SWA_KV_HEADS, SWA_QPG, HEAD_DIM, SWA_BLOCK
    scale = Dh ** -0.5
    h = x @ w_in
    q, k, v = jnp.split(h, [ATTN_HEADS * Dh, ATTN_HEADS * Dh + Kv * Dh], axis=-1)
    q = q.reshape(B, nb, L, Kv, Q, Dh)

    def band(z):
        z = jnp.pad(z.reshape(B, T, Kv, Dh), ((0, 0), (L, 0), (0, 0), (0, 0))).reshape(B, nb + 1, L, Kv, Dh)
        return jnp.concatenate([z[:, :-1], z[:, 1:]], axis=2)

    kb, vb = band(k), band(v)
    tl = jnp.arange(L, dtype=jnp.int32)
    sl = jnp.arange(2 * L, dtype=jnp.int32)
    dist = tl[:, None] + L - sl[None, :]
    bias = _rel_bias(rel_bias, dist).reshape(Kv, Q, L, 2 * L)
    abs_s = jnp.arange(nb, dtype=jnp.int32)[:, None] * L - L + sl[None, :]
    valid = ((dist >= 0) & (dist < SWA_WINDOW))[None] & (abs_s >= 0)[:, None, :]
    logits = jnp.einsum('bntgqd,bnsgd->bngqts', q, kb).astype(F32) * scale + bias
    logits = jnp.where(valid[None, :, None, None], logits, NEG_INF)
    sink = sinks.astype(F32).reshape(Kv, Q)[None, None, :, :, None, None]
    m = jnp.maximum(jnp.max(logits, axis=-1, keepdims=True), sink)
    e = jnp.exp(logits - m)
    p = e / (jnp.sum(e, axis=-1, keepdims=True) + jnp.exp(sink - m))
    o = jnp.einsum('bngqts,bnsgd->bntgqd', p.astype(x.dtype), vb).reshape(B, T, D_MODEL)
    return o @ w_out

def second_inputs(seed: int = 0) -> dict:
    key = jax.random.key(seed)
    ks = jax.random.split(key, 22)
    beta = (8.0 * DEPTH_2) ** -0.25
    D = D_MODEL

    def nrm(k, shape, scale):
        return jax.random.normal(k, shape, F32) * scale

    return {
        'x': nrm(ks[0], (BATCH, SEQ, D), 1.0),
        'rel_bias': nrm(ks[1], (REL_BUCKETS, ATTN_HEADS), 0.5),
        'ln_gain': 1.0 + nrm(ks[2], (DEPTH_2, 3, D), 0.02),
        'ln_bias': nrm(ks[3], (DEPTH_2, 3, D), 0.02),
        'ffn1_w_gate': nrm(ks[4], (DEPTH_2, D, D_FF), D ** -0.5),
        'ffn1_w_up': nrm(ks[5], (DEPTH_2, D, D_FF), D ** -0.5),
        'ffn1_w_down': nrm(ks[6], (DEPTH_2, D_FF, D), beta * D_FF ** -0.5),
        'ffn2_w_gate': nrm(ks[7], (DEPTH_2, D, D_FF), D ** -0.5),
        'ffn2_w_up': nrm(ks[8], (DEPTH_2, D, D_FF), D ** -0.5),
        'ffn2_w_down': nrm(ks[9], (DEPTH_2, D_FF, D), beta * D_FF ** -0.5),
        'nsa_w_in': nrm(ks[10], (N_NSA, D, NSA_IN), D ** -0.5),
        'nsa_w_out': nrm(ks[11], (N_NSA, D, D), beta * D ** -0.5),
        'nsa_cmp_pos': nrm(ks[12], (N_NSA, 2, CMP_LEN, HEAD_DIM), 0.1),
        'nsa_cmp_w1': nrm(ks[13], (N_NSA, 2, CMP_LEN, HEAD_DIM, CMP_HIDDEN), (CMP_LEN * HEAD_DIM) ** -0.5),
        'nsa_cmp_w2': nrm(ks[14], (N_NSA, 2, CMP_HIDDEN, HEAD_DIM), CMP_HIDDEN ** -0.5),
        'hgrn_w_in': nrm(ks[15], (N_HGRN, D, 4 * D), D ** -0.5),
        'hgrn_w_out': nrm(ks[16], (N_HGRN, D, D), beta * D ** -0.5),
        'hgrn_norm_gain': 1.0 + nrm(ks[17], (N_HGRN, HGRN_VDIM), 0.02),
        'hgrn_lb': nrm(ks[18], (DEPTH_2, D), 1.0),
        'swa_w_in': nrm(ks[19], (N_SWA, D, SWA_IN), D ** -0.5),
        'swa_w_out': nrm(ks[20], (N_SWA, D, D), beta * D ** -0.5),
        'swa_sinks': nrm(ks[21], (N_SWA, ATTN_HEADS), 0.5),
    }

def second_block(x, rel_bias, ln_gain, ln_bias, ffn1_w_gate, ffn1_w_up, ffn1_w_down,
              ffn2_w_gate, ffn2_w_up, ffn2_w_down, nsa_w_in, nsa_w_out, nsa_cmp_pos,
              nsa_cmp_w1, nsa_cmp_w2, hgrn_w_in, hgrn_w_out, hgrn_norm_gain, hgrn_lb,
              swa_w_in, swa_w_out, swa_sinks):
    alpha = (2.0 * DEPTH_2) ** 0.25
    lbs = _lower_bounds(hgrn_lb)
    for i in range(DEPTH_2):
        x = _layer_norm(alpha * x + 0.5 * _swiglu(x, ffn1_w_gate[i], ffn1_w_up[i], ffn1_w_down[i]),
                        ln_gain[i, 0], ln_bias[i, 0])
        kind, slot = i % N_MIXERS, i // N_MIXERS
        if kind == 0:
            y = _nsa(x, nsa_w_in[slot], nsa_w_out[slot], nsa_cmp_pos[slot], nsa_cmp_w1[slot],
                     nsa_cmp_w2[slot], rel_bias)
        elif kind == 1:
            y = _hgrn2(x, hgrn_w_in[slot], hgrn_w_out[slot], hgrn_norm_gain[slot], lbs[i])
        else:
            y = _swa(x, swa_w_in[slot], swa_w_out[slot], swa_sinks[slot], rel_bias)
        x = _layer_norm(alpha * x + y, ln_gain[i, 1], ln_bias[i, 1])
        x = _layer_norm(alpha * x + 0.5 * _swiglu(x, ffn2_w_gate[i], ffn2_w_up[i], ffn2_w_down[i]),
                        ln_gain[i, 2], ln_bias[i, 2])
    return x


def setup_inputs(seed=0):
    out = dict(first_inputs(seed))
    for name, value in second_inputs(seed + 1).items():
        if name != "x":
            out[name + "_2"] = value
    return out


def reference(
    x, ln1_g, w_in, pool_w, pool_scale, m_conv, m_b_i, m_b_f, m_norm_g, a_q_g, a_k_g, w_out,
    ln2_g, w_up, ffn_conv, w_down, rel_bias_2, ln_gain_2, ln_bias_2, ffn1_w_gate_2, ffn1_w_up_2,
    ffn1_w_down_2, ffn2_w_gate_2, ffn2_w_up_2, ffn2_w_down_2, nsa_w_in_2, nsa_w_out_2,
    nsa_cmp_pos_2, nsa_cmp_w1_2, nsa_cmp_w2_2, hgrn_w_in_2, hgrn_w_out_2, hgrn_norm_gain_2,
    hgrn_lb_2, swa_w_in_2, swa_w_out_2, swa_sinks_2,
):
    x = first_block(
        x, ln1_g, w_in, pool_w, pool_scale, m_conv, m_b_i, m_b_f, m_norm_g, a_q_g, a_k_g, w_out,
        ln2_g, w_up, ffn_conv, w_down,
    )
    return second_block(
        x, rel_bias_2, ln_gain_2, ln_bias_2, ffn1_w_gate_2, ffn1_w_up_2, ffn1_w_down_2,
        ffn2_w_gate_2, ffn2_w_up_2, ffn2_w_down_2, nsa_w_in_2, nsa_w_out_2, nsa_cmp_pos_2,
        nsa_cmp_w1_2, nsa_cmp_w2_2, hgrn_w_in_2, hgrn_w_out_2, hgrn_norm_gain_2, hgrn_lb_2,
        swa_w_in_2, swa_w_out_2, swa_sinks_2,
    )


_drawn_inputs = setup_inputs


def setup_inputs(seed=0):
    import zlib

    import numpy as np

    out = dict(_drawn_inputs(seed))
    spreads = {}
    factors = {'ln1_g': 3.637,
     'm_b_i': 64.0,
     'm_norm_g': 8.0,
     'a_q_g': 8.0,
     'a_k_g': 8.0,
     'ln2_g': 4.077,
     'nsa_cmp_pos_2': 3.972,
     'hgrn_norm_gain_2': 25.229,
     'hgrn_lb_2': 3.053}
    for name, (base, spread) in spreads.items():
        noise = np.random.default_rng([zlib.crc32(name.encode()), seed]).standard_normal(out[name].shape)
        drawn = base * np.exp(spread * noise) if base else spread * noise
        out[name] = __import__('jax').numpy.asarray(drawn.astype(out[name].dtype))
    for name, factor in factors.items():
        out[name] = (out[name] * factor).astype(out[name].dtype)
    return out
```

```python
import math
from contextlib import ExitStack

import numpy as np
import concourse.bass as bass
from concourse import mybir

F32 = mybir.dt.float32
F32R = mybir.dt.float32r
BF16 = mybir.dt.bfloat16
I32 = mybir.dt.int32
ACT = mybir.ActivationFunctionType
ALU = mybir.AluOpType
AX = mybir.AxisListType.X

P = 128
D = 1024
T = 256
KC = D // P
NT = T // P
D_FF = 2816
FFN_STEPS = D_FF // (2 * P)
M_HEADS = 4
A_HEADS = 8
DH = 64
N_HEADS = 16
N_GROUPS = 4
REL_BUCKETS = 32
REL_EXACT = REL_BUCKETS // 2
REL_MAX_DIST = 128
CMP_STRIDE = 16
CMP_LEN = 32
N_CMP = T // CMP_STRIDE - 1
H_HEADS = 8
LN_EPS = 1e-5
RMS_EPS = 1e-6
MASKED = -1e30
TINY = 1e-19
ALPHA = (2.0 * 2) ** 0.25
QK_SCALE = DH ** -0.5
POOL_WINDOWS = (2, 4, 8, 16)
PAD = 16
BIAS_COLS = P + T
LEVELS = (64, 32, 16, 8, 4, 2, 1)

RAW_SLOTS = 3
HALF_SLOTS = 6
ARENA = 16500


def shape_constants():
    i = np.arange(P)
    t = np.arange(T)
    parts = {}
    parts["ident"] = np.eye(P)
    parts["flip"] = np.eye(P)[::-1]
    parts["mean"] = np.full((P, P), 1.0 / D)
    parts["causal"] = np.concatenate([np.zeros((P, P)), np.where(i[None, :] > i[:, None], MASKED, 0.0)], 1)
    parts["causal_rev"] = np.where(i[None, :] > P - 1 - i[:, None], MASKED, 0.0)
    parts["late"] = np.concatenate([np.where(i[None, :] < i[:, None], -MASKED, 0.0), np.zeros((P, P))], 1)
    inv = np.zeros((P, 2, T))
    for g, w in enumerate(POOL_WINDOWS):
        inv[64 * (g % 2):64 * (g % 2) + 64, g // 2] = 1.0 / np.minimum(t + 1, w)
    parts["inv_count"] = inv.reshape(P, -1)
    restart = np.ones((P, T))
    restart[:, ::P] = 0.0
    parts["restart"] = restart
    parts["ones"] = np.ones((P, T))
    valid = np.zeros((P, NT, N_CMP))
    for a in range(NT):
        valid[:, a] = (a * P + P - 1 - i)[:, None] >= CMP_STRIDE * np.arange(N_CMP)[None, :] + CMP_LEN - 1
    parts["cmp_add"] = np.where(valid > 0, 0.0, MASKED).reshape(P, -1)
    parts["cmp_valid"] = valid.reshape(P, -1)
    heads = np.zeros((P, 8))
    heads[np.arange(8 * N_CMP), np.arange(8 * N_CMP) // N_CMP] = 1.0
    parts["own_head"] = heads
    parts["levels"] = level_masks()
    parts["eps"] = np.tile(np.array([[RMS_EPS, LN_EPS, 1.0, 0.0]]), (P, 1))
    at, cols = {}, 0
    for name, a in parts.items():
        at[name] = (cols, a.shape[1])
        cols += a.shape[1]
    return np.concatenate(list(parts.values()), 1).astype(np.float32), at


def level_masks():
    i = np.arange(P)
    levels = []
    for m in LEVELS:
        t = i[i // m % 2 == 1]
        levels.append((i[:, None] // (2 * m) == t[None, :] // (2 * m)) & (i[:, None] // m % 2 == 0))
    return np.concatenate(levels, 1)


def distance_buckets():
    def one_hot(dist):
        n = np.maximum(dist, 0)
        large = REL_EXACT + (np.log(np.maximum(n, 1) / REL_EXACT) / math.log(REL_MAX_DIST / REL_EXACT)
                             * (REL_BUCKETS - REL_EXACT)).astype(np.int64)
        b = np.where(n < REL_EXACT, n, np.minimum(large, REL_BUCKETS - 1))
        return np.eye(REL_BUCKETS)[b].T

    full = one_hot(T - 1 - np.arange(BIAS_COLS))
    cmp_ = one_hot(T - CMP_LEN - np.arange(2 * T - CMP_LEN))
    return np.concatenate([full, cmp_], 1).astype(np.float32)


def build_program(nc, io, const_at, out, stop):
    ctx = ExitStack()
    with ctx:
        def sb(name, shape, dt=F32):
            return ctx.enter_context(nc.sbuf_tensor(name, shape, dt))

        def sem(name):
            return ctx.enter_context(nc.semaphore(name))

        n_const = sum(n for _, n in const_at.values())
        consts = sb("consts", [P, n_const])
        raw = sb("raw", [P, RAW_SLOTS, 2048])
        whi = sb("whi", [P, HALF_SLOTS, 1024], F32R)
        wlo = sb("wlo", [P, HALF_SLOTS, 1024], F32R)
        xT = sb("xT", [P, KC, T])
        xc = sb("xc", [P, KC, T])
        sq = sb("sq", [P, KC, T])
        ahi = sb("ahi", [P, KC, T], F32R)
        alo = sb("alo", [P, KC, T], F32R)
        std = sb("std", [P, T])
        rstd = sb("rstd", [P, T])
        ghi = sb("ghi", [P, 2, T], F32R)
        glo = sb("glo", [P, 2, T], F32R)
        gate_act = sb("gate_act", [P, 2, T])
        conv_g = sb("conv_g", [P, 2, T])
        conv_u = sb("conv_u", [P, 2, T])
        gated = sb("gated", [P, 2, T])
        zeros = sb("zeros", [P, 512], BF16)
        par = sb("par", [P, 316])
        arena = sb("arena", [P, ARENA])
        cmp_bias = sb("cmp_bias", [P, NT, N_HEADS * N_CMP])
        scratch = nc.dram_tensor("bias_rows", (N_HEADS, 384), F32, kind="Internal").ap()
        ps = ctx.enter_context(nc.psum_tensor("ps", [P, 8, 512], F32))

        def const(name, rows=P):
            at, n = const_at[name]
            return consts[0:rows, at:at + n]

        ident = const("ident")

        def view(at, *shape, rows=P):
            n = int(np.prod(shape))
            assert at + n <= ARENA, (at, shape)
            v = arena[0:rows, at:at + n]
            if len(shape) == 2:
                v = v.rearrange("p (a b) -> p a b", a=shape[0])
            if len(shape) == 3:
                v = v.rearrange("p (a b c) -> p a b c", a=shape[0], b=shape[1])
            return at + n, v

        def bc(ap, axis, n):
            a = ap.unsqueeze(axis)
            shape = list(a.shape)
            shape[axis] = n
            return a.to_broadcast(shape)

        LN1, LN2, LNG, LNB = 0, 8, 16, 64
        MCONV, PSCALE, LB, AQ, AK, FCONV, CPOS = 112, 128, 130, 146, 147, 148, 280
        n_rows = (112, 124, 76)

        def spare(tensor, at, *shape, rows=P):
            v = tensor.rearrange("p a b -> p (a b)")[0:rows, at:at + int(np.prod(shape))]
            return v if len(shape) == 1 else v.rearrange("p (a b) -> p a b", a=shape[0])

        at, z_qk = view(0, NT, 1024)
        at, a_v = view(at, NT, 512)
        at, qkT = view(at, KC, T)
        at, m_v = view(at, NT, M_HEADS, DH + 1)
        at, m_o = view(at, NT, 256)
        at, conv_out = view(at, 4, T)
        at, decay = view(at, M_HEADS, 384)
        at, a_out = view(at, NT, 512)
        at, h_out = view(at, NT, 256)
        at, h_sq = view(at, NT, 256)
        at, att_score = view(at, 2, 384)
        at, att_prob = view(at, 2, 384)
        at, att_probT = view(at, 2, 384)
        at, att_nmax = view(at, 2, 2)
        att_end = at
        at, gates = view(at, NT, 8)
        at, ss = view(at, 32)
        at, rr = view(at, 32)
        at, a_sums = view(at, A_HEADS, 2)
        at, a_rsum = view(at, A_HEADS, 2)
        at, ucols = view(at, 16)
        at, den = view(at, NT, M_HEADS)
        at, m_ss = view(at, 8)
        at, m_rr = view(at, 8)
        at, gate_w = view(at, KC, 8)
        at, mng = view(at, 256)
        at, pool_w = view(at, 2, P)
        at, gate_bias = view(at, 2, rows=M_HEADS)
        startup = at
        i_g, f_g = (gate_act[0:M_HEADS, n, :] for n in range(2))
        f_abs, f_log = (conv_g[0:M_HEADS, n, :] for n in range(2))
        g_cum, u_g = (conv_u[0:M_HEADS, n, :] for n in range(2))
        m_cum, m_t = (gated[0:M_HEADS, n, :] for n in range(2))
        e_mt = f_abs
        conv_in = spare(xc, 0, 4, 3 + T)
        p_d = spare(xc, 4 * (3 + T), 2, T)
        p_in = spare(sq, 0, 2, PAD + T)
        p_2 = spare(sq, 2 * (PAD + T), 2, PAD + T)
        p_4 = spare(sq, 4 * (PAD + T), 2, PAD + T)
        p_8 = spare(sq, 6 * (PAD + T), 1, PAD + T)
        x_tok = spare(xc, 0, NT, D)
        at, rows = view(startup, 3, P)
        at, hot = view(at, BIAS_COLS + 2 * T - CMP_LEN, rows=REL_BUCKETS)
        at, table = view(at, N_HEADS, rows=REL_BUCKETS)
        at, bias_row = view(at, BIAS_COLS, rows=N_HEADS)

        at, bias = view(0, N_HEADS, T)
        at, n_qT = view(at, KC, T)
        at, k_sel = view(at, N_GROUPS, T)
        at, k_win = view(at, N_GROUPS, T)
        at, z_k = view(at, N_GROUPS, T + 1)
        at, z_v = view(at, N_GROUPS, T + 1)
        at, v_sel = view(at, NT, 256)
        at, v_win = view(at, NT, 256)
        at, n_acc = view(at, NT, 1024)
        at, n_score = view(at, 2, 384)
        at, n_prob = view(at, 2, 384)
        at, n_probT = view(at, 2, 384)
        at, n_nmax = view(at, 2, 2)
        at, n_gates = view(at, NT, 48)
        at, n_sums = view(at, 2 * N_HEADS, 2)
        at, n_rsum = view(at, 2 * N_HEADS, 2)
        at, n_coef = view(at, 3 * N_HEADS, 2)
        at, hidT = view(at, 2, N_GROUPS * N_CMP)
        at, hid_bias = view(at, 2)
        at, kcT = view(at, N_GROUPS * N_CMP)
        at, hid_heads = view(at, N_HEADS, N_CMP)
        at, c_max = view(at, NT, N_HEADS)
        at, c_sum = view(at, NT, N_HEADS)
        c_score = z_k.rearrange("p a b -> p (a b)")[:, 0:480].rearrange("p (a b) -> p a b", a=NT)
        c_probT = z_k.rearrange("p a b -> p (a b)")[:, 480:992].rearrange("p (a b) -> p a b", a=4)
        c_val = z_v.rearrange("p a b -> p (a b)")[:, 0:1024].rearrange("p (a b) -> p a b", a=2)
        n_tmp = spare(sq, 0, 2, 512)
        w1_k, w1_v = (spare(w, 0, 16, P) for w in (sq, xc))

        at, r_q = view(0, H_HEADS, T)
        at, r_k = view(at, H_HEADS, T)
        at, r_b = view(at, H_HEADS, T)
        at, r_v = view(at, NT, D)
        at, r_g = view(at, NT, D)
        at, r_at = view(at, 2 * H_HEADS, P)
        at, r_cross = view(at, H_HEADS, P)
        at, r_o = view(at, NT, D)
        at, r_ss = view(at, 16)
        at, r_rr = view(at, 16)
        at, lb = view(at, 4, H_HEADS)
        at, r_gain = view(at, P)

        gate_w2 = sb("gate_w2", [P, KC, 48])
        w2_k = sb("w2_k", [P, 2, DH])
        w2_v = sb("w2_v", [P, DH])

        raw_landed = [sem(f"raw_landed{n}") for n in range(RAW_SLOTS)]
        const_landed = sem("const_landed")
        x_landed = sem("x_landed")
        rows_landed = sem("rows_landed")
        small_landed = sem("small_landed")
        hi_ready = sem("hi_ready")
        lo_ready = sem("lo_ready")
        half_done = sem("half_done")
        x_turned = sem("x_turned")
        x_ready = sem("x_ready")
        x_scaled = sem("x_scaled")
        par_turned = sem("par_turned")
        par_ready = sem("par_ready")
        zeros_ready = sem("zeros_ready")
        mean_ready = sem("mean_ready")
        xc_ready = sem("xc_ready")
        sq_ready = sem("sq_ready")
        var_ready = sem("var_ready")
        std_ready = sem("std_ready")
        xn_ready = sem("xn_ready")
        aff_ready = sem("aff_ready")
        a_ready = sem("a_ready")
        evac_done = sem("evac_done")
        mix_turned = sem("mix_turned")
        mix_hi = sem("mix_hi")
        mix_lo = sem("mix_lo")
        conv0_ready = sem("conv0_ready")
        convg_ready = sem("convg_ready")
        silu_ready = sem("silu_ready")
        g_ready = sem("g_ready")
        ffn_chain = sem("ffn_chain")
        y_ready = sem("y_ready")
        out_turned = sem("out_turned")
        out_ready = sem("out_ready")
        stored = sem("stored")
        dve_chain = sem("dve_chain")
        act_chain = sem("act_chain")
        pool_chain = sem("pool_chain")
        counts = {"dve": 0, "act": 0, "pool": 0}

        def link(engine, semaphore, name, instruction):
            counts[name] += 1
            instruction.then_inc(semaphore, 1)
            engine.wait_ge(semaphore, counts[name])

        w_in, w_out = io["w_in"][0], io["w_out"][0]
        n_in, n_out = io["nsa_w_in_2"][0], io["nsa_w_out_2"][0]
        r_in, r_out = io["hgrn_w_in_2"][0], io["hgrn_w_out_2"][0]
        up0 = io["w_up"][0]
        A_COLS = [1288 + 256 * n for n in range(6)] + [256, 512, 768, 1024, 0]
        N_COLS = [256 * n for n in range(10)]
        H_COLS = [1024 + 256 * n for n in range(4)] + [256 * n for n in range(4)] + \
                 [2048 + 256 * n for n in range(8)]
        O_COLS = [256 * n for n in range(4)]

        def ffn_mats(i, which):
            return tuple(io[f"ffn{which}_w_{m}_2"][i] for m in ("gate", "up", "down"))

        plan = [
            ("lin", w_in, A_COLS),
            ("lin", w_out, O_COLS),
            ("ffn", (up0[:, 0:D_FF], up0[:, D_FF:2 * D_FF], io["w_down"][0])),
            ("ffn", ffn_mats(0, 1)),
            ("lin", n_in, N_COLS),
            ("lin", n_out, O_COLS),
            ("ffn", ffn_mats(0, 2)),
            ("ffn", ffn_mats(1, 1)),
            ("lin", r_in, H_COLS),
            ("lin", r_out, O_COLS),
            ("ffn", ffn_mats(1, 2)),
        ][:stop]
        slab0 = [0]
        for e in plan:
            slab0.append(slab0[-1] + (len(e[2]) if e[0] == "lin" else 3 * FFN_STEPS))
        half0 = [2 * s for s in slab0]
        FFN_STEP = [(0, 0), (1, 0), (0, 1), (1, 1), (2, 0), (2, 1)]
        LAST_OF = (3, 4, 6)

        def stage_of(half):
            return max(n for n in range(len(plan)) if half0[n] <= half)

        def raw_freed(slab):
            n = stage_of(2 * slab)
            if plan[n][0] == "lin":
                return 2 * slab + 2
            j, m = divmod(slab - slab0[n], 3)
            return half0[n] + 6 * j + LAST_OF[m]

        def raw_half(kind, slot, matrix, x):
            if kind == "lin" or matrix < 2:
                return raw[:, slot, :].rearrange("p (k n) -> p k n", k=KC)[:, :, x * P:(x + 1) * P]
            return raw[:, slot, x * D:(x + 1) * D]

        def split_half(w, h, kind, matrix):
            v = w[:, h % HALF_SLOTS, :]
            return v.rearrange("p (k n) -> p k n", k=KC) if kind == "lin" or matrix < 2 else v

        def half_place(h):
            n = stage_of(h)
            if plan[n][0] == "lin":
                return "lin", 0, h % 2, h // 2
            j, s = divmod(h - half0[n], 6)
            m, x = FFN_STEP[s]
            return "ffn", m, x, slab0[n] + 3 * j + m

        n_halves = half0[-1]

        def act_split(act, h):
            if h >= n_halves:
                return
            kind, m, x, slab = half_place(h)
            act.wait_ge(raw_landed[slab % RAW_SLOTS], 16 * (slab // RAW_SLOTS + 1))
            if h >= HALF_SLOTS:
                act.wait_ge(half_done, h - HALF_SLOTS + 1)
            act.activation(split_half(whi, h, kind, m), raw_half(kind, slab % RAW_SLOTS, m, x),
                           ACT.Copy).then_inc(hi_ready, 1)

        def dve_split(dve, h):
            if h >= n_halves:
                return
            kind, m, x, slab = half_place(h)
            dve.wait_ge(hi_ready, h + 1)
            dve.tensor_tensor(split_half(wlo, h, kind, m), raw_half(kind, slab % RAW_SLOTS, m, x),
                              split_half(whi, h, kind, m).bitcast(F32), ALU.subtract).then_inc(lo_ready, 1)

        def act_split_next(act, n, j, s):
            m, x = FFN_STEP[s]
            slab = slab0[n] + 3 + m
            h = half0[n] + 6 + s
            act.wait_ge(raw_landed[slab % RAW_SLOTS], j * 16 + 16 * (slab // RAW_SLOTS + 1))
            act.wait_ge(half_done, j * 6 + (h - HALF_SLOTS + 1))
            act.activation(split_half(whi, h, "ffn", m), raw_half("ffn", slab % RAW_SLOTS, m, x),
                           ACT.Copy).then_inc(hi_ready, 1)

        def dve_split_next(dve, n, j, s):
            m, x = FFN_STEP[s]
            slab = slab0[n] + 3 + m
            h = half0[n] + 6 + s
            dve.wait_ge(hi_ready, j * 6 + (h + 1))
            dve.tensor_tensor(split_half(wlo, h, "ffn", m), raw_half("ffn", slab % RAW_SLOTS, m, x),
                              split_half(whi, h, "ffn", m).bitcast(F32), ALU.subtract).then_inc(lo_ready, 1)

        def three_pass(pe, dst, wh, wl, ah, al, first, last):
            pe.matmul(dst, wh, ah, start=first, stop=False, skip_group_check=True)
            pe.matmul(dst, wh, al, start=False, stop=False, skip_group_check=True)
            return pe.matmul(dst, wl, ah, start=False, stop=last, skip_group_check=True)

        def pe_half_channels(pe, h, dst, waited=True):
            if waited:
                pe.wait_ge(lo_ready, h + 1)
            wh, wl = (w[:, h % HALF_SLOTS, :].rearrange("p (k n) -> p k n", k=KC) for w in (whi, wlo))
            for k in range(KC):
                last = three_pass(pe, dst, wh[:, k, :], wl[:, k, :], ahi[:, k, :], alo[:, k, :], k == 0, k == KC - 1)
            last.then_inc(half_done, 1)

        def pe_slab_tokens(pe, h, tile, dst):
            s = h % HALF_SLOTS
            wh, wl = (w[:, s:s + 2, :].rearrange("p s (k n) -> p s k n", k=KC) for w in (whi, wlo))
            out2 = dst.rearrange("p (s n) -> p s n", s=2)
            for k in range(KC):
                a_h, a_l = (a[:, k, tile * P:(tile + 1) * P] for a in (ahi, alo))
                pe.matmul(out2, a_h, wh[:, :, k, :], start=k == 0, stop=False, skip_group_check=True)
                pe.matmul(out2, a_l, wh[:, :, k, :], start=False, stop=False, skip_group_check=True)
                last = pe.matmul(out2, a_h, wl[:, :, k, :], start=False, stop=k == KC - 1, skip_group_check=True)
            return last

        X_STAGES = [1, 2, 3, 5, 6, 7, 9, 10]
        n_pre = 1 + sum(s < len(plan) for s in X_STAGES)

        def x_count(p):
            return 4 + 8 * p

        PRE = [("rms", LN1, None, 4), ("rms", LN2, None, 4), ("none", None, None, 0),
               ("ln", LNG + 0, LNB + 0, 0), ("ln", LNG + 8, LNB + 8, 4), ("ln", LNG + 16, LNB + 16, 0),
               ("ln", LNG + 24, LNB + 24, 0), ("ln", LNG + 32, LNB + 32, 4), ("ln", LNG + 40, LNB + 40, 0)]

        def norm_index(p):
            return sum(PRE[n][0] != "none" for n in range(p)), sum(PRE[n][0] == "ln" for n in range(p))

        def pe_pre(pe, p):
            kind, _, _, bank = PRE[p]
            ni, li = norm_index(p)
            if kind == "none":
                return
            if kind == "ln":
                for k in range(KC):
                    pe.wait_ge(x_ready, x_count(p) - KC + k + 1)
                    last = pe.matmul(ps[:, bank, 0:T], const("mean"), xT[:, k, :], start=k == 0, stop=k == KC - 1)
                last.then_inc(mean_ready, 1)
            for half in range(2):
                pe.wait_ge(sq_ready, 2 * ni + half + 1)
                for k in range(4 * half, 4 * half + 4):
                    last = pe.matmul(ps[:, bank + 1, 0:T], const("mean"), sq[:, k, :], start=k == 0, stop=k == KC - 1)
            last.then_inc(var_ready, 1)

        def act_pre(act, p):
            kind, gain, shift, bank = PRE[p]
            ni, li = norm_index(p)
            if kind == "none":
                return
            for half in range(2):
                cs = slice(4 * half, 4 * half + 4)
                if kind == "ln":
                    act.wait_ge(xc_ready, 2 * li + half + 1)
                else:
                    act.wait_ge(x_ready, x_count(p))
                act.activation(sq[:, cs, :], (xc if kind == "ln" else xT)[:, cs, :], ACT.Square).then_inc(sq_ready, 1)
            act.wait_ge(var_ready, ni + 1)
            at_eps = const_at["eps"][0] + (kind == "ln")
            act.activation(std[:, :], ps[:, bank + 1, 0:T], ACT.Sqrt,
                           bias=consts[:, at_eps:at_eps + 1]).then_inc(std_ready, 1)
            dst = xT if kind == "ln" else xc
            for k in range(KC):
                act.wait_ge(xn_ready, 2 * ni + k // 4 + 1)
                act.activation(dst[:, k, :], xc[:, k, :], ACT.Identity, scale=par[:, gain + k:gain + k + 1],
                               bias=par[:, shift + k:shift + k + 1] if kind == "ln" else 0.0).then_inc(aff_ready, 1)

        def dve_pre(dve, p, split=True):
            kind, _, _, bank = PRE[p]
            ni, li = norm_index(p)
            if kind != "none":
                if kind == "ln":
                    dve.wait_ge(mean_ready, li + 1)
                    for half in range(2):
                        cs = slice(4 * half, 4 * half + 4)
                        dve.tensor_tensor(xc[:, cs, :], xT[:, cs, :], bc(ps[:, bank, 0:T], 1, 4),
                                          ALU.subtract).then_inc(xc_ready, 1)
                dve.wait_ge(std_ready, ni + 1)
                link(dve, dve_chain, "dve", dve.reciprocal(rstd[:, :], std[:, :]))
                for half in range(2):
                    cs = slice(4 * half, 4 * half + 4)
                    if kind == "ln":
                        dve.wait_ge(xc_ready, 2 * li + half + 1)
                    dve.tensor_tensor(xc[:, cs, :], (xc if kind == "ln" else xT)[:, cs, :],
                                      bc(rstd[:, :], 1, 4), ALU.mult).then_inc(xn_ready, 1)
            src = xc if kind == "rms" else xT
            if not split:
                return
            for pair in range(4):
                cs = slice(2 * pair, 2 * pair + 2)
                if kind == "none":
                    dve.wait_ge(x_ready, x_count(p) - KC + 2 * pair + 2)
                else:
                    dve.wait_ge(aff_ready, KC * ni + 2 * pair + 2)
                link(dve, dve_chain, "dve", dve.tensor_copy(ahi[:, cs, :], src[:, cs, :]))
                dve.tensor_tensor(alo[:, cs, :], src[:, cs, :], ahi[:, cs, :].bitcast(F32),
                                  ALU.subtract).then_inc(a_ready, 1)

        def pool_scale_x(pool, p):
            pool.wait_ge(a_ready, 4 * (p + 1))
            if p == 4 - 1:
                pool.wait_ge(nsa_gates_done, 1)
            pool.tensor_scalar(xT[:, :, :], xT[:, :, :], ALPHA, None, ALU.mult).then_inc(x_scaled, 1)

        def mix_count(n):
            return 4 * ((1, 5, 9).index(n) + 1)

        def pe_project(pe, n, p):
            pe.wait_ge(mix_lo, mix_count(n))
            for s in range(8):
                if s >= 4:
                    pe.wait_ge(x_ready, x_count(p) + s - 3)
                pe_half_channels(pe, half0[n] + s, ps[:, s % 4, 0:T])

        def act_project(act, n):
            for s in range(8):
                act_split(act, half0[n] + s + HALF_SLOTS)

        def dve_project(dve, n, p, scaled):
            if scaled:
                dve.wait_ge(x_scaled, scaled)
            for s in range(8):
                dve.wait_ge(half_done, half0[n] + s + 1)
                dve.tensor_tensor(xT[:, s, :], xT[:, s, :], ps[:, s % 4, 0:T], ALU.add).then_inc(x_ready, 1)
                dve_split(dve, half0[n] + s + HALF_SLOTS)

        def ffn_index(n):
            return (2, 3, 6, 7, 10).index(n)

        def pe_ffn(pe, n, p):
            f = ffn_index(n)
            pe.wait_ge(a_ready, 4 * (p + 1))
            if f == 0:
                pe.wait_ge(zeros_ready, 1)
            for b in range(4):
                pe.matmul(ps[:, 4 + b, :], zeros[:, 0:P], zeros[:, :], start=True, stop=False, skip_group_check=True)
            with pe.Fori(0, FFN_STEPS) as j:
                for s in range(6):
                    h = half0[n] + s
                    m, x = FFN_STEP[s]
                    pe.wait_ge(lo_ready, j * 6 + (h + 1))
                    if m < 2:
                        pe_half_channels(pe, h, ps[:, 2 * x + m, 0:T], waited=False)
                        continue
                    pe.wait_ge(g_ready, j * 2 + (2 * FFN_STEPS * f + x + 1))
                    for c in range(KC):
                        cols = slice(c * P, (c + 1) * P)
                        last = three_pass(pe, ps[:, 4 + c // 2, (c % 2) * T:(c % 2 + 1) * T],
                                          whi[:, h % HALF_SLOTS, cols], wlo[:, h % HALF_SLOTS, cols],
                                          ghi[:, x, :], glo[:, x, :], False, False)
                    last.then_inc(half_done, 1)

        def act_ffn(act, n, p):
            f = ffn_index(n)

            def step(j, splits):
                for s in range(6):
                    m, x = FFN_STEP[s]
                    if m < 2 and n == 2:
                        act.wait_ge(half_done, j * 6 + (half0[n] + s + 1))
                        conv = (conv_g, conv_u)[m]
                        tap = par[:, bass.ds(j * 2 + (FCONV + 88 + 22 * m + x), 1)]
                        act.activation(conv[:, x, :], ps[:, 2 * x + m, 0:T], ACT.Copy,
                                       scale=tap).then_inc(conv0_ready, 1)
                        if m == 1:
                            act.wait_ge(convg_ready, j * 2 + (x + 1))
                            act.activation(gate_act[:, x, :], conv_g[:, x, :], ACT.Silu).then_inc(silu_ready, 1)
                    elif m == 0:
                        act.wait_ge(half_done, j * 6 + (half0[n] + s + 1))
                        act.activation(gate_act[:, x, :], ps[:, 2 * x, 0:T], ACT.Silu).then_inc(silu_ready, 1)
                    splits(j, s)

            with act.Fori(0, FFN_STEPS - 1) as j:
                step(j, lambda j, s: act_split_next(act, n, j, s))
            step(FFN_STEPS - 1, lambda j, s: act_split(act, half0[n + 1] + s))

        def dve_ffn(dve, n, p, scaled):
            f = ffn_index(n)
            links = 5 if n == 2 else 2

            def step(j, splits):
                done = 0

                def chain(ins):
                    nonlocal done
                    done += 1
                    before = 0 if f == 0 else 2 * FFN_STEPS * (5 + 2 * (f - 1))
                    ins.then_inc(ffn_chain, 1)
                    dve.wait_ge(ffn_chain, j * (2 * links) + (before + done))

                for s in range(6):
                    m, x = FFN_STEP[s]
                    if m < 2 and n == 2:
                        conv = (conv_g, conv_u)[m]
                        dve.wait_ge(conv0_ready, j * 4 + (2 * x + m + 1))
                        for back in (1, 2):
                            tap = par[:, bass.ds(j * 2 + (FCONV + 44 * (2 - back) + 22 * m + x), 1)]
                            ins = dve.scalar_tensor_tensor(conv[:, x, back:T], ps[:, 2 * x + m, 0:T - back], tap,
                                                           conv[:, x, back:T], ALU.mult, ALU.add)
                            if m == 0 and back == 2:
                                ins.then_inc(convg_ready, 1)
                            else:
                                chain(ins)
                    if m == 1:
                        dve.wait_ge(half_done, j * 6 + (half0[n] + s + 1))
                        dve.wait_ge(silu_ready, j * 2 + (2 * FFN_STEPS * f + x + 1))
                        up = conv_u[:, x, :] if n == 2 else ps[:, 2 * x + 1, 0:T]
                        chain(dve.tensor_tensor(gated[:, x, :], gate_act[:, x, :], up, ALU.mult))
                        chain(dve.tensor_copy(ghi[:, x, :], gated[:, x, :]))
                        dve.tensor_tensor(glo[:, x, :], gated[:, x, :], ghi[:, x, :].bitcast(F32),
                                          ALU.subtract).then_inc(g_ready, 1)
                    splits(j, s)

            with dve.Fori(0, FFN_STEPS - 1) as j:
                step(j, lambda j, s: dve_split_next(dve, n, j, s))
            if scaled:
                dve.wait_ge(x_scaled, scaled)
            step(FFN_STEPS - 1, lambda j, s: dve_split(dve, half0[n + 1] + s))
            dve.wait_ge(half_done, half0[n + 1])
            for c in range(KC):
                y = ps[:, 4 + c // 2, (c % 2) * T:(c % 2 + 1) * T]
                dve.scalar_tensor_tensor(xT[:, c, :], y, 0.5 if scaled else 1.0, xT[:, c, :],
                                         ALU.mult, ALU.add).then_inc(x_ready, 1)

        gates_done = sem("gates_done")
        gates_evac = sem("gates_evac")
        nsa_gates_done = sem("nsa_gates_done")
        rows_done = sem("rows_done")
        rows_evac = sem("rows_evac")
        rows_stored = sem("rows_stored")
        cmp_bias_done = sem("cmp_bias_done")
        cmp_bias_ready = sem("cmp_bias_ready")
        bias_landed = sem("bias_landed")
        bias_ready = sem("bias_ready")

        def pe_start(pe):
            pe.wait_ge(const_landed, 16)
            pe.wait_ge(x_landed, 16)
            for b in range(4):
                for c in range(2):
                    for a in range(NT):
                        last = pe.transpose(ps[:, b, c * T + a * P:c * T + (a + 1) * P],
                                            x_tok[:, a, (2 * b + c) * P:(2 * b + c + 1) * P], ident)
                last.then_inc(x_turned, 1)
            pe.wait_ge(rows_landed, 16 * N_ROW_DMAS)
            for g in range(3):
                last = pe.transpose(ps[:, 6, g * P:g * P + n_rows[g]], rows[0:n_rows[g], g, :],
                                    ident[0:n_rows[g], 0:n_rows[g]])
            last.then_inc(par_turned, 1)

        def pe_bias_rows(pe):
            pe.wait_ge(small_landed, 16 * N_SMALL_DMAS)
            pe.matmul(ps[0:N_HEADS, 7, 0:BIAS_COLS], table, hot[:, 0:BIAS_COLS], start=True,
                      stop=True).then_inc(rows_done, 1)
            for a in range(NT):
                for n in range(N_CMP):
                    col = BIAS_COLS + P - a * P + CMP_STRIDE * n
                    last = pe.matmul(ps[:, 2 + a, n * N_HEADS:(n + 1) * N_HEADS], hot[:, col:col + P], table,
                                     start=True, stop=True)
                if a == 0:
                    pe.wait_ge(x_ready, 4)
            last.then_inc(cmp_bias_done, 1)

        def act_start(act):
            act.wait_ge(par_turned, 1)
            at = 0
            for g in range(3):
                last = act.activation(par[:, at:at + n_rows[g]], ps[:, 6, g * P:g * P + n_rows[g]], ACT.Copy)
                at += n_rows[g]
            link(act, act_chain, "act", last)
            act.activation(par[:, AQ:AQ + 1], par[:, AQ:AQ + 1], ACT.Copy, scale=QK_SCALE).then_inc(par_ready, 1)
            act.wait_ge(par_ready, 1)

        def act_bias_rows(act):
            act.wait_ge(rows_done, 1)
            act.activation(bias_row, ps[0:N_HEADS, 7, 0:BIAS_COLS], ACT.Copy).then_inc(rows_evac, 1)

        def dve_start(dve):
            dve.memset(zeros[:, :], 0.0).then_inc(zeros_ready, 1)
            for b in range(4):
                dve.wait_ge(x_turned, b + 1)
                dve.tensor_copy(xT[:, 2 * b:2 * b + 2, :], ps[:, b, :].rearrange("p (a b) -> p a b", a=2)).then_inc(x_ready, 1)

        def dve_bias_rows(dve):
            dve.wait_ge(cmp_bias_done, 1)
            for a in range(NT):
                dve.tensor_tensor(cmp_bias[:, a, :].rearrange("p (h n) -> p h n", h=N_HEADS),
                                  ps[:, 2 + a, 0:N_CMP * N_HEADS].rearrange("p (n h) -> p h n", n=N_CMP),
                                  bc(const("cmp_add")[:, a * N_CMP:(a + 1) * N_CMP], 1, N_HEADS),
                                  ALU.add).then_inc(cmp_bias_ready, 1)

        scores_done = sem("scores_done")
        max_ready = sem("max_ready")
        exp_done = sem("exp_done")
        probT_done = sem("probT_done")
        probT_ready = sem("probT_ready")
        heads_done = sem("heads_done")

        def pe_attention(pe, u0, n, q, k, v, dst, buf):
            _, prob, probT, _, _ = buf

            def scores(i):
                u = u0 + i
                if u >= 2:
                    pe.wait_ge(max_ready, u - 1)
                b = u % 2
                pe.matmul(ps[:, b, 0:P], q(i, 0), k(i, 1), start=True, stop=True)
                pe.matmul(ps[:, b, P:3 * P], q(i, 1), k(i, 2), start=True, stop=True).then_inc(scores_done, 1)

            def turn(i):
                u = u0 + i
                pe.wait_ge(exp_done, u + 1)
                if u >= 2:
                    pe.wait_ge(probT_ready, u - 1)
                for m in range(3):
                    last = pe.transpose(ps[:, 2 + u % 2, m * P:(m + 1) * P], prob[:, u % 2, m * P:(m + 1) * P], ident)
                last.then_inc(probT_done, 1)

            def values(i):
                u = u0 + i
                pe.wait_ge(probT_ready, u + 1)
                t = probT[:, u % 2, :]
                pe.matmul(dst(i, 0), t[:, 0:P], v(i, 0), start=True, stop=True)
                pe.matmul(dst(i, 1), t[:, P:2 * P], v(i, 0), start=True, stop=False)
                pe.matmul(dst(i, 1), t[:, 2 * P:3 * P], v(i, 1), start=False, stop=True).then_inc(heads_done, 1)

            for i in range(n + 2):
                if i < n:
                    scores(i)
                if 1 <= i <= n:
                    turn(i - 1)
                if i >= 2:
                    values(i - 2)

        def dve_attention(dve, u0, n, add, buf):
            score, _, _, nmax, _ = buf
            for i in range(n):
                u = u0 + i
                s = score[:, u % 2, :]
                dve.wait_ge(scores_done, u + 1)
                if u >= 2:
                    dve.wait_ge(exp_done, u - 1)
                dve.tensor_tensor(s[:, P:3 * P], ps[:, u % 2, P:3 * P], add(i), ALU.add)
                link(dve, dve_chain, "dve", dve.tensor_tensor(s[:, 0:P], ps[:, u % 2, 0:P], add(i)[:, P:2 * P], ALU.add))
                dve.tensor_reduce(nmax[:, u % 2, 0:1], s[:, 0:P], AX, ALU.max, negate=True)
                dve.tensor_reduce(nmax[:, u % 2, 1:2], s[:, P:3 * P], AX, ALU.max, negate=True).then_inc(max_ready, 1)

        def act_attention(act, u0, n, buf):
            score, prob, probT, nmax, sums = buf

            def evacuate(i):
                u = u0 + i
                act.wait_ge(probT_done, u + 1)
                if u >= 2:
                    act.wait_ge(heads_done, u - 1)
                act.activation(probT[:, u % 2, :], ps[:, 2 + u % 2, 0:3 * P], ACT.Copy).then_inc(probT_ready, 1)

            for i in range(n):
                u = u0 + i
                act.wait_ge(max_ready, u + 1)
                if u >= 2:
                    act.wait_ge(probT_done, u - 1)
                act.activation(prob[:, u % 2, 0:P], score[:, u % 2, 0:P], ACT.Exp, bias=nmax[:, u % 2, 0:1],
                               accum_out=sums[:, i, 0:1])
                act.activation(prob[:, u % 2, P:3 * P], score[:, u % 2, P:3 * P], ACT.Exp, bias=nmax[:, u % 2, 1:2],
                               accum_out=sums[:, i, 1:2]).then_inc(exp_done, 1)
                if i >= 1:
                    evacuate(i - 1)
            evacuate(n - 1)

        EV_A, EV_N, EV_H = 0, 22, 42
        token_tile = sem("token_tile")
        TT_A, TT_N, TT_H = 0, 8, 10
        pads_ready = sem("pads_ready")
        ones_ready = sem("ones_ready")
        gates_turned = sem("gates_turned")
        fabs_ready = sem("fabs_ready")
        softplus_ready = sem("softplus_ready")
        mt_ready = sem("mt_ready")
        emt_ready = sem("emt_ready")
        ucols_turned = sem("ucols_turned")
        ucols_read = sem("ucols_read")
        mcum_spread = sem("mcum_spread")
        decay_arg = sem("decay_arg")
        decay_ready = sem("decay_ready")
        qk_sq = sem("qk_sq")
        qk_var = sem("qk_var")
        qk_std = sem("qk_std")
        qk_normed = sem("qk_normed")
        qk_turned = sem("qk_turned")
        qk_ready = sem("qk_ready")
        conv_ready = sem("conv_ready")
        mqk_ready = sem("mqk_ready")
        mqk_done = sem("mqk_done")
        mw_ready = sem("mw_ready")
        num_done = sem("num_done")
        hc_ready = sem("hc_ready")
        hsq_ready = sem("hsq_ready")
        hvar_ready = sem("hvar_ready")
        hstd_ready = sem("hstd_ready")
        hm_ready = sem("hm_ready")
        ao_ready = sem("ao_ready")
        pool_ready = sem("pool_ready")
        pool_done = sem("pool_done")
        po_ready = sem("po_ready")

        def pe_tile_tokens(pe, base, ev, o):
            pe.wait_ge(lo_ready, base + o + 2)
            for a in range(NT):
                if o + a >= 4:
                    pe.wait_ge(evac_done, ev + o + a - 3)
                last = pe_slab_tokens(pe, base + o, a, ps[:, (o + a) % 4, 0:T])
                if a == 0:
                    last.then_inc(token_tile, 1)
                else:
                    last.then_inc(half_done, 2)

        def pe_tile_channels(pe, base, ev, o):
            if o >= 4:
                pe.wait_ge(evac_done, ev + o - 3)
            pe_half_channels(pe, base + o, ps[:, o % 4, 0:T])

        def pe_first(pe):
            pe.wait_ge(aff_ready, KC)
            pe.wait_ge(a_ready, 4)
            for a in range(NT):
                for k in range(KC):
                    last = pe.matmul(ps[:, 6, a * 8:(a + 1) * 8], xc[:, k, a * P:(a + 1) * P], gate_w[:, k, :],
                                     start=k == 0, stop=k == KC - 1)
            last.then_inc(gates_done, 1)
            for o in range(0, 22, 2):
                if o == 2:
                    pe.wait_ge(gates_evac, 1)
                    for m in range(2):
                        for a in range(NT):
                            last = pe.transpose(ps[0:M_HEADS, 7, m * T + a * P:m * T + (a + 1) * P],
                                                gates[:, a, 4 * m:4 * m + 4], ident)
                    last.then_inc(gates_turned, 1)
                if o == 8:
                    pe.wait_ge(mt_ready, 1)
                    pe.wait_ge(emt_ready, 1)
                    for m, row in enumerate((u_g, e_mt)):
                        for a in range(NT):
                            last = pe.transpose(ps[:, 6, 8 * m + 4 * a:8 * m + 4 * a + 4], row[:, a * P:(a + 1) * P],
                                                ident[0:M_HEADS, 0:M_HEADS])
                    last.then_inc(ucols_turned, 1)
                if o == 10:
                    pe.wait_ge(ucols_read, 1)
                    for h in range(M_HEADS):
                        last = pe.matmul(ps[:, 7 - h // 2, (h % 2) * T:(h % 2 + 1) * T],
                                         ident[0:M_HEADS, h:h + 1].to_broadcast([M_HEADS, P]), m_cum,
                                         start=True, stop=True)
                    last.then_inc(mcum_spread, 1)
                if o in (14, 16):
                    m = (o - 14) // 2
                    pe.wait_ge(qk_normed, 1)
                    if m:
                        pe.wait_ge(qk_ready, 1)
                    for c in range(4):
                        for a in range(NT):
                            last = pe.transpose(ps[:, 4 + c // 2, (c % 2) * T + a * P:(c % 2) * T + (a + 1) * P],
                                                z_qk[:, a, (4 * m + c) * P:(4 * m + c + 1) * P], ident)
                    last.then_inc(qk_turned, 1)
                if 12 <= o < 16 or o >= 20:
                    pe_tile_channels(pe, half0[0], EV_A, o)
                    pe_tile_channels(pe, half0[0], EV_A, o + 1)
                else:
                    pe_tile_tokens(pe, half0[0], EV_A, o)
            pe.wait_ge(qk_ready, 2)
            pe.wait_ge(evac_done, EV_A + 22)
            pe_attention(pe, 0, A_HEADS,
                         lambda i, t: qkT[64 * (i % 2):64 * (i % 2) + 64, i // 2, t * P:(t + 1) * P],
                         lambda i, n: qkT[64 * (i % 2):64 * (i % 2) + 64, 4 + i // 2, 0:n * P],
                         lambda i, t: a_v[:, t, i * DH:(i + 1) * DH],
                         lambda i, t: ps[:, 4 + t, i * DH:(i + 1) * DH],
                         (att_score, att_prob, att_probT, att_nmax, a_sums))
            pe.wait_ge(decay_arg, 1)
            pe.wait_ge(pool_ready, 1)
            for c in range(2):
                last = pe.matmul(ps[:, 7, c * T:(c + 1) * T], pool_w[:, c, :], p_d[:, c, :], start=True, stop=True)
            last.then_inc(pool_done, 1)
            pe.wait_ge(mqk_ready, 1)
            for h in range(M_HEADS):
                lo = 64 * (h % 2)
                q, k = conv_out[lo:lo + 64, h // 2, :], conv_out[lo:lo + 64, 2 + h // 2, :]
                pe.matmul(ps[:, h, 0:T], k[:, 0:P], q, start=True, stop=True)
                pe.matmul(ps[:, h, T:T + P], k[:, P:T], q[:, P:T], start=True, stop=True).then_inc(mqk_done, 1)
            pe.wait_ge(ao_ready, 2)
            pe.wait_ge(mw_ready, 2)
            for c in range(4):
                for a in range(NT):
                    last = pe.transpose(ps[:, c // 2, (c % 2) * T + a * P:(c % 2) * T + (a + 1) * P],
                                        a_out[:, a, c * P:(c + 1) * P], ident)
                if c % 2:
                    last.then_inc(mix_turned, 1)
            pe.wait_ge(ones_ready, 1)
            for h in range(M_HEADS):
                pe.wait_ge(mw_ready, h + 1)
                col = slice(h * (DH + 1), (h + 1) * (DH + 1))
                pe.matmul(ps[:, 4, col], decay[:, h, 0:P], m_v[:, 0, h, :], start=True, stop=True)
                pe.matmul(ps[:, 5, col], decay[:, h, P:T], m_v[:, 0, h, :], start=True, stop=False)
                last = pe.matmul(ps[:, 5, col], decay[:, h, T:T + P], m_v[:, 1, h, :], start=False, stop=True)
            last.then_inc(num_done, 1)
            pe.wait_ge(hm_ready, 1)
            for c in range(2):
                for a in range(NT):
                    last = pe.transpose(ps[:, 6, c * T + a * P:c * T + (a + 1) * P], h_out[:, a, c * P:(c + 1) * P], ident)
            last.then_inc(mix_turned, 1)

        def act_mix(act, count, src, cs, turned):
            act.wait_ge(mix_turned, turned)
            act.activation(ahi[:, cs:cs + 2, :], src, ACT.Copy).then_inc(mix_hi, 1)

        def dve_mix(dve, count, src, cs):
            dve.wait_ge(mix_hi, count)
            dve.tensor_tensor(alo[:, cs:cs + 2, :], src, ahi[:, cs:cs + 2, :].bitcast(F32), ALU.subtract).then_inc(mix_lo, 1)

        def bank2(b):
            return ps[:, b, :].rearrange("p (a b) -> p a b", a=2)

        def act_first(act):
            for o in range(22):
                slab, x = o // 2, o % 2
                channels = slab in (6, 7, 10)
                src = ps[:, o % 4, 0:T]
                if channels or x == 1:
                    act.wait_ge(half_done, half0[0] + o + 1)
                else:
                    act.wait_ge(token_tile, TT_A + (slab if slab < 6 else slab - 2) + 1)
                if slab < 4:
                    act.activation(z_qk[:, x, 256 * slab:256 * slab + 256], src, ACT.Copy).then_inc(evac_done, 1)
                elif slab < 6:
                    act.activation(a_v[:, x, 256 * (slab - 4):256 * (slab - 3)], src, ACT.Copy).then_inc(evac_done, 1)
                elif slab < 8:
                    if o == 12:
                        act.wait_ge(pads_ready, 2)
                    act.activation(conv_in[:, o - 12, 3:3 + T], src, ACT.Copy).then_inc(evac_done, 1)
                elif slab == 8:
                    act.activation(m_v[:, x, :, 0:DH], src.rearrange("p (h d) -> p h d", h=M_HEADS),
                                   ACT.Copy).then_inc(evac_done, 1)
                elif slab == 9:
                    act.activation(m_o[:, x, :], src, ACT.Sigmoid).then_inc(evac_done, 1)
                else:
                    if x == 0:
                        act.wait_ge(qk_var, 1)
                    act.activation(p_in[:, x, PAD:PAD + T], src, ACT.Copy).then_inc(evac_done, 1)
                act_split(act, half0[0] + o + HALF_SLOTS)
                if o == 0:
                    act.wait_ge(gates_done, 1)
                    act.activation(gates[:, :, :], ps[:, 6, 0:16].rearrange("p (a b) -> p a b", a=NT),
                                   ACT.Copy).then_inc(gates_evac, 1)
                if o == 4:
                    act.wait_ge(fabs_ready, 1)
                    link(act, act_chain, "act", act.activation(f_abs, f_abs, ACT.Exp, scale=-1.0))
                    act.activation(f_abs, f_abs, ACT.Ln, bias=1.0).then_inc(softplus_ready, 1)
                if o == 5:
                    act.wait_ge(mt_ready, 1)
                    act.activation(e_mt, m_t, ACT.Exp, scale=-1.0).then_inc(emt_ready, 1)
                if o == 7:
                    act.wait_ge(evac_done, EV_A + 8)
                    act.activation(sq[:, :, :].rearrange("p a b -> p (a b)"), z_qk.rearrange("p a b -> p (a b)"),
                                   ACT.Square).then_inc(qk_sq, 1)
                if o == 9:
                    act.wait_ge(qk_var, 1)
                    act.activation(rr, ss, ACT.Sqrt).then_inc(qk_std, 1)
                if o in (15, 17):
                    m = (o - 15) // 2
                    act.wait_ge(qk_turned, m + 1)
                    act.activation(qkT[:, 4 * m:4 * m + 4, :], ps[:, 4:6, :].rearrange("p a (b c) -> p (a b) c", b=2),
                                   ACT.Copy, scale=par[:, AQ + m:AQ + m + 1]).then_inc(qk_ready, 1)
                if o == 19:
                    act.wait_ge(conv_ready, 1)
                    act.activation(conv_out, conv_out, ACT.Silu).then_inc(mqk_ready, 1)
            act.wait_ge(decay_arg, 1)
            act.activation(decay, decay, ACT.Exp, scale=-1.0).then_inc(decay_ready, 1)
            act_attention(act, 0, A_HEADS, (att_score, att_prob, att_probT, att_nmax, a_sums))
            act_mix(act, 1, bank2(0), 4, 1)
            act_mix(act, 2, bank2(1), 6, 2)
            act.wait_ge(pool_done, 1)
            for c in range(2):
                last = act.activation(p_d[:, c, :], ps[:, 7, c * T:(c + 1) * T], ACT.Copy,
                                      scale=par[:, PSCALE + c:PSCALE + c + 1])
            last.then_inc(po_ready, 1)
            act.wait_ge(po_ready, 1)
            act.activation(ahi[:, 0:2, :], p_d, ACT.Copy).then_inc(mix_hi, 1)
            act.wait_ge(hc_ready, 1)
            act.activation(h_sq, h_out, ACT.Square).then_inc(hsq_ready, 1)
            act.wait_ge(hvar_ready, 1)
            act.activation(m_rr, m_ss, ACT.Sqrt).then_inc(hstd_ready, 1)
            act_mix(act, 4, bank2(6), 2, 3)

        def dve_first(dve):
            def chain(ins):
                link(dve, dve_chain, "dve", ins)

            for o in range(22):
                dve_split(dve, half0[0] + o + HALF_SLOTS)
                if o == 2:
                    dve.wait_ge(gates_turned, 1)
                    dve.tensor_scalar(i_g, ps[0:M_HEADS, 7, 0:T], gate_bias[:, 0:1], None, ALU.add)
                    chain(dve.tensor_scalar(f_g, ps[0:M_HEADS, 7, T:2 * T], gate_bias[:, 1:2], None, ALU.add))
                    dve.scalar_tensor_tensor(f_abs, f_g, -1.0, f_g, ALU.mult, ALU.max).then_inc(fabs_ready, 1)
                if o == 4:
                    dve.wait_ge(softplus_ready, 1)
                    chain(dve.scalar_tensor_tensor(f_log, f_g, 0.0, f_abs, ALU.min, ALU.subtract))
                    chain(dve.tensor_tensor_scan(g_cum, const("ones", M_HEADS), f_log, 0.0, ALU.mult, ALU.add))
                    chain(dve.tensor_tensor(u_g, i_g, g_cum, ALU.subtract))
                    chain(dve.tensor_tensor_scan(m_cum, const("ones", M_HEADS), u_g, 0.0, ALU.mult, ALU.max))
                    dve.tensor_tensor(m_t, g_cum, m_cum, ALU.add).then_inc(mt_ready, 1)
                if o == 8:
                    dve.wait_ge(ucols_turned, 1)
                    dve.tensor_copy(ucols, ps[:, 6, 0:16]).then_inc(ucols_read, 1)
                    dve.wait_ge(qk_sq, 1)
                    chain(dve.tensor_reduce(ss, sq[:, :, :].rearrange("p a b -> p (a b)").rearrange("p (g d) -> p g d", d=DH),
                                            AX, ALU.add))
                    dve.tensor_scalar(ss, ss, 1.0 / DH, RMS_EPS, ALU.mult, ALU.add).then_inc(qk_var, 1)
                if o == 10:
                    dve.wait_ge(qk_std, 1)
                    chain(dve.reciprocal(rr, rr))
                    z = z_qk.rearrange("p a (g d) -> p (a g) d", d=DH)
                    dve.tensor_tensor(z, z, bc(rr, 2, DH), ALU.mult).then_inc(qk_normed, 1)
                if o == 11:
                    dve.wait_ge(mcum_spread, 1)
                    dve.wait_ge(ucols_read, 1)
                    for h in range(M_HEADS):
                        m = ps[:, 7 - h // 2, (h % 2) * T:(h % 2 + 1) * T]
                        dve.scalar_tensor_tensor(decay[:, h, 0:T], m, ucols[:, h:h + 1], const("late"),
                                                 ALU.subtract, ALU.max)
                        last = dve.scalar_tensor_tensor(decay[:, h, T:T + P], m[:, P:T], ucols[:, 4 + h:5 + h],
                                                        const("late")[:, 0:P], ALU.subtract, ALU.max)
                    last.then_inc(decay_arg, 1)
                if o == 16:
                    dve.wait_ge(pads_ready, 2)
                    dve.wait_ge(evac_done, EV_A + 16)
                    for j in range(4):
                        for c in range(4):
                            x = conv_in[:, c, j:j + T]
                            tap = par[:, MCONV + 4 * j + c:MCONV + 4 * j + c + 1]
                            if j == 0:
                                last = dve.tensor_scalar(conv_out[:, c, :], x, tap, None, ALU.mult)
                            else:
                                last = dve.scalar_tensor_tensor(conv_out[:, c, :], x, tap, conv_out[:, c, :],
                                                                ALU.mult, ALU.add)
                        if j < 3:
                            chain(last)
                    last.then_inc(conv_ready, 1)
            dve_attention(dve, 0, A_HEADS, lambda i: const("causal"),
                          (att_score, att_prob, att_probT, att_nmax, a_sums))
            dve.wait_ge(heads_done, A_HEADS)
            chain(dve.reciprocal(a_rsum, a_sums))
            for a in range(NT):
                dve.tensor_tensor(a_out[:, a, :].rearrange("p (h d) -> p h d", d=DH),
                                  ps[:, 4 + a, :].rearrange("p (h d) -> p h d", d=DH),
                                  bc(a_rsum[:, :, a], 2, DH), ALU.mult).then_inc(ao_ready, 1)
            dve.wait_ge(decay_ready, 1)
            for h in range(M_HEADS):
                dve.wait_ge(mqk_done, h + 1)
                dve.scalar_tensor_tensor(decay[:, h, :], ps[:, h, 0:384], QK_SCALE, decay[:, h, :],
                                         ALU.mult, ALU.mult).then_inc(mw_ready, 1)
            dve_mix(dve, 1, bank2(0), 4)
            dve_mix(dve, 2, bank2(1), 6)
            dve.wait_ge(num_done, 1)
            num = [ps[:, 4 + a, 0:M_HEADS * (DH + 1)].rearrange("p (h e) -> p h e", h=M_HEADS) for a in range(NT)]
            least = ucols[:, 8:16].rearrange("p (a h) -> p a h", a=NT)
            for a in range(NT):
                last = dve.scalar_tensor_tensor(den[:, a, :], num[a][:, :, DH], -1.0, least[:, a, :], ALU.mult, ALU.max)
            chain(last)
            for a in range(NT):
                last = dve.tensor_tensor(den[:, a, :], num[a][:, :, DH], den[:, a, :], ALU.max)
            chain(last)
            chain(dve.reciprocal(den, den))
            for a in range(NT):
                last = dve.tensor_tensor(h_out[:, a, :].rearrange("p (h d) -> p h d", d=DH), num[a][:, :, 0:DH],
                                         bc(den[:, a, :], 2, DH), ALU.mult)
            last.then_inc(hc_ready, 1)
            dve_mix(dve, 3, p_d, 0)
            dve.wait_ge(hsq_ready, 1)
            chain(dve.tensor_reduce(m_ss, h_sq.rearrange("p a (h d) -> p (a h) d", d=DH), AX, ALU.add))
            dve.tensor_scalar(m_ss, m_ss, 1.0 / DH, RMS_EPS, ALU.mult, ALU.add).then_inc(hvar_ready, 1)
            dve.wait_ge(hc_ready, 1)
            chain(dve.tensor_tensor(m_o, m_o, bc(mng, 1, NT), ALU.mult))
            chain(dve.tensor_tensor(h_out, h_out, m_o, ALU.mult))
            dve.wait_ge(hstd_ready, 1)
            chain(dve.reciprocal(m_rr, m_rr))
            hh = h_out.rearrange("p a (h d) -> p (a h) d", d=DH)
            dve.tensor_tensor(hh, hh, bc(m_rr, 2, DH), ALU.mult).then_inc(hm_ready, 1)
            dve_mix(dve, 4, bank2(6), 2)

        def pool_first(pool):
            def chain(ins):
                link(pool, pool_chain, "pool", ins)

            pool.wait_ge(gates_done, 1)
            pool.wait_ge(a_ready, 4)
            pool.memset(conv_in[:, :, 0:3], 0.0).then_inc(pads_ready, 1)
            pool.wait_ge(qk_var, 1)
            pool.memset(p_in[:, :, 0:PAD], 0.0).then_inc(pads_ready, 1)
            pool.wait_ge(pads_ready, 3)
            pool.wait_ge(evac_done, EV_A + 22)
            n = PAD + T
            chain(pool.tensor_tensor(p_2[:, :, 1:n], p_in[:, :, 1:n], p_in[:, :, 0:n - 1], ALU.add))
            chain(pool.tensor_tensor(p_4[:, :, 3:n], p_2[:, :, 3:n], p_2[:, :, 1:n - 2], ALU.add))
            chain(pool.tensor_tensor(p_8[:, 0, 7:n], p_4[:, 1, 7:n], p_4[:, 1, 3:n - 4], ALU.add))
            p_16 = p_2[64:128, 0, :]
            chain(pool.tensor_tensor(p_16[:, 15:n], p_8[64:128, 0, 15:n], p_8[64:128, 0, 7:n - 8], ALU.add))
            inv = const("inv_count").rearrange("p (a b) -> p a b", a=2)
            pool.tensor_tensor(p_d[0:64, 0, :], p_2[0:64, 0, PAD:n], inv[0:64, 0, :], ALU.mult)
            pool.tensor_tensor(p_d[64:128, 0, :], p_4[64:128, 0, PAD:n], inv[64:128, 0, :], ALU.mult)
            pool.tensor_tensor(p_d[0:64, 1, :], p_8[0:64, 0, PAD:n], inv[0:64, 1, :], ALU.mult)
            chain(pool.tensor_tensor(p_d[64:128, 1, :], p_16[:, PAD:n], inv[64:128, 1, :], ALU.mult))
            pool.tensor_tensor(p_d, p_d, p_in[:, :, PAD:n], ALU.subtract).then_inc(pool_ready, 1)

        def pe_finish(pe, normed):
            if normed:
                pe.wait_ge(aff_ready, KC * sum(PRE[p][0] != "none" for p in range(9)))
            else:
                pe.wait_ge(x_ready, x_count(n_pre - 1))
            for a in range(NT):
                for b in range(2):
                    for c in range(4):
                        last = pe.transpose(ps[:, 2 * a + b if not normed else 2 + 2 * a + b, c * P:(c + 1) * P],
                                            xT[:, 4 * b + c, a * P:(a + 1) * P], ident)
                last.then_inc(out_turned, 1)

        def dve_finish(dve):
            b0 = 2 if len(plan) == 11 else 0
            for a in range(NT):
                dve.wait_ge(out_turned, a + 1)
                dve.tensor_copy(x_tok[:, a, :].rearrange("p (b c) -> p b c", b=2),
                                ps[:, b0 + 2 * a:b0 + 2 * a + 2, :]).then_inc(out_ready, 1)

        dup_landed = [sem(f"dup_landed{m}") for m in range(4)]
        w1_landed = sem("w1_landed")
        n_gates_raw = sem("n_gates_raw")
        n_gates_turned = sem("n_gates_turned")
        n_gates_ready = sem("n_gates_ready")
        hid_done = sem("hid_done")
        hid_bias_ready = sem("hid_bias_ready")
        hid_ready = sem("hid_ready")
        hid_spread = sem("hid_spread")
        kc_done = sem("kc_done")
        kc_ready = sem("kc_ready")
        vc_done = sem("vc_done")
        vc_ready = sem("vc_ready")
        c_scores_done = sem("c_scores_done")
        c_arg_ready = sem("c_arg_ready")
        c_exp_ready = sem("c_exp_ready")
        c_prob_ready = sem("c_prob_ready")
        c_turned = sem("c_turned")
        c_probT_ready = sem("c_probT_ready")
        c_done = sem("c_done")
        coef_ready = sem("coef_ready")
        part_ready = sem("part_ready")
        acc_ready = sem("acc_ready")
        n_bufs = [(n_score, n_prob, n_probT, n_nmax, n_sums[:, b * N_HEADS:(b + 1) * N_HEADS, :]) for b in range(2)]

        def pool_load_nsa(pool):
            pool.wait_ge(x_ready, x_count(1))
            pool.wait_ge(rows_stored, 16)
            shifted = bass.AP(tensor=scratch.tensor, offset=scratch.offset, ap=[[1, P], [BIAS_COLS, N_HEADS], [1, T]])
            pool.dma_start(bias, shifted).then_inc(bias_landed, 16)

        def pool_nsa(pool):
            pool.wait_ge(bias_landed, 16)
            pool.tensor_tensor(bias[:, :, P:T], bias[:, :, P:T], bc(const("causal_rev"), 1, N_HEADS),
                               ALU.add).then_inc(bias_ready, 1)
            pool.wait_ge(a_ready, 4 * 4)
            for z, dst in enumerate((w1_k, w1_v)):
                pool.dma_start(dst, io["nsa_cmp_w1_2"][0, z].rearrange("l d e -> (l d) e").rearrange("(m p) e -> p m e", p=P)) \
                    .then_inc(w1_landed, 16)
            pool_scale_x(pool, 3)
            for m, (dst, slab) in enumerate(((z_k, 4), (z_v, 5), (k_sel, 6), (k_win, 8))):
                pool.wait_ge(evac_done, EV_N + 2 * slab + 2)
                off = 1 if m < 2 else 0
                for g in range(N_GROUPS):
                    lo, hi = dst[0:64, g, off:off + T], dst[64:128, g, 0:T]
                    pool.dma_start(hi if g % 2 == 0 else lo, lo if g % 2 == 0 else hi).then_inc(dup_landed[m], 16)
            for part in range(8):
                pool.wait_ge(part_ready, part + 1)
                a, half = part // 2 % 2, part % 2
                cols = n_acc[:, a, half * 512:(half + 1) * 512]
                pool.tensor_tensor(cols, cols, n_tmp[:, part % 2, :], ALU.add).then_inc(acc_ready, 1)

        def n_bank(a, half):
            return ps[:, 4 + 2 * a + half, :]

        def pe_nsa(pe):
            pe.wait_ge(a_ready, 4 * 4)
            for a in range(NT):
                for k in range(KC):
                    last = pe.matmul(ps[:, 4, a * 48:(a + 1) * 48],
                                     xT[:, k, a * P:(a + 1) * P], gate_w2[:, k, :],
                                     start=k == 0, stop=k == KC - 1)
            last.then_inc(nsa_gates_done, 1)
            for o in range(0, 20, 2):
                if o == 2:
                    pe.wait_ge(n_gates_raw, 1)
                    pe.matmul(ps[:, 5, 0:96], const("flip"), n_gates.rearrange("p a b -> p (a b)"), start=True,
                              stop=True).then_inc(n_gates_turned, 1)
                if o == 16:
                    pe.wait_ge(w1_landed, 32)
                    for z, (src, w1) in enumerate(((z_k, w1_k), (z_v, w1_v))):
                        pe.wait_ge(dup_landed[z], 64)
                        for m in range(CMP_LEN // 2):
                            blocks = src[:, :, 1 + 2 * m:2 + 2 * m + CMP_STRIDE * (N_CMP - 1):CMP_STRIDE]
                            pe.matmul(ps[:, 5, z * 64:z * 64 + 60].rearrange("p (g n) -> p g n", g=N_GROUPS),
                                      w1[:, m, :], blocks, start=m == 0, stop=m == CMP_LEN // 2 - 1)
                        for m in range(CMP_LEN // 2):
                            last = pe.matmul(ps[:, 6, z:z + 1], w1[:, m, :],
                                             par[:, CPOS + 16 * z + m:CPOS + 16 * z + m + 1],
                                             start=m == 0, stop=m == CMP_LEN // 2 - 1)
                        last.then_inc(hid_done, 1)
                if o == 18:
                    pe.wait_ge(hid_ready, 2)
                    pe.matmul(ps[:, 7, 0:60], w2_k[:, :, :].rearrange("p a b -> p (a b)"), hidT[:, 0, :],
                              start=True, stop=True).then_inc(kc_done, 1)
                    pe.wait_ge(hid_spread, 1)
                    for half in range(2):
                        last = pe.matmul(ps[0:8 * N_CMP, 4, half * DH:(half + 1) * DH],
                                         hid_heads[:, half * 8:half * 8 + 8, :].rearrange("p a b -> p (a b)"),
                                         w2_v[:, :], start=True, stop=True)
                    last.then_inc(vc_done, 1)
                if o in (14, 18):
                    pe_tile_tokens(pe, half0[4], EV_N, o)
                else:
                    pe_tile_channels(pe, half0[4], EV_N, o)
                    pe_tile_channels(pe, half0[4], EV_N, o + 1)
            def q(i, t):
                return n_qT[64 * (i % 2):64 * (i % 2) + 64, i // 2, t * P:(t + 1) * P]

            pe.wait_ge(evac_done, EV_N + 20)
            pe.wait_ge(kc_ready, 1)
            pe.wait_ge(hid_bias_ready, 2)
            pe.wait_ge(vc_ready, 1)
            for i in range(N_HEADS):
                lo, g = 64 * (i % 2), i // 4
                for a in range(NT):
                    last = pe.matmul(ps[:, 4 + 2 * (i % 2) + a, (i // 2) * N_CMP:(i // 2 + 1) * N_CMP], q(i, a),
                                     kcT[lo:lo + 64, g * N_CMP:(g + 1) * N_CMP], start=True, stop=True)
            last.then_inc(c_scores_done, 1)
            pe.wait_ge(c_prob_ready, 1)
            for a in range(NT):
                for half in range(2):
                    last = pe.transpose(ps[0:8 * N_CMP, 0, (2 * a + half) * P:(2 * a + half + 1) * P],
                                        c_score[:, a, half * 120:(half + 1) * 120], ident)
            last.then_inc(c_turned, 1)
            pe.wait_ge(c_probT_ready, 1)
            for a in range(NT):
                for half in range(2):
                    pe.matmul(n_bank(a, half), c_probT[0:8 * N_CMP, 2 * a + half, :], c_val[0:8 * N_CMP, half, :],
                              start=True, stop=True).then_inc(c_done, 1)
            for b, (k, v) in enumerate(((k_sel, v_sel), (k_win, v_win))):
                pe.wait_ge(dup_landed[2 + b], 64)
                if b == 0:
                    pe.wait_ge(coef_ready, 4)
                else:
                    pe.wait_ge(part_ready, 4)
                pe_attention(pe, A_HEADS + b * N_HEADS, N_HEADS, q,
                             lambda i, n: k[64 * (i % 2):64 * (i % 2) + 64, i // 4, 0:n * P],
                             lambda i, t: v[:, t, (i // 4) * DH:(i // 4 + 1) * DH],
                             lambda i, t: n_bank(t, i // 8)[:, (i % 8) * DH:(i % 8 + 1) * DH], n_bufs[b])
            pe_turn_mix(pe, n_acc, acc_ready, 8, 3, "flip")

        def pe_turn_mix(pe, src, ready, count, before, how):
            pe.wait_ge(ready, count)
            for c in range(KC):
                for a in range(NT):
                    dst = ps[:, c // 2, (c % 2) * T + a * P:(c % 2) * T + (a + 1) * P]
                    if how == "flip":
                        last = pe.matmul(dst, src[:, a, c * P:(c + 1) * P], const("flip"), start=True, stop=True)
                    else:
                        last = pe.transpose(dst, src[:, a, c * P:(c + 1) * P], ident)
                if c % 2:
                    last.then_inc(mix_turned, 1)

        def act_mix_all(act, before):
            for b in range(4):
                act_mix(act, 0, bank2(b), 2 * b, before + b + 1)

        def dve_mix_all(dve, before):
            for b in range(4):
                dve_mix(dve, before + b + 1, bank2(b), 2 * b)

        def act_nsa(act):
            act.wait_ge(nsa_gates_done, 1)
            act.activation(n_gates, ps[:, 4, 0:96].rearrange("p (a b) -> p a b", a=NT), ACT.Copy).then_inc(n_gates_raw, 1)
            for o in range(20):
                slab, x = o // 2, o % 2
                src = ps[:, o % 4, 0:T]
                if slab in (7, 9) and x == 0:
                    act.wait_ge(token_tile, TT_N + (slab - 5) // 2)
                else:
                    act.wait_ge(half_done, half0[4] + o + 1)
                if slab < 4:
                    for a in range(NT):
                        last = act.activation(n_qT[:, o, a * P:(a + 1) * P][:, ::-1], src[:, a * P:(a + 1) * P],
                                              ACT.Copy, scale=QK_SCALE)
                    last.then_inc(evac_done, 1)
                elif slab in (7, 9):
                    act.activation((v_sel if slab == 7 else v_win)[:, x, :], src, ACT.Copy).then_inc(evac_done, 1)
                else:
                    dst, off = {4: (z_k, 1), 5: (z_v, 1), 6: (k_sel, 0), 8: (k_win, 0)}[slab]
                    act.activation(dst[0:64, 2 * x, off:off + T], src[0:64, :], ACT.Copy)
                    act.activation(dst[64:128, 2 * x + 1, 0:T], src[64:128, :], ACT.Copy).then_inc(evac_done, 1)
                act_split(act, half0[4] + o + HALF_SLOTS)
                if o == 1:
                    act.wait_ge(n_gates_turned, 1)
                    act.activation(n_gates, ps[:, 5, 0:96].rearrange("p (a b) -> p a b", a=NT),
                                   ACT.Sigmoid).then_inc(n_gates_ready, 1)
                if o == 16:
                    for z in range(2):
                        act.wait_ge(hid_done, z + 1)
                        act.activation(hid_bias[:, z:z + 1], ps[:, 6, z:z + 1], ACT.Copy).then_inc(hid_bias_ready, 1)
                    act.wait_ge(hid_bias_ready, 2)
                    for z in range(2):
                        act.activation(hidT[:, z, :], ps[:, 5, z * 64:z * 64 + 60], ACT.Gelu_apprx_tanh,
                                       bias=hid_bias[:, z:z + 1]).then_inc(hid_ready, 1)
                if o == 18:
                    act.wait_ge(kc_done, 1)
                    act.activation(kcT, ps[:, 7, 0:60], ACT.Copy).then_inc(kc_ready, 1)
            act.wait_ge(c_arg_ready, 1)
            act.activation(c_score, c_score, ACT.Exp).then_inc(c_exp_ready, 1)
            act.wait_ge(c_turned, 1)
            act.activation(c_probT[0:8 * N_CMP, :, :], ps[0:8 * N_CMP, 0, :].rearrange("p (a b) -> p a b", a=4),
                           ACT.Copy).then_inc(c_probT_ready, 1)
            for b in range(2):
                act_attention(act, A_HEADS + b * N_HEADS, N_HEADS, n_bufs[b])
            act_mix_all(act, 3)

        def dve_gated(dve, a, half, branch, dst):
            co = n_coef[:, branch * N_HEADS + 8 * half:branch * N_HEADS + 8 * half + 8, a]
            return dve.tensor_tensor(dst.rearrange("p (h d) -> p h d", d=DH),
                                     n_bank(a, half).rearrange("p (h d) -> p h d", d=DH), bc(co, 2, DH), ALU.mult)

        def dve_nsa(dve):
            def chain(ins):
                link(dve, dve_chain, "dve", ins)

            for o in range(20):
                dve_split(dve, half0[4] + o + HALF_SLOTS)
                if o == 17:
                    dve.wait_ge(hid_ready, 2)
                    dve.tensor_copy(hid_heads.rearrange("p (g q) n -> p g q n", g=N_GROUPS),
                                    bc(hidT[:, 1, :].rearrange("p (g n) -> p g n", g=N_GROUPS), 2, 4)).then_inc(hid_spread, 1)
                if o == 18:
                    dve.wait_ge(vc_done, 1)
                    for half in range(2):
                        last = dve.tensor_tensor(c_val[0:120, half, :].rearrange("p (h d) -> p h d", d=DH),
                                                 bc(ps[0:120, 4, half * DH:(half + 1) * DH], 1, 8),
                                                 bc(const("own_head", 120), 2, DH), ALU.mult)
                    last.then_inc(vc_ready, 1)
            dve.wait_ge(hid_done, 2)
            dve.wait_ge(cmp_bias_ready, 2)
            dve.wait_ge(c_scores_done, 1)
            for odd in range(2):
                score, add = (x.rearrange("p a (h b n) -> p a h b n", b=2, n=N_CMP)[:, :, :, odd, :]
                              for x in (c_score, cmp_bias[:, :, :]))
                src = ps[:, 4 + 2 * odd:6 + 2 * odd, 0:120].rearrange("p a (h n) -> p a h n", n=N_CMP)
                last = dve.tensor_tensor(score, src, add, ALU.add)
            chain(last)
            by_head = c_score.rearrange("p a (h n) -> p (a h) n", n=N_CMP)
            c_m, c_s = (x.rearrange("p a h -> p (a h)") for x in (c_max, c_sum))
            chain(dve.tensor_reduce(c_m, by_head, AX, ALU.max))
            dve.tensor_tensor(by_head, by_head, bc(c_m, 2, N_CMP), ALU.subtract).then_inc(c_arg_ready, 1)
            dve.wait_ge(c_exp_ready, 1)
            chain(dve.tensor_reduce(c_s, by_head, AX, ALU.add))
            for a in range(NT):
                last = dve.tensor_tensor(c_score[:, a, :].rearrange("p (h n) -> p h n", n=N_CMP),
                                         c_score[:, a, :].rearrange("p (h n) -> p h n", n=N_CMP),
                                         bc(const("cmp_valid")[:, a * N_CMP:(a + 1) * N_CMP], 1, N_HEADS), ALU.mult)
            last.then_inc(c_prob_ready, 1)
            chain(dve.reciprocal(c_s, c_s))
            dve.wait_ge(n_gates_ready, 1)
            chain(dve.tensor_tensor(n_coef[:, 0:N_HEADS, :].rearrange("p h a -> p a h"), c_sum,
                                    n_gates.rearrange("p a (h b) -> p a h b", b=3)[:, :, :, 0], ALU.mult))
            dve.wait_ge(c_prob_ready, 1)
            for a in range(NT):
                for half in range(2):
                    dve.wait_ge(c_done, 2 * a + half + 1)
                    dve_gated(dve, a, half, 0, n_acc[:, a, half * 512:(half + 1) * 512]).then_inc(coef_ready, 1)
            dve.wait_ge(bias_ready, 1)
            for b in range(2):
                dve_attention(dve, A_HEADS + b * N_HEADS, N_HEADS, lambda i: bias[:, i, :], n_bufs[b])
                dve.wait_ge(heads_done, A_HEADS + (b + 1) * N_HEADS)
                hs = slice(b * N_HEADS, (b + 1) * N_HEADS)
                chain(dve.reciprocal(n_rsum[:, hs, :], n_sums[:, hs, :]))
                chain(dve.tensor_tensor(n_coef[:, (b + 1) * N_HEADS:(b + 2) * N_HEADS, :].rearrange("p h a -> p a h"),
                                        n_rsum[:, hs, :].rearrange("p h a -> p a h"),
                                        n_gates.rearrange("p a (h b) -> p a h b", b=3)[:, :, :, b + 1], ALU.mult))
                for a in range(NT):
                    for half in range(2):
                        part = 4 * b + 2 * a + half
                        if part >= 2:
                            dve.wait_ge(acc_ready, part - 1)
                        dve_gated(dve, a, half, b + 1, n_tmp[:, part % 2, :]).then_inc(part_ready, 1)
            dve_mix_all(dve, 4)


        N_LEVELS = len(LEVELS)
        r_gain_landed = sem("r_gain_landed")
        lb_arg = sem("lb_arg")
        lb_exp = sem("lb_exp")
        f_ready = sem("f_ready")
        logf_ready = sem("logf_ready")
        k_ready = sem("k_ready")
        level_arg = sem("level_arg")
        level_exp = sem("level_exp")
        level_ready = sem("level_ready")
        level_scored = sem("level_scored")
        level_placed = sem("level_placed")
        diag_done = sem("diag_done")
        diag_ready = sem("diag_ready")
        cross_ready = sem("cross_ready")
        r_out_done = sem("r_out_done")
        r_sq_ready = sem("r_sq_ready")
        r_var_ready = sem("r_var_ready")
        r_std_ready = sem("r_std_ready")
        r_silu_ready = sem("r_silu_ready")
        r_gate_ready = sem("r_gate_ready")
        r_o_ready = sem("r_o_ready")
        level_buf = (xc, sq)

        def halves(v, m):
            return v.rearrange("p a b -> p (a b)").rearrange("p (n b m) -> p n b m", b=2, m=m)

        def tiles(v):
            return v.rearrange("p a b -> p (a b)").rearrange("p (i n) -> p i n", n=P)

        def level_bank(u):
            b = 4 + 2 * (u % 2)
            return ps[:, b:b + 2, :]

        def pool_hgrn(pool):
            pool.wait_ge(x_ready, x_count(4))
            pool.dma_start(r_gain, spread(io["hgrn_norm_gain_2"][0], P)).then_inc(r_gain_landed, 16)
            pool_scale_x(pool, 6)
            pool.wait_ge(evac_done, EV_H + 16)
            pool.wait_ge(k_ready, 1)
            for u in range(N_LEVELS + 1):
                pool.wait_ge(level_exp, u + 1)
                m = LEVELS[u] if u < N_LEVELS else P
                y, k, q = (halves(v, m) for v in (level_buf[u % 2][:, :, :], r_k, r_q))
                pool.tensor_tensor(y[:, :, 0, :], y[:, :, 0, :], k[:, :, 0, :], ALU.mult)
                pool.tensor_tensor(y[:, :, 1, :], y[:, :, 1, :], q[:, :, 1, :], ALU.mult).then_inc(level_ready, 1)
            pool.wait_ge(r_silu_ready, 1)
            pool.wait_ge(r_gain_landed, 16)
            g = r_g.rearrange("p a (h d) -> p (a h) d", d=P)
            pool.tensor_tensor(g, g, bc(r_gain, 1, NT * H_HEADS), ALU.mult).then_inc(r_gate_ready, 1)

        def pe_hgrn(pe):
            pe.wait_ge(a_ready, 4 * 7)

            def level(u):
                pe.wait_ge(level_ready, u + 1)
                if u < 2:
                    pe.wait_ge(diag_ready, 1)
                else:
                    pe.wait_ge(level_placed, u - 1)
                y = tiles(level_buf[u % 2][:, :, :])
                for i in range(2 * H_HEADS):
                    odd = y[:, i, :].rearrange("p (n b m) -> p n b m", b=2, m=LEVELS[u])[:, :, 1, :]
                    dst = level_bank(u)[:, i // 8, (i % 8) * 64:(i % 8 + 1) * 64]
                    last = pe.matmul(dst.rearrange("p (n m) -> p n m", m=LEVELS[u]), y[:, i, :], odd, start=True, stop=True)
                last.then_inc(level_scored, 1)

            for o in range(0, 32, 2):
                if o == 16:
                    pe.wait_ge(evac_done, EV_H + 16)
                    pe.wait_ge(k_ready, 1)
                    for i in range(2 * H_HEADS):
                        last = pe.matmul(ps[:, 4 + i // 4, (i % 4) * P:(i % 4 + 1) * P], tiles(r_k)[:, i, :],
                                         tiles(r_q)[:, i, :], start=True, stop=True)
                    last.then_inc(diag_done, 1)
                if o >= 18:
                    level((o - 18) // 2)
                if o < 16:
                    pe_tile_channels(pe, half0[8], EV_H, o)
                    pe_tile_channels(pe, half0[8], EV_H, o + 1)
                else:
                    pe_tile_tokens(pe, half0[8], EV_H, o)
            pe.wait_ge(level_ready, N_LEVELS + 1)
            pe.wait_ge(level_placed, N_LEVELS - 1)
            y = level_buf[N_LEVELS % 2]
            for h in range(H_HEADS):
                last = pe.matmul(level_bank(N_LEVELS)[:, h // 4, (h % 4) * P:(h % 4 + 1) * P], y[:, h, 0:P], y[:, h, P:T],
                                 start=True, stop=True)
            last.then_inc(level_scored, 1)
            pe.wait_ge(level_placed, N_LEVELS)
            pe.wait_ge(evac_done, EV_H + 24)
            pe.wait_ge(cross_ready, 1)
            for a in range(NT):
                for h in range(H_HEADS):
                    dst = ps[:, 4 + 2 * a + h // 4, (h % 4) * P:(h % 4 + 1) * P]
                    cols = slice(h * P, (h + 1) * P)
                    if a == 1:
                        pe.matmul(dst, r_cross[:, h, :], r_v[:, 0, cols], start=True, stop=False)
                    last = pe.matmul(dst, r_at[:, 2 * h + a, :], r_v[:, a, cols], start=a == 0, stop=True)
                last.then_inc(r_out_done, 1)
            pe.wait_ge(evac_done, EV_H + 32)
            pe_turn_mix(pe, r_o, r_o_ready, NT, 7, "transpose")

        def act_hgrn(act):
            act.wait_ge(lb_arg, 1)
            act.activation(lb[:, 0:2, :], lb[:, 0:2, :], ACT.Exp).then_inc(lb_exp, 1)

            def exps(u):
                act.wait_ge(level_arg, u + 1)
                buf = level_buf[u % 2][:, :, :]
                act.activation(buf, buf, ACT.Exp).then_inc(level_exp, 1)

            for o in range(32):
                slab, x = o // 2, o % 2
                src = ps[:, o % 4, 0:T]
                if slab >= 8 and x == 0:
                    act.wait_ge(token_tile, TT_H + slab - 7)
                else:
                    act.wait_ge(half_done, half0[8] + o + 1)
                if slab < 4:
                    act.activation(r_k[:, o, :], src, ACT.Sigmoid, scale=-1.0)
                    act.activation(r_b[:, o, :], src, ACT.Sigmoid).then_inc(evac_done, 1)
                elif slab < 8:
                    act.activation(r_q[:, o - 8, :], src, ACT.Silu).then_inc(evac_done, 1)
                else:
                    act.activation((r_v if slab < 12 else r_g)[:, x, 256 * (slab % 4):256 * (slab % 4 + 1)], src,
                                   ACT.Copy).then_inc(evac_done, 1)
                act_split(act, half0[8] + o + HALF_SLOTS)
                if o == 7:
                    act.wait_ge(f_ready, 1)
                    for h in range(H_HEADS):
                        act.activation(r_b[:, h, :], r_b[:, h, :], ACT.Ln, scale=lb[:, 3, h:h + 1],
                                       bias=lb[:, 2, h:h + 1]).then_inc(logf_ready, 1)
                if o in (16, 17):
                    exps(o - 16)
                if o >= 20 and o % 2 == 0:
                    exps((o - 20) // 2 + 2)
            act.wait_ge(level_scored, N_LEVELS + 1)
            act.activation(r_cross.rearrange("p (b h) n -> p b (h n)", b=2), level_bank(N_LEVELS), ACT.Copy).then_inc(cross_ready, 1)
            act.wait_ge(evac_done, EV_H + 32)
            act.activation(r_g, r_g, ACT.Silu).then_inc(r_silu_ready, 1)
            for a in range(NT):
                act.wait_ge(r_out_done, a + 1)
                act.activation(xc[:, 4 * a:4 * a + 4, :].rearrange("p a b -> p (a b)"),
                               ps[:, 4 + 2 * a:6 + 2 * a, :].rearrange("p a b -> p (a b)"), ACT.Square).then_inc(r_sq_ready, 1)
            for a in range(NT):
                act.wait_ge(r_var_ready, a + 1)
                act.activation(r_rr[:, 8 * a:8 * a + 8], r_ss[:, 8 * a:8 * a + 8], ACT.Sqrt).then_inc(r_std_ready, 1)
            act_mix_all(act, 7)

        def dve_hgrn(dve):
            def chain(ins):
                link(dve, dve_chain, "dve", ins)

            raw0, raw1 = par[:, LB:LB + 8], par[:, LB + 8:LB + 16]
            e0, e1, low, top = (lb[:, n, :] for n in range(4))
            chain(dve.tensor_tensor(low, raw0, raw1, ALU.max))
            dve.tensor_tensor(e0, raw0, low, ALU.subtract)
            dve.tensor_tensor(e1, raw1, low, ALU.subtract).then_inc(lb_arg, 1)
            dve.wait_ge(lb_exp, 1)
            chain(dve.tensor_tensor(top, e0, e1, ALU.add))
            chain(dve.reciprocal(top, top))
            dve.tensor_tensor(e0, e0, top, ALU.mult)
            chain(dve.tensor_tensor(e1, e1, top, ALU.mult))
            chain(dve.tensor_tensor(low, e0, e1, ALU.add))
            chain(dve.tensor_tensor(low, low, e0, ALU.subtract))
            chain(dve.tensor_scalar(top, low, -1.0, 1.0, ALU.mult, ALU.add))

            def args(u):
                if u >= 2:
                    dve.wait_ge(level_scored, u - 1)
                m = LEVELS[u] if u < N_LEVELS else P
                e, b = (halves(v, m) for v in (level_buf[u % 2][:, :, :], r_b))
                ref = b[:, :, 0, m - 1:m].to_broadcast([P, H_HEADS * T // (2 * m), m])
                dve.tensor_tensor(e[:, :, 0, :], ref, b[:, :, 0, :], ALU.subtract)
                if u < N_LEVELS:
                    dve.tensor_tensor(e[:, :, 1, :], b[:, :, 1, :], ref, ALU.subtract).then_inc(level_arg, 1)
                else:
                    dve.tensor_copy(e[:, :, 1, :], b[:, :, 1, :]).then_inc(level_arg, 1)

            def place(u):
                dve.wait_ge(level_scored, u + 1)
                m = LEVELS[u]
                mask = const("levels")[:, u * 64:(u + 1) * 64].bitcast(I32)
                mask = bc(mask, 1, 2 * H_HEADS).rearrange("p a (n m) -> p a n m", m=m)
                dst = r_at.rearrange("p a (n b m) -> p a n b m", b=2, m=m)[:, :, :, 1, :]
                src = level_bank(u).rearrange("p b (i n m) -> p (b i) n m", n=64 // m, m=m)
                dve.copy_predicated(dst, mask, src).then_inc(level_placed, 1)

            for o in range(32):
                dve_split(dve, half0[8] + o + HALF_SLOTS)
                if o == 7:
                    dve.wait_ge(evac_done, EV_H + 8)
                    dve.tensor_scalar(r_b, r_b, TINY, None, ALU.max).then_inc(f_ready, 1)
                    dve.tensor_tensor(r_k, r_k, bc(top, 2, T), ALU.mult).then_inc(k_ready, 1)
                if o == 9:
                    for h in range(H_HEADS):
                        dve.wait_ge(logf_ready, h + 1)
                        last = dve.tensor_tensor_scan(r_b[:, h, :], const("restart"), r_b[:, h, :], 0.0, ALU.mult, ALU.add)
                    chain(last)
                if o in (12, 14):
                    args((o - 12) // 2)
                if o == 17:
                    dve.wait_ge(diag_done, 1)
                    dve.tensor_tensor(r_at, ps[:, 4:8, :].rearrange("p b (i n) -> p (b i) n", n=P),
                                      bc(ident, 1, 2 * H_HEADS), ALU.mult).then_inc(diag_ready, 1)
                    dve.wait_ge(diag_ready, 1)
                if o >= 19 and o % 2:
                    u = (o - 19) // 2
                    place(u)
                    if u + 2 <= N_LEVELS:
                        args(u + 2)
            for a in range(NT):
                dve.wait_ge(r_sq_ready, a + 1)
                cols = slice(8 * a, 8 * a + 8)
                chain(dve.tensor_reduce(r_ss[:, cols], xc[:, 4 * a:4 * a + 4, :].rearrange("p a b -> p (a b)")
                                        .rearrange("p (h d) -> p h d", d=P), AX, ALU.add))
                dve.tensor_scalar(r_ss[:, cols], r_ss[:, cols], 1.0 / P, RMS_EPS, ALU.mult, ALU.add).then_inc(r_var_ready, 1)
            dve.wait_ge(r_gate_ready, 1)
            for a in range(NT):
                cols = slice(8 * a, 8 * a + 8)
                dve.wait_ge(r_std_ready, a + 1)
                chain(dve.reciprocal(r_rr[:, cols], r_rr[:, cols]))
                chain(dve.tensor_tensor(r_o[:, a, :].rearrange("p (h d) -> p h d", d=P),
                                        ps[:, 4 + 2 * a:6 + 2 * a, :].rearrange("p b (h d) -> p (b h) d", d=P),
                                        bc(r_rr[:, cols], 2, P), ALU.mult))
                dve.tensor_tensor(r_o[:, a, :], r_o[:, a, :], r_g[:, a, :], ALU.mult).then_inc(r_o_ready, 1)
            dve_mix_all(dve, 8)

        block = ctx.enter_context(nc.Block())

        @block.sync
        def _(sp):
            def load(slab, matrix, ap):
                dst = raw[:, slab % RAW_SLOTS, :]
                if matrix < 2:
                    dst = dst.rearrange("p (k n) -> p k n", k=KC)
                    src = ap.rearrange("(k p) n -> p k n", p=P)
                else:
                    dst = dst.rearrange("p (c n) -> p c n", c=2)
                    src = ap.rearrange("(c p) n -> p c n", p=P)
                sp.dma_start(dst, src).then_inc(raw_landed[slab % RAW_SLOTS], 16)

            for n, e in enumerate(plan):
                if e[0] == "lin":
                    for i, col in enumerate(e[2]):
                        slab = slab0[n] + i
                        if slab >= RAW_SLOTS:
                            sp.wait_ge(lo_ready, raw_freed(slab - RAW_SLOTS))
                        load(slab, 0, e[1][:, col:col + 256])
                    continue
                for m in range(3):
                    sp.wait_ge(lo_ready, raw_freed(slab0[n] + m - RAW_SLOTS))
                    w = e[1][m]
                    load(slab0[n] + m, m, w[:, 0:256] if m < 2 else w[0:256, :])
                with sp.Fori(1, FFN_STEPS) as j:
                    for m in range(3):
                        sp.wait_ge(lo_ready, j * 6 + (half0[n] - 6 + LAST_OF[m]))
                        w = e[1][m]
                        load(slab0[n] + m, m, w[:, bass.ds(j * 256, 256)] if m < 2 else w[bass.ds(j * 256, 256), :])
            sp.wait_ge(out_ready, 2)
            sp.dma_start(out[0].rearrange("(a p) d -> p a d", p=P), x_tok[:, :, :]).then_inc(stored, 16)
            sp.wait_ge(stored, 16)

        row_sources = [
            (0, 0, io["ln1_g"].rearrange("a (k p) -> (a k) p", p=P)),
            (0, LN2, io["ln2_g"].rearrange("a (k p) -> (a k) p", p=P)),
            (0, LNG, io["ln_gain_2"].rearrange("i j (k p) -> (i j k) p", p=P)),
            (0, LNB, io["ln_bias_2"].rearrange("i j (k p) -> (i j k) p", p=P)),
            (1, 0, io["m_conv"].rearrange("a j (c p) -> (a j c) p", p=P)),
            (1, PSCALE - MCONV, io["pool_scale"].rearrange("a (c p) -> (a c) p", p=P)),
            (1, LB - MCONV, io["hgrn_lb_2"].rearrange("i (k p) -> (i k) p", p=P)),
            (1, FCONV - MCONV, io["ffn_conv"][0, 0:2].rearrange("j (c p) -> (j c) p", p=P)),
            (2, 0, io["ffn_conv"][0, 2:3].rearrange("j (c p) -> (j c) p", p=P)),
            (2, CPOS - FCONV - 88, io["nsa_cmp_pos_2"][0].rearrange("z (l q) d -> (z l) (q d)", q=2)),
        ]
        N_ROW_DMAS = len(row_sources) + 4
        N_SMALL_DMAS = 14

        def spread(ap, n):
            return bass.AP(tensor=ap.tensor, offset=ap.offset, ap=[[0, P], [1, n]])

        @block.gpsimd
        def _(pool):
            for g, row, src in row_sources:
                pool.dma_start(rows[row:row + src.shape[0], g, :], src).then_inc(rows_landed, 16)
            for n, name in ((AQ, "a_q_g"), (AK, "a_k_g")):
                for twice in range(2):
                    pool.dma_start(rows[n - MCONV:n - MCONV + 1, 1, twice * DH:(twice + 1) * DH],
                                   io[name]).then_inc(rows_landed, 16)
            pool.memset(m_v[:, :, :, DH:DH + 1], 1.0).then_inc(ones_ready, 1)
            pool.memset(pool_w, 0.0).then_inc(pads_ready, 1)
            pool.wait_ge(pads_ready, 1)
            small = [(gate_w, w_in[:, 1280:1288].rearrange("(k p) n -> p k n", p=P)),
                     (hot, io["distance_buckets"]), (table, io["rel_bias_2"]),
                     (gate_w2[:, :, :], n_in[:, 2560:2608].rearrange("(k p) n -> p k n", p=P)),
                     (w2_k[:, 0, :], io["nsa_cmp_w2_2"][0, 0]), (w2_k[:, 1, :], io["nsa_cmp_w2_2"][0, 0]),
                     (w2_v[:, :], io["nsa_cmp_w2_2"][0, 1]),
                     (mng, spread(io["m_norm_g"][0], 256)),
                     (gate_bias[:, 0:1], io["m_b_i"].rearrange("a h -> h a")),
                     (gate_bias[:, 1:2], io["m_b_f"].rearrange("a h -> h a"))]
            small += [(pool_w[64 * (g % 2):64 * (g % 2) + 64, g // 2, 64 * (g % 2):64 * (g % 2) + 64],
                       io["pool_w"][0, g]) for g in range(4)]
            for dst, src in small:
                pool.dma_start(dst, src).then_inc(small_landed, 16)
            assert len(small) == N_SMALL_DMAS
            pool.wait_ge(rows_evac, 1)
            pool.dma_start(scratch, bias_row).then_inc(rows_stored, 16)
            pool_first(pool)
            pool_scale_x(pool, 2)
            pool_load_nsa(pool)
            pool_nsa(pool)
            pool_scale_x(pool, 4)
            pool_scale_x(pool, 5)
            pool_hgrn(pool)
            pool_scale_x(pool, 7)
            pool.wait_ge(rows_stored, 16)

        @block.scalar
        def _(act):
            act.dma_start(x_tok, io["x"][0].rearrange("(a p) d -> p a d", p=P)).then_inc(x_landed, 16)
            act.dma_start(consts[:, :], io["shape_constants"]).then_inc(const_landed, 16)
            act_start(act)
            act_pre(act, 0)
            act_bias_rows(act)
            for h in range(HALF_SLOTS):
                act_split(act, h)
            act_first(act)
            act_project(act, 1)
            act_pre(act, 1)
            act_ffn(act, 2, 1)
            act_pre(act, 2)
            act_ffn(act, 3, 2)
            act_pre(act, 3)
            act_nsa(act)
            act_project(act, 5)
            act_pre(act, 4)
            act_ffn(act, 6, 4)
            act_pre(act, 5)
            act_ffn(act, 7, 5)
            act_pre(act, 6)
            act_hgrn(act)
            act_project(act, 9)
            act_pre(act, 7)
            act_ffn(act, 10, 7)
            act_pre(act, 8)

        @block.vector
        def _(dve):
            dve_start(dve)
            dve.wait_ge(const_landed, 16)
            dve.wait_ge(small_landed, 16 * N_SMALL_DMAS)
            dve_pre(dve, 0)
            dve_bias_rows(dve)
            for h in range(HALF_SLOTS):
                dve_split(dve, h)
            dve_first(dve)
            dve_project(dve, 1, 0, 0)
            dve_pre(dve, 1)
            dve_ffn(dve, 2, 1, 0)
            dve_pre(dve, 2)
            dve_ffn(dve, 3, 2, 1)
            dve_pre(dve, 3)
            dve_nsa(dve)
            dve_project(dve, 5, 3, 2)
            dve_pre(dve, 4)
            dve_ffn(dve, 6, 4, 3)
            dve_pre(dve, 5)
            dve_ffn(dve, 7, 5, 4)
            dve_pre(dve, 6)
            dve_hgrn(dve)
            dve_project(dve, 9, 6, 5)
            dve_pre(dve, 7)
            dve_ffn(dve, 10, 7, 6)
            dve_pre(dve, 8, split=False)
            dve_finish(dve)

        @block.tensor
        def _(pe):
            pe_start(pe)
            pe_pre(pe, 0)
            pe_bias_rows(pe)
            pe_first(pe)
            pe_project(pe, 1, 0)
            pe_pre(pe, 1)
            pe_ffn(pe, 2, 1)
            pe_pre(pe, 2)
            pe_ffn(pe, 3, 2)
            pe_pre(pe, 3)
            pe_nsa(pe)
            pe_project(pe, 5, 3)
            pe_pre(pe, 4)
            pe_ffn(pe, 6, 4)
            pe_pre(pe, 5)
            pe_ffn(pe, 7, 5)
            pe_pre(pe, 6)
            pe_hgrn(pe)
            pe_project(pe, 9, 6)
            pe_pre(pe, 7)
            pe_ffn(pe, 10, 7)
            pe_pre(pe, 8)
            pe_finish(pe, True)


_INS = ["x", "ln1_g", "w_in", "pool_w", "pool_scale", "m_conv", "m_b_i", "m_b_f", "m_norm_g", "a_q_g", "a_k_g",
        "w_out", "ln2_g", "w_up", "ffn_conv", "w_down", "rel_bias_2", "ln_gain_2", "ln_bias_2", "ffn1_w_gate_2",
        "ffn1_w_up_2", "ffn1_w_down_2", "ffn2_w_gate_2", "ffn2_w_up_2", "ffn2_w_down_2", "nsa_w_in_2",
        "nsa_w_out_2", "nsa_cmp_pos_2", "nsa_cmp_w1_2", "nsa_cmp_w2_2", "hgrn_w_in_2", "hgrn_w_out_2",
        "hgrn_norm_gain_2", "hgrn_lb_2"]
STOP = 11


def kernel(**inputs):
    import concourse.bacc as bacc
    from concourse.bass_utils import run_bass_kernel_spmd

    nc = bacc.Bacc("TRN2", target_bir_lowering=False, num_devices=1)
    arrays, io = {}, {}
    for name in _INS:
        arrays[name] = np.ascontiguousarray(inputs[name])
    arrays["shape_constants"], const_at = shape_constants()
    arrays["distance_buckets"] = distance_buckets()
    for name, a in arrays.items():
        io[name] = nc.dram_tensor(name, a.shape, mybir.dt.from_np(a.dtype), kind="ExternalInput").ap()
    out = nc.dram_tensor("out", (1, T, D), F32, kind="ExternalOutput").ap()
    build_program(nc, io, const_at, out, STOP)
    result = run_bass_kernel_spmd(nc, [arrays], core_ids=[0])
    return result.results[0]["out"]
```

```python
import math
from contextlib import ExitStack

import numpy as np
import concourse.bass as bass
from concourse import mybir

F32 = mybir.dt.float32
F32R = mybir.dt.float32r
BF16 = mybir.dt.bfloat16
I32 = mybir.dt.int32
ACT = mybir.ActivationFunctionType
ALU = mybir.AluOpType
AX = mybir.AxisListType.X

P = 128
D = 1024
T = 256
KC = D // P
NT = T // P
D_FF = 2816
FFN_STEPS = D_FF // (2 * P)
M_HEADS = 4
A_HEADS = 8
DH = 64
N_HEADS = 16
N_GROUPS = 4
REL_BUCKETS = 32
REL_EXACT = REL_BUCKETS // 2
REL_MAX_DIST = 128
CMP_STRIDE = 16
CMP_LEN = 32
N_CMP = T // CMP_STRIDE - 1
H_HEADS = 8
LN_EPS = 1e-5
RMS_EPS = 1e-6
MASKED = -1e30
TINY = 1e-19
ALPHA = (2.0 * 2) ** 0.25
QK_SCALE = DH ** -0.5
POOL_WINDOWS = (2, 4, 8, 16)
PAD = 16
BIAS_COLS = P + T
LEVELS = (64, 32, 16, 8, 4, 2, 1)

RAW_SLOTS = 3
HALF_SLOTS = 6
ARENA = 16500


def shape_constants():
    i = np.arange(P)
    t = np.arange(T)
    parts = {}
    parts["ident"] = np.eye(P)
    parts["flip"] = np.eye(P)[::-1]
    parts["mean"] = np.full((P, P), 1.0 / D)
    parts["causal"] = np.concatenate([np.zeros((P, P)), np.where(i[None, :] > i[:, None], MASKED, 0.0)], 1)
    parts["causal_rev"] = np.where(i[None, :] > P - 1 - i[:, None], MASKED, 0.0)
    parts["late"] = np.concatenate([np.where(i[None, :] < i[:, None], -MASKED, 0.0), np.zeros((P, P))], 1)
    inv = np.zeros((P, 2, T))
    for g, w in enumerate(POOL_WINDOWS):
        inv[64 * (g % 2):64 * (g % 2) + 64, g // 2] = 1.0 / np.minimum(t + 1, w)
    parts["inv_count"] = inv.reshape(P, -1)
    restart = np.ones((P, T))
    restart[:, ::P] = 0.0
    parts["restart"] = restart
    parts["ones"] = np.ones((P, T))
    valid = np.zeros((P, NT, N_CMP))
    for a in range(NT):
        valid[:, a] = (a * P + P - 1 - i)[:, None] >= CMP_STRIDE * np.arange(N_CMP)[None, :] + CMP_LEN - 1
    parts["cmp_add"] = np.where(valid > 0, 0.0, MASKED).reshape(P, -1)
    parts["cmp_valid"] = valid.reshape(P, -1)
    heads = np.zeros((P, 8))
    heads[np.arange(8 * N_CMP), np.arange(8 * N_CMP) // N_CMP] = 1.0
    parts["own_head"] = heads
    parts["levels"] = level_masks()
    parts["one"] = np.ones((P, 1))
    at, cols = {}, 0
    for name, a in parts.items():
        at[name] = (cols, a.shape[1])
        cols += a.shape[1]
    return np.concatenate(list(parts.values()), 1).astype(np.float32), at


def level_masks():
    i = np.arange(P)
    levels = []
    for m in LEVELS:
        t = i[i // m % 2 == 1]
        levels.append((i[:, None] // (2 * m) == t[None, :] // (2 * m)) & (i[:, None] // m % 2 == 0))
    return np.concatenate(levels, 1)


def distance_buckets():
    def one_hot(dist):
        n = np.maximum(dist, 0)
        large = REL_EXACT + (np.log(np.maximum(n, 1) / REL_EXACT) / math.log(REL_MAX_DIST / REL_EXACT)
                             * (REL_BUCKETS - REL_EXACT)).astype(np.int64)
        b = np.where(n < REL_EXACT, n, np.minimum(large, REL_BUCKETS - 1))
        return np.eye(REL_BUCKETS)[b].T

    full = one_hot(T - 1 - np.arange(BIAS_COLS))
    cmp_ = one_hot(T - CMP_LEN - np.arange(2 * T - CMP_LEN))
    return np.concatenate([full, cmp_], 1).astype(np.float32)


def build_program(nc, io, const_at, out, stop):
    ctx = ExitStack()
    with ctx:
        def sb(name, shape, dt=F32):
            return ctx.enter_context(nc.sbuf_tensor(name, shape, dt))

        def sem(name):
            return ctx.enter_context(nc.semaphore(name))

        n_const = sum(n for _, n in const_at.values())
        consts = sb("consts", [P, n_const])
        raw = sb("raw", [P, RAW_SLOTS, 2048])
        whi = sb("whi", [P, HALF_SLOTS, 1024], F32R)
        wlo = sb("wlo", [P, HALF_SLOTS, 1024], F32R)
        xT = sb("xT", [P, KC, T])
        xc = sb("xc", [P, KC, T])
        sq = sb("sq", [P, KC, T])
        ahi = sb("ahi", [P, KC, T], F32R)
        alo = sb("alo", [P, KC, T], F32R)
        var = sb("var", [P, T])
        rstd = sb("rstd", [P, T])
        table_use = sb("table_use", [P, 1])
        ghi = sb("ghi", [P, 2, T], F32R)
        glo = sb("glo", [P, 2, T], F32R)
        gate_act = sb("gate_act", [P, 2, T])
        conv_g = sb("conv_g", [P, 2, T])
        conv_u = sb("conv_u", [P, 2, T])
        gated = sb("gated", [P, 2, T])
        zeros = sb("zeros", [P, 512], BF16)
        par = sb("par", [P, 316])
        arena = sb("arena", [P, ARENA])
        cmp_bias = sb("cmp_bias", [P, NT, N_HEADS * N_CMP])
        scratch = nc.dram_tensor("bias_rows", (N_HEADS, 384), F32, kind="Internal").ap()
        ps = ctx.enter_context(nc.psum_tensor("ps", [P, 8, 512], F32))

        def const(name, rows=P):
            at, n = const_at[name]
            return consts[0:rows, at:at + n]

        ident = const("ident")

        def view(at, *shape, rows=P):
            n = int(np.prod(shape))
            assert at + n <= ARENA, (at, shape)
            v = arena[0:rows, at:at + n]
            if len(shape) == 2:
                v = v.rearrange("p (a b) -> p a b", a=shape[0])
            if len(shape) == 3:
                v = v.rearrange("p (a b c) -> p a b c", a=shape[0], b=shape[1])
            return at + n, v

        def bc(ap, axis, n):
            a = ap.unsqueeze(axis)
            shape = list(a.shape)
            shape[axis] = n
            return a.to_broadcast(shape)

        LN1, LN2, LNG, LNB = 0, 8, 16, 64
        MCONV, PSCALE, LB, AQ, AK, FCONV, CPOS = 112, 128, 130, 146, 147, 148, 280
        n_rows = (112, 124, 76)

        def spare(tensor, at, *shape, rows=P):
            v = tensor.rearrange("p a b -> p (a b)")[0:rows, at:at + int(np.prod(shape))]
            return v if len(shape) == 1 else v.rearrange("p (a b) -> p a b", a=shape[0])

        at, z_qk = view(0, NT, 1024)
        at, a_v = view(at, NT, 512)
        at, qkT = view(at, KC, T)
        at, m_v = view(at, NT, M_HEADS, DH + 1)
        at, m_o = view(at, NT, 256)
        at, conv_out = view(at, 4, T)
        at, decay = view(at, M_HEADS, 384)
        at, a_out = view(at, NT, 512)
        at, h_out = view(at, NT, 256)
        at, h_sq = view(at, NT, 256)
        at, att_score = view(at, 2, 384)
        at, att_prob = view(at, 2, 384)
        at, att_probT = view(at, 2, 384)
        at, att_nmax = view(at, 2, 2)
        att_end = at
        at, gates = view(at, NT, 8)
        at, ss = view(at, 32)
        at, rr = view(at, 32)
        at, a_sums = view(at, A_HEADS, 2)
        at, a_rsum = view(at, A_HEADS, 2)
        at, ucols = view(at, 16)
        at, den = view(at, NT, M_HEADS)
        at, m_ss = view(at, 8)
        at, m_rr = view(at, 8)
        at, gate_w = view(at, KC, 8)
        at, mng = view(at, 256)
        at, pool_w = view(at, 2, P)
        at, gate_bias = view(at, 2, rows=M_HEADS)
        startup = at
        i_g, f_g = (gate_act[0:M_HEADS, n, :] for n in range(2))
        f_abs, f_log = (conv_g[0:M_HEADS, n, :] for n in range(2))
        g_cum, u_g = (conv_u[0:M_HEADS, n, :] for n in range(2))
        m_cum, m_t = (gated[0:M_HEADS, n, :] for n in range(2))
        e_mt = f_abs
        conv_in = spare(xc, 0, 4, 3 + T)
        p_d = spare(xc, 4 * (3 + T), 2, T)
        p_in = spare(sq, 0, 2, PAD + T)
        p_2 = spare(sq, 2 * (PAD + T), 2, PAD + T)
        p_4 = spare(sq, 4 * (PAD + T), 2, PAD + T)
        p_8 = spare(sq, 6 * (PAD + T), 1, PAD + T)
        x_tok = spare(xc, 0, NT, D)
        at, rows = view(startup, 3, P)
        at, hot = view(at, BIAS_COLS + 2 * T - CMP_LEN, rows=REL_BUCKETS)
        at, table = view(at, N_HEADS, rows=REL_BUCKETS)
        at, bias_row = view(at, BIAS_COLS, rows=N_HEADS)

        at, bias = view(0, N_HEADS, T)
        at, n_qT = view(at, KC, T)
        at, k_sel = view(at, N_GROUPS, T)
        at, k_win = view(at, N_GROUPS, T)
        at, z_k = view(at, N_GROUPS, T + 1)
        at, z_v = view(at, N_GROUPS, T + 1)
        at, v_sel = view(at, NT, 256)
        at, v_win = view(at, NT, 256)
        at, n_acc = view(at, NT, 1024)
        at, n_score = view(at, 2, 384)
        at, n_prob = view(at, 2, 384)
        at, n_probT = view(at, 2, 384)
        at, n_nmax = view(at, 2, 2)
        at, n_gates = view(at, NT, 48)
        at, n_sums = view(at, 2 * N_HEADS, 2)
        at, n_rsum = view(at, 2 * N_HEADS, 2)
        at, n_coef = view(at, 3 * N_HEADS, 2)
        at, hidT = view(at, 2, N_GROUPS * N_CMP)
        at, hid_bias = view(at, 2)
        at, kcT = view(at, N_GROUPS * N_CMP)
        at, hid_heads = view(at, N_HEADS, N_CMP)
        at, c_max = view(at, NT, N_HEADS)
        at, c_sum = view(at, NT, N_HEADS)
        c_score = z_k.rearrange("p a b -> p (a b)")[:, 0:480].rearrange("p (a b) -> p a b", a=NT)
        c_probT = z_k.rearrange("p a b -> p (a b)")[:, 480:992].rearrange("p (a b) -> p a b", a=4)
        c_val = z_v.rearrange("p a b -> p (a b)")[:, 0:1024].rearrange("p (a b) -> p a b", a=2)
        n_tmp = spare(sq, 0, 2, 512)
        w1_k, w1_v = (spare(w, 0, 16, P) for w in (sq, xc))

        at, r_q = view(0, H_HEADS, T)
        at, r_k = view(at, H_HEADS, T)
        at, r_b = view(at, H_HEADS, T)
        at, r_v = view(at, NT, D)
        at, r_g = view(at, NT, D)
        at, r_at = view(at, 2 * H_HEADS, P)
        at, r_cross = view(at, H_HEADS, P)
        at, r_o = view(at, NT, D)
        at, r_ss = view(at, 16)
        at, r_rr = view(at, 16)
        at, lb = view(at, 4, H_HEADS)
        at, r_gain = view(at, P)

        gate_w2 = sb("gate_w2", [P, KC, 48])
        w2_k = sb("w2_k", [P, 2, DH])
        w2_v = sb("w2_v", [P, DH])

        raw_landed = [sem(f"raw_landed{n}") for n in range(RAW_SLOTS)]
        const_landed = sem("const_landed")
        x_landed = sem("x_landed")
        rows_landed = sem("rows_landed")
        small_landed = sem("small_landed")
        hi_ready = sem("hi_ready")
        lo_ready = sem("lo_ready")
        half_done = sem("half_done")
        x_turned = sem("x_turned")
        x_ready = sem("x_ready")
        x_scaled = sem("x_scaled")
        par_turned = sem("par_turned")
        par_ready = sem("par_ready")
        zeros_ready = sem("zeros_ready")
        sq_ready = sem("sq_ready")
        xs_ready = sem("xs_ready")
        sqs_ready = sem("sqs_ready")
        stats_done = sem("stats_done")
        mean_sq_ready = sem("mean_sq_ready")
        std_ready = sem("std_ready")
        xg_ready = sem("xg_ready")
        ahi_ready = sem("ahi_ready")
        var_ready = sem("var_ready")
        a_ready = sem("a_ready")
        evac_done = sem("evac_done")
        mix_turned = sem("mix_turned")
        mix_hi = sem("mix_hi")
        mix_lo = sem("mix_lo")
        conv0_ready = sem("conv0_ready")
        convg_ready = sem("convg_ready")
        silu_ready = sem("silu_ready")
        g_ready = sem("g_ready")
        ffn_chain = sem("ffn_chain")
        y_ready = sem("y_ready")
        out_turned = sem("out_turned")
        out_ready = sem("out_ready")
        stored = sem("stored")
        dve_chain = sem("dve_chain")
        act_chain = sem("act_chain")
        pool_chain = sem("pool_chain")
        counts = {"dve": 0, "act": 0, "pool": 0}

        def link(engine, semaphore, name, instruction):
            counts[name] += 1
            instruction.then_inc(semaphore, 1)
            engine.wait_ge(semaphore, counts[name])

        w_in, w_out = io["w_in"][0], io["w_out"][0]
        n_in, n_out = io["nsa_w_in_2"][0], io["nsa_w_out_2"][0]
        r_in, r_out = io["hgrn_w_in_2"][0], io["hgrn_w_out_2"][0]
        up0 = io["w_up"][0]
        A_COLS = [1288 + 256 * n for n in range(6)] + [256, 512, 768, 1024, 0]
        N_COLS = [256 * n for n in range(10)]
        H_COLS = [1024 + 256 * n for n in range(4)] + [256 * n for n in range(4)] + \
                 [2048 + 256 * n for n in range(8)]
        O_COLS = [256 * n for n in range(4)]

        def ffn_mats(i, which):
            return tuple(io[f"ffn{which}_w_{m}_2"][i] for m in ("gate", "up", "down"))

        plan = [
            ("lin", w_in, A_COLS),
            ("lin", w_out, O_COLS),
            ("ffn", (up0[:, 0:D_FF], up0[:, D_FF:2 * D_FF], io["w_down"][0])),
            ("ffn", ffn_mats(0, 1)),
            ("lin", n_in, N_COLS),
            ("lin", n_out, O_COLS),
            ("ffn", ffn_mats(0, 2)),
            ("ffn", ffn_mats(1, 1)),
            ("lin", r_in, H_COLS),
            ("lin", r_out, O_COLS),
            ("ffn", ffn_mats(1, 2)),
        ][:stop]
        slab0 = [0]
        for e in plan:
            slab0.append(slab0[-1] + (len(e[2]) if e[0] == "lin" else 3 * FFN_STEPS))
        half0 = [2 * s for s in slab0]
        FFN_STEP = [(0, 0), (1, 0), (0, 1), (1, 1), (2, 0), (2, 1)]
        LAST_OF = (3, 4, 6)

        def stage_of(half):
            return max(n for n in range(len(plan)) if half0[n] <= half)

        def raw_freed(slab):
            n = stage_of(2 * slab)
            if plan[n][0] == "lin":
                return 2 * slab + 2
            j, m = divmod(slab - slab0[n], 3)
            return half0[n] + 6 * j + LAST_OF[m]

        def raw_half(kind, slot, matrix, x):
            if kind == "lin" or matrix < 2:
                return raw[:, slot, :].rearrange("p (k n) -> p k n", k=KC)[:, :, x * P:(x + 1) * P]
            return raw[:, slot, x * D:(x + 1) * D]

        def split_half(w, h, kind, matrix):
            v = w[:, h % HALF_SLOTS, :]
            return v.rearrange("p (k n) -> p k n", k=KC) if kind == "lin" or matrix < 2 else v

        def half_place(h):
            n = stage_of(h)
            if plan[n][0] == "lin":
                return "lin", 0, h % 2, h // 2
            j, s = divmod(h - half0[n], 6)
            m, x = FFN_STEP[s]
            return "ffn", m, x, slab0[n] + 3 * j + m

        n_halves = half0[-1]

        def act_split(act, h):
            if h >= n_halves:
                return
            kind, m, x, slab = half_place(h)
            act.wait_ge(raw_landed[slab % RAW_SLOTS], 16 * (slab // RAW_SLOTS + 1))
            if h >= HALF_SLOTS:
                act.wait_ge(half_done, h - HALF_SLOTS + 1)
            act.activation(split_half(whi, h, kind, m), raw_half(kind, slab % RAW_SLOTS, m, x),
                           ACT.Copy).then_inc(hi_ready, 1)

        def dve_split(dve, h):
            if h >= n_halves:
                return
            kind, m, x, slab = half_place(h)
            dve.wait_ge(hi_ready, h + 1)
            dve.tensor_tensor(split_half(wlo, h, kind, m), raw_half(kind, slab % RAW_SLOTS, m, x),
                              split_half(whi, h, kind, m).bitcast(F32), ALU.subtract).then_inc(lo_ready, 1)

        def act_split_next(act, n, j, s):
            m, x = FFN_STEP[s]
            slab = slab0[n] + 3 + m
            h = half0[n] + 6 + s
            act.wait_ge(raw_landed[slab % RAW_SLOTS], j * 16 + 16 * (slab // RAW_SLOTS + 1))
            act.wait_ge(half_done, j * 6 + (h - HALF_SLOTS + 1))
            act.activation(split_half(whi, h, "ffn", m), raw_half("ffn", slab % RAW_SLOTS, m, x),
                           ACT.Copy).then_inc(hi_ready, 1)

        def dve_split_next(dve, n, j, s):
            m, x = FFN_STEP[s]
            slab = slab0[n] + 3 + m
            h = half0[n] + 6 + s
            dve.wait_ge(hi_ready, j * 6 + (h + 1))
            dve.tensor_tensor(split_half(wlo, h, "ffn", m), raw_half("ffn", slab % RAW_SLOTS, m, x),
                              split_half(whi, h, "ffn", m).bitcast(F32), ALU.subtract).then_inc(lo_ready, 1)

        def three_pass(pe, dst, wh, wl, ah, al, first, last):
            pe.matmul(dst, wh, ah, start=first, stop=False, skip_group_check=True)
            pe.matmul(dst, wh, al, start=False, stop=False, skip_group_check=True)
            return pe.matmul(dst, wl, ah, start=False, stop=last, skip_group_check=True)

        def pe_half_channels(pe, h, dst, waited=True, a0=None):
            if waited:
                pe.wait_ge(lo_ready, h + 1)
            wh, wl = (w[:, h % HALF_SLOTS, :].rearrange("p (k n) -> p k n", k=KC) for w in (whi, wlo))
            for k in range(KC):
                if a0 is not None:
                    pe.wait_ge(a_ready, a0 + k + 1)
                last = three_pass(pe, dst, wh[:, k, :], wl[:, k, :], ahi[:, k, :], alo[:, k, :], k == 0, k == KC - 1)
            last.then_inc(half_done, 1)

        def pe_slab_tokens(pe, h, tile, dst, a0=None):
            s = h % HALF_SLOTS
            wh, wl = (w[:, s:s + 2, :].rearrange("p s (k n) -> p s k n", k=KC) for w in (whi, wlo))
            out2 = dst.rearrange("p (s n) -> p s n", s=2)
            for k in range(KC):
                if a0 is not None:
                    pe.wait_ge(a_ready, a0 + k + 1)
                a_h, a_l = (a[:, k, tile * P:(tile + 1) * P] for a in (ahi, alo))
                pe.matmul(out2, a_h, wh[:, :, k, :], start=k == 0, stop=False, skip_group_check=True)
                pe.matmul(out2, a_l, wh[:, :, k, :], start=False, stop=False, skip_group_check=True)
                last = pe.matmul(out2, a_h, wl[:, :, k, :], start=False, stop=k == KC - 1, skip_group_check=True)
            return last

        def bank2(b):
            return ps[:, b, :].rearrange("p (a b) -> p a b", a=2)

        X_STAGES = [1, 2, 3, 5, 6, 7, 9, 10]
        n_pre = 1 + sum(s < len(plan) for s in X_STAGES)

        def x_count(p):
            return 4 + 8 * p

        PRE = [("rms", LN1, None, 4), ("rms", LN2, None, 4), ("none", None, None, 0),
               ("ln", LNG + 0, LNB + 0, 0), ("ln", LNG + 8, LNB + 8, 4), ("ln", LNG + 16, LNB + 16, 0),
               ("ln", LNG + 24, LNB + 24, 0), ("ln", LNG + 32, LNB + 32, 4), ("ln", LNG + 40, LNB + 40, 0)]

        def norm_index(p):
            return sum(PRE[n][0] != "none" for n in range(p))

        def x_pair(p, j):
            return j + 1 if p == 0 else x_count(p) - KC + 2 * j + 2

        def pe_stats(pe, p, j):
            kind, _, _, bank = PRE[p]
            ni = norm_index(p)
            if kind == "none":
                return
            if kind == "ln":
                pe.wait_ge(xs_ready, 4 * (ni - 2) + j + 1)
                pe.matmul(ps[:, bank, 0:T], const("mean"), xc[:, j, :], start=j == 0, stop=j == 3)
            pe.wait_ge(sqs_ready, 4 * ni + j + 1)
            last = pe.matmul(ps[:, bank + 1, 0:T], const("mean"), sq[:, 2 * j, :], start=j == 0, stop=j == 3)
            if j == 3:
                last.then_inc(stats_done, 1)

        def act_table(act, function):
            act.activation(table_use[:, :], const("one"), function)

        def act_squares(act, p, j):
            cs = slice(2 * j, 2 * j + 2)
            if j == 0 and PRE[p][0] != "none":
                act_table(act, ACT.Sqrt)
            act.wait_ge(x_ready, x_pair(p, j))
            if PRE[p][0] == "none":
                act.activation(ahi[:, cs, :], xT[:, cs, :], ACT.Copy).then_inc(ahi_ready, 2)
            else:
                act.activation(sq[:, cs, :], xT[:, cs, :], ACT.Square).then_inc(sq_ready, 1)

        def dve_sums(dve, p, j):
            kind = PRE[p][0]
            ni = norm_index(p)
            c = 2 * j
            dve.wait_ge(x_ready, x_pair(p, j))
            if kind == "none":
                dve.wait_ge(ahi_ready, KC * p + c + 2)
                dve.tensor_tensor(alo[:, c:c + 2, :], xT[:, c:c + 2, :], ahi[:, c:c + 2, :].bitcast(F32),
                                  ALU.subtract).then_inc(a_ready, 2)
                return
            if kind == "ln":
                dve.tensor_tensor(xc[:, j, :], xT[:, c, :], xT[:, c + 1, :], ALU.add).then_inc(xs_ready, 1)
            dve.wait_ge(sq_ready, 4 * ni + j + 1)
            dve.tensor_tensor(sq[:, c, :], sq[:, c, :], sq[:, c + 1, :], ALU.add).then_inc(sqs_ready, 1)

        def dve_norm(dve, p):
            kind, gain, shift, bank = PRE[p]
            ni = norm_index(p)
            if kind == "none":
                return
            dve.wait_ge(stats_done, ni + 1)
            mean, square = ps[:, bank, 0:T], ps[:, bank + 1, 0:T]
            if kind == "ln":
                dve.wait_ge(mean_sq_ready, ni - 1)
                link(dve, dve_chain, "dve", dve.scalar_tensor_tensor(var[:, :], var[:, :], -1.0, square, ALU.mult, ALU.add))
                dve.tensor_scalar(var[:, :], var[:, :], 0.0, LN_EPS, ALU.max, ALU.add).then_inc(var_ready, 1)
                for j in range(4):
                    cs = slice(2 * j, 2 * j + 2)
                    last = dve.tensor_tensor(xc[:, cs, :], xT[:, cs, :], bc(mean, 1, 2), ALU.subtract)
                link(dve, dve_chain, "dve", last)
            else:
                dve.tensor_scalar(var[:, :], square, RMS_EPS, None, ALU.add).then_inc(var_ready, 1)
            dve.wait_ge(std_ready, ni + 1)
            link(dve, dve_chain, "dve", dve.reciprocal(rstd[:, :], var[:, :]))

            def tail(k):
                dve.wait_ge(ahi_ready, KC * p + k + 1)
                hi = ahi[:, k, :].bitcast(F32)
                if kind == "ln":
                    ins = dve.scalar_tensor_tensor(alo[:, k, :], xc[:, k, :], par[:, shift + k:shift + k + 1], hi,
                                                   ALU.add, ALU.subtract)
                else:
                    ins = dve.tensor_tensor(alo[:, k, :], xc[:, k, :], hi, ALU.subtract)
                ins.then_inc(a_ready, 1)

            for k in range(KC):
                dve.scalar_tensor_tensor(xc[:, k, :], (xc if kind == "ln" else xT)[:, k, :],
                                         par[:, gain + k:gain + k + 1], rstd[:, :], ALU.mult, ALU.mult).then_inc(xg_ready, 1)
                if k >= 2 and p < 8:
                    tail(k - 2)
            if p < 8:
                tail(KC - 2)
                tail(KC - 1)

        def act_norm(act, p):
            kind, _, shift, bank = PRE[p]
            ni = norm_index(p)
            if kind == "none":
                return
            if kind == "ln":
                act.wait_ge(stats_done, ni + 1)
                act.activation(var[:, :], ps[:, bank, 0:T], ACT.Square).then_inc(mean_sq_ready, 1)
            act.wait_ge(var_ready, ni + 1)
            act.activation(var[:, :], var[:, :], ACT.Sqrt).then_inc(std_ready, 1)
            for k in range(KC):
                act.wait_ge(xg_ready, KC * ni + k + 1)
                dst = ahi if p < 8 else xT
                if kind == "ln":
                    ins = act.activation(dst[:, k, :], xc[:, k, :], ACT.Identity, bias=par[:, shift + k:shift + k + 1])
                else:
                    ins = act.activation(dst[:, k, :], xc[:, k, :], ACT.Copy)
                ins.then_inc(ahi_ready, 1)

        def pool_norm(pool, p):
            kind, _, shift, _ = PRE[p]
            ni = norm_index(p)
            if kind == "none":
                pool.wait_ge(a_ready, KC * (p + 1))
                pool.tensor_scalar(xT[:, :, :], xT[:, :, :], ALPHA, None, ALU.mult).then_inc(x_scaled, 1)
            if kind == "ln" and p < 8:
                for k in range(KC):
                    pool.wait_ge(xg_ready, KC * ni + k + 1)
                    last = pool.tensor_scalar(xT[:, k, :], xc[:, k, :], par[:, shift + k:shift + k + 1], ALPHA,
                                              ALU.add, ALU.mult)
                last.then_inc(x_scaled, 1)

        def mix_count(n):
            return 4 * ((1, 5, 9).index(n) + 1)

        def pe_project(pe, n, p):
            pe.wait_ge(mix_lo, mix_count(n))
            for s in range(8):
                if s >= 4:
                    pe.wait_ge(x_ready, x_count(p) + s - 3)
                pe_half_channels(pe, half0[n] + s, ps[:, s % 4, 0:T])
                if s in (3, 5, 7):
                    pe_stats(pe, p + 1, s // 2 - 1)
            pe_stats(pe, p + 1, 3)

        def act_project(act, n, p):
            for s in range(8):
                if s < 6:
                    act_split(act, half0[n] + s + HALF_SLOTS)
                if s % 2:
                    act_squares(act, p + 1, s // 2)

        def dve_project(dve, n, p, scaled):
            if scaled:
                dve.wait_ge(x_scaled, scaled)
            for s in range(8):
                dve.wait_ge(half_done, half0[n] + s + 1)
                dve.tensor_tensor(xT[:, s, :], xT[:, s, :], ps[:, s % 4, 0:T], ALU.add).then_inc(x_ready, 1)
                if s % 2:
                    dve_sums(dve, p + 1, s // 2)
                if s < 6:
                    dve_split(dve, half0[n] + s + HALF_SLOTS)

        def ffn_index(n):
            return (2, 3, 6, 7, 10).index(n)

        def pe_ffn(pe, n, p):
            f = ffn_index(n)
            if f == 0:
                pe.wait_ge(zeros_ready, 1)
            if PRE[p][0] != "none":
                pe.wait_ge(xg_ready, KC * norm_index(p) + 1)
            for b in range(4):
                if PRE[p][0] == "none":
                    pe.wait_ge(a_ready, KC * p + 2 * b + 2)
                pe.matmul(ps[:, 4 + b, :], zeros[:, 0:P], zeros[:, :], start=True, stop=False, skip_group_check=True)
            def down(h, x, c):
                cols = slice(c * P, (c + 1) * P)
                return three_pass(pe, ps[:, 4 + c // 2, (c % 2) * T:(c % 2 + 1) * T],
                                  whi[:, h % HALF_SLOTS, cols], wlo[:, h % HALF_SLOTS, cols],
                                  ghi[:, x, :], glo[:, x, :], False, False)

            with pe.Fori(0, FFN_STEPS - 1) as j:
                for s in range(6):
                    h = half0[n] + s
                    m, x = FFN_STEP[s]
                    pe.wait_ge(lo_ready, j * 6 + (h + 1))
                    if m < 2:
                        pe_half_channels(pe, h, ps[:, 2 * x + m, 0:T], waited=False, a0=KC * p if s == 0 else None)
                        continue
                    pe.wait_ge(g_ready, j * 2 + (2 * FFN_STEPS * f + x + 1))
                    for c in range(KC):
                        last = down(h, x, c)
                    last.then_inc(half_done, 1)
            h = half0[n + 1] - 6
            for s in range(4):
                m, x = FFN_STEP[s]
                pe_half_channels(pe, h + s, ps[:, 2 * x + m, 0:T])
            pe.wait_ge(lo_ready, h + 6)
            pe.wait_ge(g_ready, 2 * FFN_STEPS * (f + 1))
            for i in range(4):
                for c in (2 * i, 2 * i + 1):
                    for x in range(2):
                        last = down(h + 4 + x, x, c)
                if i < 3:
                    last.then_inc(y_ready, 1)
                else:
                    last.then_inc(half_done, 2)
                if i >= 1:
                    pe_stats(pe, p + 1, i - 1)
            pe_stats(pe, p + 1, 3)

        def act_ffn(act, n, p):
            f = ffn_index(n)

            def step(j, splits):
                for s in range(6):
                    m, x = FFN_STEP[s]
                    if m < 2 and n == 2:
                        act.wait_ge(half_done, j * 6 + (half0[n] + s + 1))
                        conv = (conv_g, conv_u)[m]
                        tap = par[:, bass.ds(j * 2 + (FCONV + 88 + 22 * m + x), 1)]
                        act.activation(conv[:, x, :], ps[:, 2 * x + m, 0:T], ACT.Copy,
                                       scale=tap).then_inc(conv0_ready, 1)
                        if m == 1:
                            act.wait_ge(convg_ready, j * 2 + (x + 1))
                            act.activation(gate_act[:, x, :], conv_g[:, x, :], ACT.Silu).then_inc(silu_ready, 1)
                    elif m == 0:
                        act.wait_ge(half_done, j * 6 + (half0[n] + s + 1))
                        act.activation(gate_act[:, x, :], ps[:, 2 * x, 0:T], ACT.Silu).then_inc(silu_ready, 1)
                    splits(j, s)

            act_table(act, ACT.Silu)
            with act.Fori(0, FFN_STEPS - 1) as j:
                step(j, lambda j, s: act_split_next(act, n, j, s))
            step(FFN_STEPS - 1, lambda j, s: act_split(act, half0[n + 1] + s) if s < 4 else None)
            for i in range(4):
                act_squares(act, p + 1, i)

        def dve_ffn(dve, n, p, scaled):
            f = ffn_index(n)
            links = 5 if n == 2 else 2

            def step(j, splits):
                done = 0

                def chain(ins):
                    nonlocal done
                    done += 1
                    before = 0 if f == 0 else 2 * FFN_STEPS * (5 + 2 * (f - 1))
                    ins.then_inc(ffn_chain, 1)
                    dve.wait_ge(ffn_chain, j * (2 * links) + (before + done))

                for s in range(6):
                    m, x = FFN_STEP[s]
                    if m < 2 and n == 2:
                        conv = (conv_g, conv_u)[m]
                        dve.wait_ge(conv0_ready, j * 4 + (2 * x + m + 1))
                        for back in (1, 2):
                            tap = par[:, bass.ds(j * 2 + (FCONV + 44 * (2 - back) + 22 * m + x), 1)]
                            ins = dve.scalar_tensor_tensor(conv[:, x, back:T], ps[:, 2 * x + m, 0:T - back], tap,
                                                           conv[:, x, back:T], ALU.mult, ALU.add)
                            if m == 0 and back == 2:
                                ins.then_inc(convg_ready, 1)
                            else:
                                chain(ins)
                    if m == 1:
                        dve.wait_ge(half_done, j * 6 + (half0[n] + s + 1))
                        dve.wait_ge(silu_ready, j * 2 + (2 * FFN_STEPS * f + x + 1))
                        up = conv_u[:, x, :] if n == 2 else ps[:, 2 * x + 1, 0:T]
                        chain(dve.tensor_tensor(gated[:, x, :], gate_act[:, x, :], up, ALU.mult))
                        chain(dve.tensor_copy(ghi[:, x, :], gated[:, x, :]))
                        dve.tensor_tensor(glo[:, x, :], gated[:, x, :], ghi[:, x, :].bitcast(F32),
                                          ALU.subtract).then_inc(g_ready, 1)
                    splits(j, s)

            with dve.Fori(0, FFN_STEPS - 1) as j:
                step(j, lambda j, s: dve_split_next(dve, n, j, s))
            step(FFN_STEPS - 1, lambda j, s: dve_split(dve, half0[n + 1] + s) if s < 4 else None)
            if scaled:
                dve.wait_ge(x_scaled, scaled)
            for i in range(4):
                if i < 3:
                    dve.wait_ge(y_ready, 3 * f + i + 1)
                else:
                    dve.wait_ge(half_done, half0[n + 1])
                cs = slice(2 * i, 2 * i + 2)
                dve.scalar_tensor_tensor(xT[:, cs, :], bank2(4 + i), 0.5 if scaled else 1.0, xT[:, cs, :],
                                         ALU.mult, ALU.add).then_inc(x_ready, 2)
                dve_sums(dve, p + 1, i)

        gates_done = sem("gates_done")
        gates_evac = sem("gates_evac")
        nsa_gates_done = sem("nsa_gates_done")
        rows_done = sem("rows_done")
        rows_evac = sem("rows_evac")
        rows_stored = sem("rows_stored")
        cmp_bias_done = sem("cmp_bias_done")
        cmp_bias_ready = sem("cmp_bias_ready")
        bias_landed = sem("bias_landed")
        bias_ready = sem("bias_ready")

        def pe_start(pe):
            pe.wait_ge(const_landed, 16)
            pe.wait_ge(x_landed, 16)
            for b in range(4):
                for c in range(2):
                    for a in range(NT):
                        last = pe.transpose(ps[:, b, c * T + a * P:c * T + (a + 1) * P],
                                            x_tok[:, a, (2 * b + c) * P:(2 * b + c + 1) * P], ident)
                last.then_inc(x_turned, 1)

        def pe_params(pe):
            pe.wait_ge(rows_landed, 16 * N_ROW_DMAS)
            for g in range(3):
                last = pe.transpose(ps[:, 6, g * P:g * P + n_rows[g]], rows[0:n_rows[g], g, :],
                                    ident[0:n_rows[g], 0:n_rows[g]])
            last.then_inc(par_turned, 1)

        def pe_bias_rows(pe):
            pe.wait_ge(small_landed, 16 * N_SMALL_DMAS)
            pe.matmul(ps[0:N_HEADS, 7, 0:BIAS_COLS], table, hot[:, 0:BIAS_COLS], start=True,
                      stop=True).then_inc(rows_done, 1)
            for a in range(NT):
                for n in range(N_CMP):
                    col = BIAS_COLS + P - a * P + CMP_STRIDE * n
                    last = pe.matmul(ps[:, 2 + a, n * N_HEADS:(n + 1) * N_HEADS], hot[:, col:col + P], table,
                                     start=True, stop=True)
                if a == 0:
                    pe.wait_ge(x_ready, 4)
            last.then_inc(cmp_bias_done, 1)

        def act_start(act):
            act.wait_ge(par_turned, 1)
            at = 0
            for g in range(3):
                last = act.activation(par[:, at:at + n_rows[g]], ps[:, 6, g * P:g * P + n_rows[g]], ACT.Copy)
                at += n_rows[g]
            link(act, act_chain, "act", last)
            act.activation(par[:, AQ:AQ + 1], par[:, AQ:AQ + 1], ACT.Copy, scale=QK_SCALE).then_inc(par_ready, 1)
            act.wait_ge(par_ready, 1)

        def act_bias_rows(act):
            act.wait_ge(rows_done, 1)
            act.activation(bias_row, ps[0:N_HEADS, 7, 0:BIAS_COLS], ACT.Copy).then_inc(rows_evac, 1)

        def dve_start(dve):
            dve.memset(zeros[:, :], 0.0).then_inc(zeros_ready, 1)
            for b in range(4):
                dve.wait_ge(x_turned, b + 1)
                dve.tensor_copy(xT[:, 2 * b:2 * b + 2, :], bank2(b)).then_inc(x_ready, 1)
                dve_sums(dve, 0, b)

        def dve_bias_rows(dve):
            dve.wait_ge(cmp_bias_done, 1)
            for a in range(NT):
                dve.tensor_tensor(cmp_bias[:, a, :].rearrange("p (h n) -> p h n", h=N_HEADS),
                                  ps[:, 2 + a, 0:N_CMP * N_HEADS].rearrange("p (n h) -> p h n", n=N_CMP),
                                  bc(const("cmp_add")[:, a * N_CMP:(a + 1) * N_CMP], 1, N_HEADS),
                                  ALU.add).then_inc(cmp_bias_ready, 1)

        scores_done = sem("scores_done")
        max_ready = sem("max_ready")
        exp_done = sem("exp_done")
        probT_done = sem("probT_done")
        probT_ready = sem("probT_ready")
        heads_done = sem("heads_done")

        def pe_attention(pe, u0, n, q, k, v, dst, buf):
            _, prob, probT, _, _ = buf

            def scores(i):
                u = u0 + i
                if u >= 2:
                    pe.wait_ge(max_ready, u - 1)
                b = u % 2
                pe.matmul(ps[:, b, 0:P], q(i, 0), k(i, 1), start=True, stop=True)
                pe.matmul(ps[:, b, P:3 * P], q(i, 1), k(i, 2), start=True, stop=True).then_inc(scores_done, 1)

            def turn(i):
                u = u0 + i
                pe.wait_ge(exp_done, u + 1)
                if u >= 2:
                    pe.wait_ge(probT_ready, u - 1)
                for m in range(3):
                    last = pe.transpose(ps[:, 2 + u % 2, m * P:(m + 1) * P], prob[:, u % 2, m * P:(m + 1) * P], ident)
                last.then_inc(probT_done, 1)

            def values(i):
                u = u0 + i
                pe.wait_ge(probT_ready, u + 1)
                t = probT[:, u % 2, :]
                pe.matmul(dst(i, 0), t[:, 0:P], v(i, 0), start=True, stop=True)
                pe.matmul(dst(i, 1), t[:, P:2 * P], v(i, 0), start=True, stop=False)
                pe.matmul(dst(i, 1), t[:, 2 * P:3 * P], v(i, 1), start=False, stop=True).then_inc(heads_done, 1)

            for i in range(n + 2):
                if i < n:
                    scores(i)
                if 1 <= i <= n:
                    turn(i - 1)
                if i >= 2:
                    values(i - 2)

        def dve_attention(dve, u0, n, add, buf):
            score, _, _, nmax, _ = buf
            for i in range(n):
                u = u0 + i
                s = score[:, u % 2, :]
                dve.wait_ge(scores_done, u + 1)
                if u >= 2:
                    dve.wait_ge(exp_done, u - 1)
                dve.tensor_tensor(s[:, P:3 * P], ps[:, u % 2, P:3 * P], add(i), ALU.add)
                link(dve, dve_chain, "dve", dve.tensor_tensor(s[:, 0:P], ps[:, u % 2, 0:P], add(i)[:, P:2 * P], ALU.add))
                dve.tensor_reduce(nmax[:, u % 2, 0:1], s[:, 0:P], AX, ALU.max, negate=True)
                dve.tensor_reduce(nmax[:, u % 2, 1:2], s[:, P:3 * P], AX, ALU.max, negate=True).then_inc(max_ready, 1)

        def act_attention(act, u0, n, buf):
            score, prob, probT, nmax, sums = buf

            def evacuate(i):
                u = u0 + i
                act.wait_ge(probT_done, u + 1)
                if u >= 2:
                    act.wait_ge(heads_done, u - 1)
                act.activation(probT[:, u % 2, :], ps[:, 2 + u % 2, 0:3 * P], ACT.Copy).then_inc(probT_ready, 1)

            for i in range(n):
                u = u0 + i
                act.wait_ge(max_ready, u + 1)
                if u >= 2:
                    act.wait_ge(probT_done, u - 1)
                act.activation(prob[:, u % 2, 0:P], score[:, u % 2, 0:P], ACT.Exp, bias=nmax[:, u % 2, 0:1],
                               accum_out=sums[:, i, 0:1])
                act.activation(prob[:, u % 2, P:3 * P], score[:, u % 2, P:3 * P], ACT.Exp, bias=nmax[:, u % 2, 1:2],
                               accum_out=sums[:, i, 1:2]).then_inc(exp_done, 1)
                if i >= 1:
                    evacuate(i - 1)
            evacuate(n - 1)

        EV_A, EV_N, EV_H = 0, 22, 42
        token_tile = sem("token_tile")
        TT_A, TT_N, TT_H = 0, 8, 10
        pads_ready = sem("pads_ready")
        ones_ready = sem("ones_ready")
        gates_turned = sem("gates_turned")
        fabs_ready = sem("fabs_ready")
        softplus_ready = sem("softplus_ready")
        mt_ready = sem("mt_ready")
        emt_ready = sem("emt_ready")
        ucols_turned = sem("ucols_turned")
        ucols_read = sem("ucols_read")
        mcum_spread = sem("mcum_spread")
        decay_arg = sem("decay_arg")
        decay_ready = sem("decay_ready")
        qk_sq = sem("qk_sq")
        qk_var = sem("qk_var")
        qk_std = sem("qk_std")
        qk_normed = sem("qk_normed")
        qk_turned = sem("qk_turned")
        qk_ready = sem("qk_ready")
        conv_ready = sem("conv_ready")
        mqk_ready = sem("mqk_ready")
        mqk_done = sem("mqk_done")
        mw_ready = sem("mw_ready")
        num_done = sem("num_done")
        hc_ready = sem("hc_ready")
        hsq_ready = sem("hsq_ready")
        hvar_ready = sem("hvar_ready")
        hstd_ready = sem("hstd_ready")
        hm_ready = sem("hm_ready")
        ao_ready = sem("ao_ready")
        pool_ready = sem("pool_ready")
        pool_done = sem("pool_done")
        po_ready = sem("po_ready")

        def pe_tile_tokens(pe, base, ev, o, a0=None):
            pe.wait_ge(lo_ready, base + o + 2)
            for a in range(NT):
                if o + a >= 4:
                    pe.wait_ge(evac_done, ev + o + a - 3)
                last = pe_slab_tokens(pe, base + o, a, ps[:, (o + a) % 4, 0:T], a0)
                if a == 0:
                    last.then_inc(token_tile, 1)
                else:
                    last.then_inc(half_done, 2)

        def pe_tile_channels(pe, base, ev, o, a0=None):
            if o >= 4:
                pe.wait_ge(evac_done, ev + o - 3)
            pe_half_channels(pe, base + o, ps[:, o % 4, 0:T], a0=a0)

        def pe_first(pe):
            pe.wait_ge(a_ready, KC)
            for a in range(NT):
                for k in range(KC):
                    last = pe.matmul(ps[:, 6, a * 8:(a + 1) * 8], xc[:, k, a * P:(a + 1) * P], gate_w[:, k, :],
                                     start=k == 0, stop=k == KC - 1)
            last.then_inc(gates_done, 1)
            for o in range(0, 22, 2):
                if o == 2:
                    pe.wait_ge(gates_evac, 1)
                    for m in range(2):
                        for a in range(NT):
                            last = pe.transpose(ps[0:M_HEADS, 7, m * T + a * P:m * T + (a + 1) * P],
                                                gates[:, a, 4 * m:4 * m + 4], ident)
                    last.then_inc(gates_turned, 1)
                if o == 8:
                    pe.wait_ge(mt_ready, 1)
                    pe.wait_ge(emt_ready, 1)
                    for m, row in enumerate((u_g, e_mt)):
                        for a in range(NT):
                            last = pe.transpose(ps[:, 6, 8 * m + 4 * a:8 * m + 4 * a + 4], row[:, a * P:(a + 1) * P],
                                                ident[0:M_HEADS, 0:M_HEADS])
                    last.then_inc(ucols_turned, 1)
                if o == 10:
                    pe.wait_ge(ucols_read, 1)
                    for h in range(M_HEADS):
                        last = pe.matmul(ps[:, 7 - h // 2, (h % 2) * T:(h % 2 + 1) * T],
                                         ident[0:M_HEADS, h:h + 1].to_broadcast([M_HEADS, P]), m_cum,
                                         start=True, stop=True)
                    last.then_inc(mcum_spread, 1)
                if o in (14, 16):
                    m = (o - 14) // 2
                    pe.wait_ge(qk_normed, 1)
                    if m:
                        pe.wait_ge(qk_ready, 1)
                    for c in range(4):
                        for a in range(NT):
                            last = pe.transpose(ps[:, 4 + c // 2, (c % 2) * T + a * P:(c % 2) * T + (a + 1) * P],
                                                z_qk[:, a, (4 * m + c) * P:(4 * m + c + 1) * P], ident)
                    last.then_inc(qk_turned, 1)
                if 12 <= o < 16 or o >= 20:
                    pe_tile_channels(pe, half0[0], EV_A, o)
                    pe_tile_channels(pe, half0[0], EV_A, o + 1)
                else:
                    pe_tile_tokens(pe, half0[0], EV_A, o)
            pe.wait_ge(qk_ready, 2)
            pe.wait_ge(evac_done, EV_A + 22)
            pe_attention(pe, 0, A_HEADS,
                         lambda i, t: qkT[64 * (i % 2):64 * (i % 2) + 64, i // 2, t * P:(t + 1) * P],
                         lambda i, n: qkT[64 * (i % 2):64 * (i % 2) + 64, 4 + i // 2, 0:n * P],
                         lambda i, t: a_v[:, t, i * DH:(i + 1) * DH],
                         lambda i, t: ps[:, 4 + t, i * DH:(i + 1) * DH],
                         (att_score, att_prob, att_probT, att_nmax, a_sums))
            pe.wait_ge(decay_arg, 1)
            pe.wait_ge(pool_ready, 1)
            for c in range(2):
                last = pe.matmul(ps[:, 7, c * T:(c + 1) * T], pool_w[:, c, :], p_d[:, c, :], start=True, stop=True)
            last.then_inc(pool_done, 1)
            pe.wait_ge(mqk_ready, 1)
            for h in range(M_HEADS):
                lo = 64 * (h % 2)
                q, k = conv_out[lo:lo + 64, h // 2, :], conv_out[lo:lo + 64, 2 + h // 2, :]
                pe.matmul(ps[:, h, 0:T], k[:, 0:P], q, start=True, stop=True)
                pe.matmul(ps[:, h, T:T + P], k[:, P:T], q[:, P:T], start=True, stop=True).then_inc(mqk_done, 1)
            pe.wait_ge(ao_ready, 2)
            pe.wait_ge(mw_ready, 2)
            for c in range(4):
                for a in range(NT):
                    last = pe.transpose(ps[:, c // 2, (c % 2) * T + a * P:(c % 2) * T + (a + 1) * P],
                                        a_out[:, a, c * P:(c + 1) * P], ident)
                if c % 2:
                    last.then_inc(mix_turned, 1)
            pe.wait_ge(ones_ready, 1)
            for h in range(M_HEADS):
                pe.wait_ge(mw_ready, h + 1)
                col = slice(h * (DH + 1), (h + 1) * (DH + 1))
                pe.matmul(ps[:, 4, col], decay[:, h, 0:P], m_v[:, 0, h, :], start=True, stop=True)
                pe.matmul(ps[:, 5, col], decay[:, h, P:T], m_v[:, 0, h, :], start=True, stop=False)
                last = pe.matmul(ps[:, 5, col], decay[:, h, T:T + P], m_v[:, 1, h, :], start=False, stop=True)
            last.then_inc(num_done, 1)
            pe.wait_ge(hm_ready, 1)
            for c in range(2):
                for a in range(NT):
                    last = pe.transpose(ps[:, 6, c * T + a * P:c * T + (a + 1) * P], h_out[:, a, c * P:(c + 1) * P], ident)
            last.then_inc(mix_turned, 1)

        def act_mix(act, count, src, cs, turned):
            act.wait_ge(mix_turned, turned)
            act.activation(ahi[:, cs:cs + 2, :], src, ACT.Copy).then_inc(mix_hi, 1)

        def dve_mix(dve, count, src, cs):
            dve.wait_ge(mix_hi, count)
            dve.tensor_tensor(alo[:, cs:cs + 2, :], src, ahi[:, cs:cs + 2, :].bitcast(F32), ALU.subtract).then_inc(mix_lo, 1)

        def act_first(act):
            for o in range(22):
                slab, x = o // 2, o % 2
                channels = slab in (6, 7, 10)
                src = ps[:, o % 4, 0:T]
                if channels or x == 1:
                    act.wait_ge(half_done, half0[0] + o + 1)
                else:
                    act.wait_ge(token_tile, TT_A + (slab if slab < 6 else slab - 2) + 1)
                if slab < 4:
                    act.activation(z_qk[:, x, 256 * slab:256 * slab + 256], src, ACT.Copy).then_inc(evac_done, 1)
                elif slab < 6:
                    act.activation(a_v[:, x, 256 * (slab - 4):256 * (slab - 3)], src, ACT.Copy).then_inc(evac_done, 1)
                elif slab < 8:
                    if o == 12:
                        act.wait_ge(pads_ready, 2)
                    act.activation(conv_in[:, o - 12, 3:3 + T], src, ACT.Copy).then_inc(evac_done, 1)
                elif slab == 8:
                    act.activation(m_v[:, x, :, 0:DH], src.rearrange("p (h d) -> p h d", h=M_HEADS),
                                   ACT.Copy).then_inc(evac_done, 1)
                elif slab == 9:
                    act.activation(m_o[:, x, :], src, ACT.Sigmoid).then_inc(evac_done, 1)
                else:
                    if x == 0:
                        act.wait_ge(qk_var, 1)
                    act.activation(p_in[:, x, PAD:PAD + T], src, ACT.Copy).then_inc(evac_done, 1)
                act_split(act, half0[0] + o + HALF_SLOTS)
                if o == 0:
                    act.wait_ge(gates_done, 1)
                    act.activation(gates[:, :, :], ps[:, 6, 0:16].rearrange("p (a b) -> p a b", a=NT),
                                   ACT.Copy).then_inc(gates_evac, 1)
                if o == 4:
                    act.wait_ge(fabs_ready, 1)
                    link(act, act_chain, "act", act.activation(f_abs, f_abs, ACT.Exp, scale=-1.0))
                    act.activation(f_abs, f_abs, ACT.Ln, bias=1.0).then_inc(softplus_ready, 1)
                if o == 5:
                    act.wait_ge(mt_ready, 1)
                    act.activation(e_mt, m_t, ACT.Exp, scale=-1.0).then_inc(emt_ready, 1)
                if o == 7:
                    act.wait_ge(evac_done, EV_A + 8)
                    act.activation(sq[:, :, :].rearrange("p a b -> p (a b)"), z_qk.rearrange("p a b -> p (a b)"),
                                   ACT.Square).then_inc(qk_sq, 1)
                if o == 9:
                    act.wait_ge(qk_var, 1)
                    act.activation(rr, ss, ACT.Sqrt).then_inc(qk_std, 1)
                if o in (15, 17):
                    m = (o - 15) // 2
                    act.wait_ge(qk_turned, m + 1)
                    act.activation(qkT[:, 4 * m:4 * m + 4, :], ps[:, 4:6, :].rearrange("p a (b c) -> p (a b) c", b=2),
                                   ACT.Copy, scale=par[:, AQ + m:AQ + m + 1]).then_inc(qk_ready, 1)
                if o == 19:
                    act.wait_ge(conv_ready, 1)
                    act.activation(conv_out, conv_out, ACT.Silu).then_inc(mqk_ready, 1)
            act.wait_ge(decay_arg, 1)
            act.activation(decay, decay, ACT.Exp, scale=-1.0).then_inc(decay_ready, 1)
            act_attention(act, 0, A_HEADS, (att_score, att_prob, att_probT, att_nmax, a_sums))
            act_mix(act, 1, bank2(0), 4, 1)
            act_mix(act, 2, bank2(1), 6, 2)
            act.wait_ge(pool_done, 1)
            for c in range(2):
                last = act.activation(p_d[:, c, :], ps[:, 7, c * T:(c + 1) * T], ACT.Copy,
                                      scale=par[:, PSCALE + c:PSCALE + c + 1])
            last.then_inc(po_ready, 1)
            act.wait_ge(po_ready, 1)
            act.activation(ahi[:, 0:2, :], p_d, ACT.Copy).then_inc(mix_hi, 1)
            act.wait_ge(hc_ready, 1)
            act.activation(h_sq, h_out, ACT.Square).then_inc(hsq_ready, 1)
            act.wait_ge(hvar_ready, 1)
            act.activation(m_rr, m_ss, ACT.Sqrt).then_inc(hstd_ready, 1)
            act_mix(act, 4, bank2(6), 2, 3)

        def dve_first(dve):
            def chain(ins):
                link(dve, dve_chain, "dve", ins)

            for o in range(22):
                dve_split(dve, half0[0] + o + HALF_SLOTS)
                if o == 2:
                    dve.wait_ge(gates_turned, 1)
                    dve.tensor_scalar(i_g, ps[0:M_HEADS, 7, 0:T], gate_bias[:, 0:1], None, ALU.add)
                    chain(dve.tensor_scalar(f_g, ps[0:M_HEADS, 7, T:2 * T], gate_bias[:, 1:2], None, ALU.add))
                    dve.scalar_tensor_tensor(f_abs, f_g, -1.0, f_g, ALU.mult, ALU.max).then_inc(fabs_ready, 1)
                if o == 4:
                    dve.wait_ge(softplus_ready, 1)
                    chain(dve.scalar_tensor_tensor(f_log, f_g, 0.0, f_abs, ALU.min, ALU.subtract))
                    chain(dve.tensor_tensor_scan(g_cum, const("ones", M_HEADS), f_log, 0.0, ALU.mult, ALU.add))
                    chain(dve.tensor_tensor(u_g, i_g, g_cum, ALU.subtract))
                    chain(dve.tensor_tensor_scan(m_cum, const("ones", M_HEADS), u_g, 0.0, ALU.mult, ALU.max))
                    dve.tensor_tensor(m_t, g_cum, m_cum, ALU.add).then_inc(mt_ready, 1)
                if o == 8:
                    dve.wait_ge(ucols_turned, 1)
                    dve.tensor_copy(ucols, ps[:, 6, 0:16]).then_inc(ucols_read, 1)
                    dve.wait_ge(qk_sq, 1)
                    chain(dve.tensor_reduce(ss, sq[:, :, :].rearrange("p a b -> p (a b)").rearrange("p (g d) -> p g d", d=DH),
                                            AX, ALU.add))
                    dve.tensor_scalar(ss, ss, 1.0 / DH, RMS_EPS, ALU.mult, ALU.add).then_inc(qk_var, 1)
                if o == 10:
                    dve.wait_ge(qk_std, 1)
                    chain(dve.reciprocal(rr, rr))
                    z = z_qk.rearrange("p a (g d) -> p (a g) d", d=DH)
                    dve.tensor_tensor(z, z, bc(rr, 2, DH), ALU.mult).then_inc(qk_normed, 1)
                if o == 11:
                    dve.wait_ge(mcum_spread, 1)
                    dve.wait_ge(ucols_read, 1)
                    for h in range(M_HEADS):
                        m = ps[:, 7 - h // 2, (h % 2) * T:(h % 2 + 1) * T]
                        dve.scalar_tensor_tensor(decay[:, h, 0:T], m, ucols[:, h:h + 1], const("late"),
                                                 ALU.subtract, ALU.max)
                        last = dve.scalar_tensor_tensor(decay[:, h, T:T + P], m[:, P:T], ucols[:, 4 + h:5 + h],
                                                        const("late")[:, 0:P], ALU.subtract, ALU.max)
                    last.then_inc(decay_arg, 1)
                if o == 16:
                    dve.wait_ge(pads_ready, 2)
                    dve.wait_ge(evac_done, EV_A + 16)
                    for j in range(4):
                        for c in range(4):
                            x = conv_in[:, c, j:j + T]
                            tap = par[:, MCONV + 4 * j + c:MCONV + 4 * j + c + 1]
                            if j == 0:
                                last = dve.tensor_scalar(conv_out[:, c, :], x, tap, None, ALU.mult)
                            else:
                                last = dve.scalar_tensor_tensor(conv_out[:, c, :], x, tap, conv_out[:, c, :],
                                                                ALU.mult, ALU.add)
                        if j < 3:
                            chain(last)
                    last.then_inc(conv_ready, 1)
            dve_attention(dve, 0, A_HEADS, lambda i: const("causal"),
                          (att_score, att_prob, att_probT, att_nmax, a_sums))
            dve.wait_ge(heads_done, A_HEADS)
            chain(dve.reciprocal(a_rsum, a_sums))
            for a in range(NT):
                dve.tensor_tensor(a_out[:, a, :].rearrange("p (h d) -> p h d", d=DH),
                                  ps[:, 4 + a, :].rearrange("p (h d) -> p h d", d=DH),
                                  bc(a_rsum[:, :, a], 2, DH), ALU.mult).then_inc(ao_ready, 1)
            dve.wait_ge(decay_ready, 1)
            for h in range(M_HEADS):
                dve.wait_ge(mqk_done, h + 1)
                dve.scalar_tensor_tensor(decay[:, h, :], ps[:, h, 0:384], QK_SCALE, decay[:, h, :],
                                         ALU.mult, ALU.mult).then_inc(mw_ready, 1)
            dve_mix(dve, 1, bank2(0), 4)
            dve_mix(dve, 2, bank2(1), 6)
            dve.wait_ge(num_done, 1)
            num = [ps[:, 4 + a, 0:M_HEADS * (DH + 1)].rearrange("p (h e) -> p h e", h=M_HEADS) for a in range(NT)]
            least = ucols[:, 8:16].rearrange("p (a h) -> p a h", a=NT)
            for a in range(NT):
                last = dve.scalar_tensor_tensor(den[:, a, :], num[a][:, :, DH], -1.0, least[:, a, :], ALU.mult, ALU.max)
            chain(last)
            for a in range(NT):
                last = dve.tensor_tensor(den[:, a, :], num[a][:, :, DH], den[:, a, :], ALU.max)
            chain(last)
            chain(dve.reciprocal(den, den))
            for a in range(NT):
                last = dve.tensor_tensor(h_out[:, a, :].rearrange("p (h d) -> p h d", d=DH), num[a][:, :, 0:DH],
                                         bc(den[:, a, :], 2, DH), ALU.mult)
            last.then_inc(hc_ready, 1)
            dve_mix(dve, 3, p_d, 0)
            dve.wait_ge(hsq_ready, 1)
            chain(dve.tensor_reduce(m_ss, h_sq.rearrange("p a (h d) -> p (a h) d", d=DH), AX, ALU.add))
            dve.tensor_scalar(m_ss, m_ss, 1.0 / DH, RMS_EPS, ALU.mult, ALU.add).then_inc(hvar_ready, 1)
            dve.wait_ge(hc_ready, 1)
            chain(dve.tensor_tensor(m_o, m_o, bc(mng, 1, NT), ALU.mult))
            chain(dve.tensor_tensor(h_out, h_out, m_o, ALU.mult))
            dve.wait_ge(hstd_ready, 1)
            chain(dve.reciprocal(m_rr, m_rr))
            hh = h_out.rearrange("p a (h d) -> p (a h) d", d=DH)
            dve.tensor_tensor(hh, hh, bc(m_rr, 2, DH), ALU.mult).then_inc(hm_ready, 1)
            dve_mix(dve, 4, bank2(6), 2)

        def pool_first(pool):
            def chain(ins):
                link(pool, pool_chain, "pool", ins)

            pool.wait_ge(gates_done, 1)
            pool.wait_ge(a_ready, KC)
            pool.memset(conv_in[:, :, 0:3], 0.0).then_inc(pads_ready, 1)
            pool.wait_ge(qk_var, 1)
            pool.memset(p_in[:, :, 0:PAD], 0.0).then_inc(pads_ready, 1)
            pool.wait_ge(pads_ready, 3)
            pool.wait_ge(evac_done, EV_A + 22)
            n = PAD + T
            chain(pool.tensor_tensor(p_2[:, :, 1:n], p_in[:, :, 1:n], p_in[:, :, 0:n - 1], ALU.add))
            chain(pool.tensor_tensor(p_4[:, :, 3:n], p_2[:, :, 3:n], p_2[:, :, 1:n - 2], ALU.add))
            chain(pool.tensor_tensor(p_8[:, 0, 7:n], p_4[:, 1, 7:n], p_4[:, 1, 3:n - 4], ALU.add))
            p_16 = p_2[64:128, 0, :]
            chain(pool.tensor_tensor(p_16[:, 15:n], p_8[64:128, 0, 15:n], p_8[64:128, 0, 7:n - 8], ALU.add))
            inv = const("inv_count").rearrange("p (a b) -> p a b", a=2)
            pool.tensor_tensor(p_d[0:64, 0, :], p_2[0:64, 0, PAD:n], inv[0:64, 0, :], ALU.mult)
            pool.tensor_tensor(p_d[64:128, 0, :], p_4[64:128, 0, PAD:n], inv[64:128, 0, :], ALU.mult)
            pool.tensor_tensor(p_d[0:64, 1, :], p_8[0:64, 0, PAD:n], inv[0:64, 1, :], ALU.mult)
            chain(pool.tensor_tensor(p_d[64:128, 1, :], p_16[:, PAD:n], inv[64:128, 1, :], ALU.mult))
            pool.tensor_tensor(p_d, p_d, p_in[:, :, PAD:n], ALU.subtract).then_inc(pool_ready, 1)

        def pe_finish(pe, normed):
            if normed:
                pe.wait_ge(ahi_ready, KC * 9)
            else:
                pe.wait_ge(x_ready, x_count(n_pre - 1))
            for a in range(NT):
                for b in range(2):
                    for c in range(4):
                        last = pe.transpose(ps[:, 2 * a + b if not normed else 2 + 2 * a + b, c * P:(c + 1) * P],
                                            xT[:, 4 * b + c, a * P:(a + 1) * P], ident)
                last.then_inc(out_turned, 1)

        def dve_finish(dve):
            b0 = 2 if len(plan) == 11 else 0
            for a in range(NT):
                dve.wait_ge(out_turned, a + 1)
                dve.tensor_copy(x_tok[:, a, :].rearrange("p (b c) -> p b c", b=2),
                                ps[:, b0 + 2 * a:b0 + 2 * a + 2, :]).then_inc(out_ready, 1)

        dup_landed = [sem(f"dup_landed{m}") for m in range(4)]
        w1_landed = sem("w1_landed")
        n_gates_raw = sem("n_gates_raw")
        n_gates_turned = sem("n_gates_turned")
        n_gates_ready = sem("n_gates_ready")
        hid_done = sem("hid_done")
        hid_bias_ready = sem("hid_bias_ready")
        hid_ready = sem("hid_ready")
        hid_spread = sem("hid_spread")
        kc_done = sem("kc_done")
        kc_ready = sem("kc_ready")
        vc_done = sem("vc_done")
        vc_ready = sem("vc_ready")
        c_scores_done = sem("c_scores_done")
        c_arg_ready = sem("c_arg_ready")
        c_exp_ready = sem("c_exp_ready")
        c_prob_ready = sem("c_prob_ready")
        c_turned = sem("c_turned")
        c_probT_ready = sem("c_probT_ready")
        c_done = sem("c_done")
        coef_ready = sem("coef_ready")
        part_ready = sem("part_ready")
        acc_ready = sem("acc_ready")
        n_bufs = [(n_score, n_prob, n_probT, n_nmax, n_sums[:, b * N_HEADS:(b + 1) * N_HEADS, :]) for b in range(2)]

        def pool_load_nsa(pool):
            pool.wait_ge(x_ready, x_count(1))
            pool.wait_ge(rows_stored, 16)
            shifted = bass.AP(tensor=scratch.tensor, offset=scratch.offset, ap=[[1, P], [BIAS_COLS, N_HEADS], [1, T]])
            pool.dma_start(bias, shifted).then_inc(bias_landed, 16)

        def pool_nsa(pool):
            pool_norm(pool, 3)
            pool.wait_ge(bias_landed, 16)
            pool.tensor_tensor(bias[:, :, P:T], bias[:, :, P:T], bc(const("causal_rev"), 1, N_HEADS),
                               ALU.add).then_inc(bias_ready, 1)
            pool.wait_ge(a_ready, KC * 4)
            pool.wait_ge(x_scaled, 2)
            for z, dst in enumerate((w1_k, w1_v)):
                pool.dma_start(dst, io["nsa_cmp_w1_2"][0, z].rearrange("l d e -> (l d) e").rearrange("(m p) e -> p m e", p=P)) \
                    .then_inc(w1_landed, 16)
            for m, (dst, slab) in enumerate(((z_k, 4), (z_v, 5), (k_sel, 6), (k_win, 8))):
                pool.wait_ge(evac_done, EV_N + 2 * slab + 2)
                off = 1 if m < 2 else 0
                for g in range(N_GROUPS):
                    lo, hi = dst[0:64, g, off:off + T], dst[64:128, g, 0:T]
                    pool.dma_start(hi if g % 2 == 0 else lo, lo if g % 2 == 0 else hi).then_inc(dup_landed[m], 16)
            for part in range(8):
                pool.wait_ge(part_ready, part + 1)
                a, half = part // 2 % 2, part % 2
                cols = n_acc[:, a, half * 512:(half + 1) * 512]
                pool.tensor_tensor(cols, cols, n_tmp[:, part % 2, :], ALU.add).then_inc(acc_ready, 1)

        def n_bank(a, half):
            return ps[:, 4 + 2 * a + half, :]

        def pe_nsa(pe):
            for o in range(0, 20, 2):
                if o == 4:
                    pe.wait_ge(x_scaled, 2)
                    for a in range(NT):
                        for k in range(KC):
                            last = pe.matmul(ps[:, 4, a * 48:(a + 1) * 48], xT[:, k, a * P:(a + 1) * P],
                                             gate_w2[:, k, :], start=k == 0, stop=k == KC - 1)
                    last.then_inc(nsa_gates_done, 1)
                if o == 6:
                    pe.wait_ge(n_gates_raw, 1)
                    pe.matmul(ps[:, 5, 0:96], const("flip"), n_gates.rearrange("p a b -> p (a b)"), start=True,
                              stop=True).then_inc(n_gates_turned, 1)
                if o == 16:
                    pe.wait_ge(w1_landed, 32)
                    for z, (src, w1) in enumerate(((z_k, w1_k), (z_v, w1_v))):
                        pe.wait_ge(dup_landed[z], 64)
                        for m in range(CMP_LEN // 2):
                            blocks = src[:, :, 1 + 2 * m:2 + 2 * m + CMP_STRIDE * (N_CMP - 1):CMP_STRIDE]
                            pe.matmul(ps[:, 5, z * 64:z * 64 + 60].rearrange("p (g n) -> p g n", g=N_GROUPS),
                                      w1[:, m, :], blocks, start=m == 0, stop=m == CMP_LEN // 2 - 1)
                        for m in range(CMP_LEN // 2):
                            last = pe.matmul(ps[:, 6, z:z + 1], w1[:, m, :],
                                             par[:, CPOS + 16 * z + m:CPOS + 16 * z + m + 1],
                                             start=m == 0, stop=m == CMP_LEN // 2 - 1)
                        last.then_inc(hid_done, 1)
                if o == 18:
                    pe.wait_ge(hid_ready, 2)
                    pe.matmul(ps[:, 7, 0:60], w2_k[:, :, :].rearrange("p a b -> p (a b)"), hidT[:, 0, :],
                              start=True, stop=True).then_inc(kc_done, 1)
                    pe.wait_ge(hid_spread, 1)
                    for half in range(2):
                        last = pe.matmul(ps[0:8 * N_CMP, 4, half * DH:(half + 1) * DH],
                                         hid_heads[:, half * 8:half * 8 + 8, :].rearrange("p a b -> p (a b)"),
                                         w2_v[:, :], start=True, stop=True)
                    last.then_inc(vc_done, 1)
                if o in (14, 18):
                    pe_tile_tokens(pe, half0[4], EV_N, o)
                else:
                    pe_tile_channels(pe, half0[4], EV_N, o, KC * 3 if o == 0 else None)
                    pe_tile_channels(pe, half0[4], EV_N, o + 1)
            def q(i, t):
                return n_qT[64 * (i % 2):64 * (i % 2) + 64, i // 2, t * P:(t + 1) * P]

            pe.wait_ge(evac_done, EV_N + 20)
            pe.wait_ge(kc_ready, 1)
            pe.wait_ge(hid_bias_ready, 2)
            pe.wait_ge(vc_ready, 1)
            for i in range(N_HEADS):
                lo, g = 64 * (i % 2), i // 4
                for a in range(NT):
                    last = pe.matmul(ps[:, 4 + 2 * (i % 2) + a, (i // 2) * N_CMP:(i // 2 + 1) * N_CMP], q(i, a),
                                     kcT[lo:lo + 64, g * N_CMP:(g + 1) * N_CMP], start=True, stop=True)
            last.then_inc(c_scores_done, 1)
            pe.wait_ge(c_prob_ready, 1)
            for a in range(NT):
                for half in range(2):
                    last = pe.transpose(ps[0:8 * N_CMP, 0, (2 * a + half) * P:(2 * a + half + 1) * P],
                                        c_score[:, a, half * 120:(half + 1) * 120], ident)
            last.then_inc(c_turned, 1)
            pe.wait_ge(c_probT_ready, 1)
            for a in range(NT):
                for half in range(2):
                    pe.matmul(n_bank(a, half), c_probT[0:8 * N_CMP, 2 * a + half, :], c_val[0:8 * N_CMP, half, :],
                              start=True, stop=True).then_inc(c_done, 1)
            for b, (k, v) in enumerate(((k_sel, v_sel), (k_win, v_win))):
                pe.wait_ge(dup_landed[2 + b], 64)
                if b == 0:
                    pe.wait_ge(coef_ready, 4)
                else:
                    pe.wait_ge(part_ready, 4)
                pe_attention(pe, A_HEADS + b * N_HEADS, N_HEADS, q,
                             lambda i, n: k[64 * (i % 2):64 * (i % 2) + 64, i // 4, 0:n * P],
                             lambda i, t: v[:, t, (i // 4) * DH:(i // 4 + 1) * DH],
                             lambda i, t: n_bank(t, i // 8)[:, (i % 8) * DH:(i % 8 + 1) * DH], n_bufs[b])
            pe_turn_mix(pe, n_acc, acc_ready, 8, 3, "flip")

        def pe_turn_mix(pe, src, ready, count, before, how):
            pe.wait_ge(ready, count)
            for c in range(KC):
                for a in range(NT):
                    dst = ps[:, c // 2, (c % 2) * T + a * P:(c % 2) * T + (a + 1) * P]
                    if how == "flip":
                        last = pe.matmul(dst, src[:, a, c * P:(c + 1) * P], const("flip"), start=True, stop=True)
                    else:
                        last = pe.transpose(dst, src[:, a, c * P:(c + 1) * P], ident)
                if c % 2:
                    last.then_inc(mix_turned, 1)

        def act_mix_all(act, before):
            for b in range(4):
                act_mix(act, 0, bank2(b), 2 * b, before + b + 1)

        def dve_mix_all(dve, before):
            for b in range(4):
                dve_mix(dve, before + b + 1, bank2(b), 2 * b)

        def act_nsa(act):
            for o in range(20):
                slab, x = o // 2, o % 2
                src = ps[:, o % 4, 0:T]
                if slab in (7, 9) and x == 0:
                    act.wait_ge(token_tile, TT_N + (slab - 5) // 2)
                else:
                    act.wait_ge(half_done, half0[4] + o + 1)
                if slab < 4:
                    for a in range(NT):
                        last = act.activation(n_qT[:, o, a * P:(a + 1) * P][:, ::-1], src[:, a * P:(a + 1) * P],
                                              ACT.Copy, scale=QK_SCALE)
                    last.then_inc(evac_done, 1)
                elif slab in (7, 9):
                    act.activation((v_sel if slab == 7 else v_win)[:, x, :], src, ACT.Copy).then_inc(evac_done, 1)
                else:
                    dst, off = {4: (z_k, 1), 5: (z_v, 1), 6: (k_sel, 0), 8: (k_win, 0)}[slab]
                    act.activation(dst[0:64, 2 * x, off:off + T], src[0:64, :], ACT.Copy)
                    act.activation(dst[64:128, 2 * x + 1, 0:T], src[64:128, :], ACT.Copy).then_inc(evac_done, 1)
                act_split(act, half0[4] + o + HALF_SLOTS)
                if o == 4:
                    act.wait_ge(nsa_gates_done, 1)
                    act.activation(n_gates, ps[:, 4, 0:96].rearrange("p (a b) -> p a b", a=NT), ACT.Copy,
                                   scale=1.0 / ALPHA).then_inc(n_gates_raw, 1)
                if o == 6:
                    act.wait_ge(n_gates_turned, 1)
                    act.activation(n_gates, ps[:, 5, 0:96].rearrange("p (a b) -> p a b", a=NT),
                                   ACT.Sigmoid).then_inc(n_gates_ready, 1)
                if o == 16:
                    for z in range(2):
                        act.wait_ge(hid_done, z + 1)
                        act.activation(hid_bias[:, z:z + 1], ps[:, 6, z:z + 1], ACT.Copy).then_inc(hid_bias_ready, 1)
                    act.wait_ge(hid_bias_ready, 2)
                    for z in range(2):
                        act.activation(hidT[:, z, :], ps[:, 5, z * 64:z * 64 + 60], ACT.Gelu_apprx_tanh,
                                       bias=hid_bias[:, z:z + 1]).then_inc(hid_ready, 1)
                if o == 18:
                    act.wait_ge(kc_done, 1)
                    act.activation(kcT, ps[:, 7, 0:60], ACT.Copy).then_inc(kc_ready, 1)
            act.wait_ge(c_arg_ready, 1)
            act.activation(c_score, c_score, ACT.Exp).then_inc(c_exp_ready, 1)
            act.wait_ge(c_turned, 1)
            act.activation(c_probT[0:8 * N_CMP, :, :], ps[0:8 * N_CMP, 0, :].rearrange("p (a b) -> p a b", a=4),
                           ACT.Copy).then_inc(c_probT_ready, 1)
            for b in range(2):
                act_attention(act, A_HEADS + b * N_HEADS, N_HEADS, n_bufs[b])
            act_mix_all(act, 3)

        def dve_gated(dve, a, half, branch, dst):
            co = n_coef[:, branch * N_HEADS + 8 * half:branch * N_HEADS + 8 * half + 8, a]
            return dve.tensor_tensor(dst.rearrange("p (h d) -> p h d", d=DH),
                                     n_bank(a, half).rearrange("p (h d) -> p h d", d=DH), bc(co, 2, DH), ALU.mult)

        def dve_nsa(dve):
            def chain(ins):
                link(dve, dve_chain, "dve", ins)

            for o in range(20):
                dve_split(dve, half0[4] + o + HALF_SLOTS)
                if o == 17:
                    dve.wait_ge(hid_ready, 2)
                    dve.tensor_copy(hid_heads.rearrange("p (g q) n -> p g q n", g=N_GROUPS),
                                    bc(hidT[:, 1, :].rearrange("p (g n) -> p g n", g=N_GROUPS), 2, 4)).then_inc(hid_spread, 1)
                if o == 18:
                    dve.wait_ge(vc_done, 1)
                    for half in range(2):
                        last = dve.tensor_tensor(c_val[0:120, half, :].rearrange("p (h d) -> p h d", d=DH),
                                                 bc(ps[0:120, 4, half * DH:(half + 1) * DH], 1, 8),
                                                 bc(const("own_head", 120), 2, DH), ALU.mult)
                    last.then_inc(vc_ready, 1)
            dve.wait_ge(hid_done, 2)
            dve.wait_ge(cmp_bias_ready, 2)
            dve.wait_ge(c_scores_done, 1)
            for odd in range(2):
                score, add = (x.rearrange("p a (h b n) -> p a h b n", b=2, n=N_CMP)[:, :, :, odd, :]
                              for x in (c_score, cmp_bias[:, :, :]))
                src = ps[:, 4 + 2 * odd:6 + 2 * odd, 0:120].rearrange("p a (h n) -> p a h n", n=N_CMP)
                last = dve.tensor_tensor(score, src, add, ALU.add)
            chain(last)
            by_head = c_score.rearrange("p a (h n) -> p (a h) n", n=N_CMP)
            c_m, c_s = (x.rearrange("p a h -> p (a h)") for x in (c_max, c_sum))
            chain(dve.tensor_reduce(c_m, by_head, AX, ALU.max))
            dve.tensor_tensor(by_head, by_head, bc(c_m, 2, N_CMP), ALU.subtract).then_inc(c_arg_ready, 1)
            dve.wait_ge(c_exp_ready, 1)
            chain(dve.tensor_reduce(c_s, by_head, AX, ALU.add))
            for a in range(NT):
                last = dve.tensor_tensor(c_score[:, a, :].rearrange("p (h n) -> p h n", n=N_CMP),
                                         c_score[:, a, :].rearrange("p (h n) -> p h n", n=N_CMP),
                                         bc(const("cmp_valid")[:, a * N_CMP:(a + 1) * N_CMP], 1, N_HEADS), ALU.mult)
            last.then_inc(c_prob_ready, 1)
            chain(dve.reciprocal(c_s, c_s))
            dve.wait_ge(n_gates_ready, 1)
            chain(dve.tensor_tensor(n_coef[:, 0:N_HEADS, :].rearrange("p h a -> p a h"), c_sum,
                                    n_gates.rearrange("p a (h b) -> p a h b", b=3)[:, :, :, 0], ALU.mult))
            dve.wait_ge(c_prob_ready, 1)
            for a in range(NT):
                for half in range(2):
                    dve.wait_ge(c_done, 2 * a + half + 1)
                    dve_gated(dve, a, half, 0, n_acc[:, a, half * 512:(half + 1) * 512]).then_inc(coef_ready, 1)
            dve.wait_ge(bias_ready, 1)
            for b in range(2):
                dve_attention(dve, A_HEADS + b * N_HEADS, N_HEADS, lambda i: bias[:, i, :], n_bufs[b])
                dve.wait_ge(heads_done, A_HEADS + (b + 1) * N_HEADS)
                hs = slice(b * N_HEADS, (b + 1) * N_HEADS)
                chain(dve.reciprocal(n_rsum[:, hs, :], n_sums[:, hs, :]))
                chain(dve.tensor_tensor(n_coef[:, (b + 1) * N_HEADS:(b + 2) * N_HEADS, :].rearrange("p h a -> p a h"),
                                        n_rsum[:, hs, :].rearrange("p h a -> p a h"),
                                        n_gates.rearrange("p a (h b) -> p a h b", b=3)[:, :, :, b + 1], ALU.mult))
                for a in range(NT):
                    for half in range(2):
                        part = 4 * b + 2 * a + half
                        if part >= 2:
                            dve.wait_ge(acc_ready, part - 1)
                        dve_gated(dve, a, half, b + 1, n_tmp[:, part % 2, :]).then_inc(part_ready, 1)
            dve_mix_all(dve, 4)


        N_LEVELS = len(LEVELS)
        r_gain_landed = sem("r_gain_landed")
        lb_arg = sem("lb_arg")
        lb_exp = sem("lb_exp")
        f_ready = sem("f_ready")
        logf_ready = sem("logf_ready")
        k_ready = sem("k_ready")
        level_arg = sem("level_arg")
        level_exp = sem("level_exp")
        level_ready = sem("level_ready")
        level_scored = sem("level_scored")
        level_placed = sem("level_placed")
        diag_done = sem("diag_done")
        diag_ready = sem("diag_ready")
        cross_ready = sem("cross_ready")
        r_out_done = sem("r_out_done")
        r_sq_ready = sem("r_sq_ready")
        r_var_ready = sem("r_var_ready")
        r_std_ready = sem("r_std_ready")
        r_silu_ready = sem("r_silu_ready")
        r_gate_ready = sem("r_gate_ready")
        r_o_ready = sem("r_o_ready")
        level_buf = (xc, sq)

        def halves(v, m):
            return v.rearrange("p a b -> p (a b)").rearrange("p (n b m) -> p n b m", b=2, m=m)

        def tiles(v):
            return v.rearrange("p a b -> p (a b)").rearrange("p (i n) -> p i n", n=P)

        def level_bank(u):
            b = 4 + 2 * (u % 2)
            return ps[:, b:b + 2, :]

        def pool_hgrn(pool):
            pool.wait_ge(x_ready, x_count(4))
            pool.dma_start(r_gain, spread(io["hgrn_norm_gain_2"][0], P)).then_inc(r_gain_landed, 16)
            pool_norm(pool, 6)
            pool.wait_ge(evac_done, EV_H + 16)
            pool.wait_ge(k_ready, 1)
            for u in range(N_LEVELS + 1):
                pool.wait_ge(level_exp, u + 1)
                m = LEVELS[u] if u < N_LEVELS else P
                y, k, q = (halves(v, m) for v in (level_buf[u % 2][:, :, :], r_k, r_q))
                pool.tensor_tensor(y[:, :, 0, :], y[:, :, 0, :], k[:, :, 0, :], ALU.mult)
                pool.tensor_tensor(y[:, :, 1, :], y[:, :, 1, :], q[:, :, 1, :], ALU.mult).then_inc(level_ready, 1)
            pool.wait_ge(r_silu_ready, 1)
            pool.wait_ge(r_gain_landed, 16)
            g = r_g.rearrange("p a (h d) -> p (a h) d", d=P)
            pool.tensor_tensor(g, g, bc(r_gain, 1, NT * H_HEADS), ALU.mult).then_inc(r_gate_ready, 1)

        def pe_hgrn(pe):

            def level(u):
                pe.wait_ge(level_ready, u + 1)
                if u < 2:
                    pe.wait_ge(diag_ready, 1)
                else:
                    pe.wait_ge(level_placed, u - 1)
                y = tiles(level_buf[u % 2][:, :, :])
                for i in range(2 * H_HEADS):
                    odd = y[:, i, :].rearrange("p (n b m) -> p n b m", b=2, m=LEVELS[u])[:, :, 1, :]
                    dst = level_bank(u)[:, i // 8, (i % 8) * 64:(i % 8 + 1) * 64]
                    last = pe.matmul(dst.rearrange("p (n m) -> p n m", m=LEVELS[u]), y[:, i, :], odd, start=True, stop=True)
                last.then_inc(level_scored, 1)

            for o in range(0, 32, 2):
                if o == 16:
                    pe.wait_ge(evac_done, EV_H + 16)
                    pe.wait_ge(k_ready, 1)
                    for i in range(2 * H_HEADS):
                        last = pe.matmul(ps[:, 4 + i // 4, (i % 4) * P:(i % 4 + 1) * P], tiles(r_k)[:, i, :],
                                         tiles(r_q)[:, i, :], start=True, stop=True)
                    last.then_inc(diag_done, 1)
                if o >= 18:
                    level((o - 18) // 2)
                if o < 16:
                    pe_tile_channels(pe, half0[8], EV_H, o, KC * 6 if o == 0 else None)
                    pe_tile_channels(pe, half0[8], EV_H, o + 1)
                else:
                    pe_tile_tokens(pe, half0[8], EV_H, o)
            pe.wait_ge(level_ready, N_LEVELS + 1)
            pe.wait_ge(level_placed, N_LEVELS - 1)
            y = level_buf[N_LEVELS % 2]
            for h in range(H_HEADS):
                last = pe.matmul(level_bank(N_LEVELS)[:, h // 4, (h % 4) * P:(h % 4 + 1) * P], y[:, h, 0:P], y[:, h, P:T],
                                 start=True, stop=True)
            last.then_inc(level_scored, 1)
            pe.wait_ge(level_placed, N_LEVELS)
            pe.wait_ge(evac_done, EV_H + 24)
            pe.wait_ge(cross_ready, 1)
            for a in range(NT):
                for h in range(H_HEADS):
                    dst = ps[:, 4 + 2 * a + h // 4, (h % 4) * P:(h % 4 + 1) * P]
                    cols = slice(h * P, (h + 1) * P)
                    if a == 1:
                        pe.matmul(dst, r_cross[:, h, :], r_v[:, 0, cols], start=True, stop=False)
                    last = pe.matmul(dst, r_at[:, 2 * h + a, :], r_v[:, a, cols], start=a == 0, stop=True)
                last.then_inc(r_out_done, 1)
            pe.wait_ge(evac_done, EV_H + 32)
            pe_turn_mix(pe, r_o, r_o_ready, NT, 7, "transpose")

        def act_hgrn(act):
            act.wait_ge(lb_arg, 1)
            act.activation(lb[:, 0:2, :], lb[:, 0:2, :], ACT.Exp).then_inc(lb_exp, 1)

            def exps(u):
                act.wait_ge(level_arg, u + 1)
                buf = level_buf[u % 2][:, :, :]
                act.activation(buf, buf, ACT.Exp).then_inc(level_exp, 1)

            for o in range(32):
                slab, x = o // 2, o % 2
                src = ps[:, o % 4, 0:T]
                if slab >= 8 and x == 0:
                    act.wait_ge(token_tile, TT_H + slab - 7)
                else:
                    act.wait_ge(half_done, half0[8] + o + 1)
                if slab < 4:
                    act.activation(r_k[:, o, :], src, ACT.Sigmoid, scale=-1.0)
                    act.activation(r_b[:, o, :], src, ACT.Sigmoid).then_inc(evac_done, 1)
                elif slab < 8:
                    act.activation(r_q[:, o - 8, :], src, ACT.Silu).then_inc(evac_done, 1)
                else:
                    act.activation((r_v if slab < 12 else r_g)[:, x, 256 * (slab % 4):256 * (slab % 4 + 1)], src,
                                   ACT.Copy).then_inc(evac_done, 1)
                act_split(act, half0[8] + o + HALF_SLOTS)
                if o == 7:
                    act.wait_ge(f_ready, 1)
                    for h in range(H_HEADS):
                        act.activation(r_b[:, h, :], r_b[:, h, :], ACT.Ln, scale=lb[:, 3, h:h + 1],
                                       bias=lb[:, 2, h:h + 1]).then_inc(logf_ready, 1)
                if o in (13, 15):
                    exps((o - 13) // 2)
                if 18 <= o < 30 and o % 2 == 0:
                    exps((o - 18) // 2 + 2)
            act.wait_ge(level_scored, N_LEVELS + 1)
            act.activation(r_cross.rearrange("p (b h) n -> p b (h n)", b=2), level_bank(N_LEVELS), ACT.Copy).then_inc(cross_ready, 1)
            act.wait_ge(evac_done, EV_H + 32)
            act.activation(r_g, r_g, ACT.Silu).then_inc(r_silu_ready, 1)
            for a in range(NT):
                act.wait_ge(r_out_done, a + 1)
                act.activation(xc[:, 4 * a:4 * a + 4, :].rearrange("p a b -> p (a b)"),
                               ps[:, 4 + 2 * a:6 + 2 * a, :].rearrange("p a b -> p (a b)"), ACT.Square).then_inc(r_sq_ready, 1)
            for a in range(NT):
                act.wait_ge(r_var_ready, a + 1)
                act.activation(r_rr[:, 8 * a:8 * a + 8], r_ss[:, 8 * a:8 * a + 8], ACT.Sqrt).then_inc(r_std_ready, 1)
            act_mix_all(act, 7)

        def dve_hgrn(dve):
            def chain(ins):
                link(dve, dve_chain, "dve", ins)

            raw0, raw1 = par[:, LB:LB + 8], par[:, LB + 8:LB + 16]
            e0, e1, low, top = (lb[:, n, :] for n in range(4))
            chain(dve.tensor_tensor(low, raw0, raw1, ALU.max))
            dve.tensor_tensor(e0, raw0, low, ALU.subtract)
            dve.tensor_tensor(e1, raw1, low, ALU.subtract).then_inc(lb_arg, 1)
            dve.wait_ge(lb_exp, 1)
            chain(dve.tensor_tensor(top, e0, e1, ALU.add))
            chain(dve.reciprocal(top, top))
            dve.tensor_tensor(e0, e0, top, ALU.mult)
            chain(dve.tensor_tensor(e1, e1, top, ALU.mult))
            chain(dve.tensor_tensor(low, e0, e1, ALU.add))
            chain(dve.tensor_tensor(low, low, e0, ALU.subtract))
            chain(dve.tensor_scalar(top, low, -1.0, 1.0, ALU.mult, ALU.add))

            def args(u):
                if u == 0:
                    dve.wait_ge(x_scaled, 5)
                if u >= 2:
                    dve.wait_ge(level_scored, u - 1)
                m = LEVELS[u] if u < N_LEVELS else P
                e, b = (halves(v, m) for v in (level_buf[u % 2][:, :, :], r_b))
                ref = b[:, :, 0, m - 1:m].to_broadcast([P, H_HEADS * T // (2 * m), m])
                dve.tensor_tensor(e[:, :, 0, :], ref, b[:, :, 0, :], ALU.subtract)
                if u < N_LEVELS:
                    dve.tensor_tensor(e[:, :, 1, :], b[:, :, 1, :], ref, ALU.subtract).then_inc(level_arg, 1)
                else:
                    dve.tensor_copy(e[:, :, 1, :], b[:, :, 1, :]).then_inc(level_arg, 1)

            def place(u):
                dve.wait_ge(level_scored, u + 1)
                m = LEVELS[u]
                mask = const("levels")[:, u * 64:(u + 1) * 64].bitcast(I32)
                mask = bc(mask, 1, 2 * H_HEADS).rearrange("p a (n m) -> p a n m", m=m)
                dst = r_at.rearrange("p a (n b m) -> p a n b m", b=2, m=m)[:, :, :, 1, :]
                src = level_bank(u).rearrange("p b (i n m) -> p (b i) n m", n=64 // m, m=m)
                dve.copy_predicated(dst, mask, src).then_inc(level_placed, 1)

            for o in range(32):
                if o >= 18 and o % 2 == 0:
                    u = (o - 18) // 2
                    place(u)
                    if u + 2 <= N_LEVELS:
                        args(u + 2)
                dve_split(dve, half0[8] + o + HALF_SLOTS)
                if o == 7:
                    dve.wait_ge(evac_done, EV_H + 8)
                    dve.tensor_scalar(r_b, r_b, TINY, None, ALU.max).then_inc(f_ready, 1)
                    dve.tensor_tensor(r_k, r_k, bc(top, 2, T), ALU.mult).then_inc(k_ready, 1)
                if o == 9:
                    for h in range(H_HEADS):
                        dve.wait_ge(logf_ready, h + 1)
                        last = dve.tensor_tensor_scan(r_b[:, h, :], const("restart"), r_b[:, h, :], 0.0, ALU.mult, ALU.add)
                    chain(last)
                if o in (12, 14):
                    args((o - 12) // 2)
                if o == 17:
                    dve.wait_ge(diag_done, 1)
                    dve.tensor_tensor(r_at, ps[:, 4:8, :].rearrange("p b (i n) -> p (b i) n", n=P),
                                      bc(ident, 1, 2 * H_HEADS), ALU.mult).then_inc(diag_ready, 1)
                    dve.wait_ge(diag_ready, 1)
            for a in range(NT):
                dve.wait_ge(r_sq_ready, a + 1)
                cols = slice(8 * a, 8 * a + 8)
                chain(dve.tensor_reduce(r_ss[:, cols], xc[:, 4 * a:4 * a + 4, :].rearrange("p a b -> p (a b)")
                                        .rearrange("p (h d) -> p h d", d=P), AX, ALU.add))
                dve.tensor_scalar(r_ss[:, cols], r_ss[:, cols], 1.0 / P, RMS_EPS, ALU.mult, ALU.add).then_inc(r_var_ready, 1)
            dve.wait_ge(r_gate_ready, 1)
            for a in range(NT):
                cols = slice(8 * a, 8 * a + 8)
                dve.wait_ge(r_std_ready, a + 1)
                chain(dve.reciprocal(r_rr[:, cols], r_rr[:, cols]))
                chain(dve.tensor_tensor(r_o[:, a, :].rearrange("p (h d) -> p h d", d=P),
                                        ps[:, 4 + 2 * a:6 + 2 * a, :].rearrange("p b (h d) -> p (b h) d", d=P),
                                        bc(r_rr[:, cols], 2, P), ALU.mult))
                dve.tensor_tensor(r_o[:, a, :], r_o[:, a, :], r_g[:, a, :], ALU.mult).then_inc(r_o_ready, 1)
            dve_mix_all(dve, 8)

        block = ctx.enter_context(nc.Block())

        @block.sync
        def _(sp):
            def load(slab, matrix, ap):
                dst = raw[:, slab % RAW_SLOTS, :]
                if matrix < 2:
                    dst = dst.rearrange("p (k n) -> p k n", k=KC)
                    src = ap.rearrange("(k p) n -> p k n", p=P)
                else:
                    dst = dst.rearrange("p (c n) -> p c n", c=2)
                    src = ap.rearrange("(c p) n -> p c n", p=P)
                sp.dma_start(dst, src).then_inc(raw_landed[slab % RAW_SLOTS], 16)

            for n, e in enumerate(plan):
                if e[0] == "lin":
                    for i, col in enumerate(e[2]):
                        slab = slab0[n] + i
                        if slab >= RAW_SLOTS:
                            sp.wait_ge(lo_ready, raw_freed(slab - RAW_SLOTS))
                        load(slab, 0, e[1][:, col:col + 256])
                    continue
                for m in range(3):
                    sp.wait_ge(lo_ready, raw_freed(slab0[n] + m - RAW_SLOTS))
                    w = e[1][m]
                    load(slab0[n] + m, m, w[:, 0:256] if m < 2 else w[0:256, :])
                with sp.Fori(1, FFN_STEPS) as j:
                    for m in range(3):
                        sp.wait_ge(lo_ready, j * 6 + (half0[n] - 6 + LAST_OF[m]))
                        w = e[1][m]
                        load(slab0[n] + m, m, w[:, bass.ds(j * 256, 256)] if m < 2 else w[bass.ds(j * 256, 256), :])
            sp.wait_ge(out_ready, 2)
            sp.dma_start(out[0].rearrange("(a p) d -> p a d", p=P), x_tok[:, :, :]).then_inc(stored, 16)
            sp.wait_ge(stored, 16)

        row_sources = [
            (0, 0, io["ln1_g"].rearrange("a (k p) -> (a k) p", p=P)),
            (0, LN2, io["ln2_g"].rearrange("a (k p) -> (a k) p", p=P)),
            (0, LNG, io["ln_gain_2"].rearrange("i j (k p) -> (i j k) p", p=P)),
            (0, LNB, io["ln_bias_2"].rearrange("i j (k p) -> (i j k) p", p=P)),
            (1, 0, io["m_conv"].rearrange("a j (c p) -> (a j c) p", p=P)),
            (1, PSCALE - MCONV, io["pool_scale"].rearrange("a (c p) -> (a c) p", p=P)),
            (1, LB - MCONV, io["hgrn_lb_2"].rearrange("i (k p) -> (i k) p", p=P)),
            (1, FCONV - MCONV, io["ffn_conv"][0, 0:2].rearrange("j (c p) -> (j c) p", p=P)),
            (2, 0, io["ffn_conv"][0, 2:3].rearrange("j (c p) -> (j c) p", p=P)),
            (2, CPOS - FCONV - 88, io["nsa_cmp_pos_2"][0].rearrange("z (l q) d -> (z l) (q d)", q=2)),
        ]
        N_ROW_DMAS = len(row_sources) + 4
        N_SMALL_DMAS = 14

        def spread(ap, n):
            return bass.AP(tensor=ap.tensor, offset=ap.offset, ap=[[0, P], [1, n]])

        @block.gpsimd
        def _(pool):
            for g, row, src in row_sources:
                pool.dma_start(rows[row:row + src.shape[0], g, :], src).then_inc(rows_landed, 16)
            for n, name in ((AQ, "a_q_g"), (AK, "a_k_g")):
                for twice in range(2):
                    pool.dma_start(rows[n - MCONV:n - MCONV + 1, 1, twice * DH:(twice + 1) * DH],
                                   io[name]).then_inc(rows_landed, 16)
            pool.memset(m_v[:, :, :, DH:DH + 1], 1.0).then_inc(ones_ready, 1)
            pool.memset(pool_w, 0.0).then_inc(pads_ready, 1)
            pool.wait_ge(pads_ready, 1)
            small = [(gate_w, w_in[:, 1280:1288].rearrange("(k p) n -> p k n", p=P)),
                     (hot, io["distance_buckets"]), (table, io["rel_bias_2"]),
                     (gate_w2[:, :, :], n_in[:, 2560:2608].rearrange("(k p) n -> p k n", p=P)),
                     (w2_k[:, 0, :], io["nsa_cmp_w2_2"][0, 0]), (w2_k[:, 1, :], io["nsa_cmp_w2_2"][0, 0]),
                     (w2_v[:, :], io["nsa_cmp_w2_2"][0, 1]),
                     (mng, spread(io["m_norm_g"][0], 256)),
                     (gate_bias[:, 0:1], io["m_b_i"].rearrange("a h -> h a")),
                     (gate_bias[:, 1:2], io["m_b_f"].rearrange("a h -> h a"))]
            small += [(pool_w[64 * (g % 2):64 * (g % 2) + 64, g // 2, 64 * (g % 2):64 * (g % 2) + 64],
                       io["pool_w"][0, g]) for g in range(4)]
            for dst, src in small:
                pool.dma_start(dst, src).then_inc(small_landed, 16)
            assert len(small) == N_SMALL_DMAS
            pool.wait_ge(rows_evac, 1)
            pool.dma_start(scratch, bias_row).then_inc(rows_stored, 16)
            pool_first(pool)
            pool_norm(pool, 2)
            pool_load_nsa(pool)
            pool_nsa(pool)
            pool_norm(pool, 4)
            pool_norm(pool, 5)
            pool_hgrn(pool)
            pool_norm(pool, 7)
            pool_norm(pool, 8)
            pool.wait_ge(rows_stored, 16)

        @block.scalar
        def _(act):
            act.dma_start(x_tok, io["x"][0].rearrange("(a p) d -> p a d", p=P)).then_inc(x_landed, 16)
            act.dma_start(consts[:, :], io["shape_constants"]).then_inc(const_landed, 16)
            act.wait_ge(const_landed, 16)
            for b in range(4):
                act_squares(act, 0, b)
            act_start(act)
            act_norm(act, 0)
            act_bias_rows(act)
            for h in range(HALF_SLOTS):
                act_split(act, h)
            act_first(act)
            act_project(act, 1, 0)
            act_norm(act, 1)
            act_split(act, half0[2] + 4)
            act_split(act, half0[2] + 5)
            act_ffn(act, 2, 1)
            act_norm(act, 2)
            act_split(act, half0[3] + 4)
            act_split(act, half0[3] + 5)
            act_ffn(act, 3, 2)
            act_norm(act, 3)
            act_split(act, half0[4] + 4)
            act_split(act, half0[4] + 5)
            act_nsa(act)
            act_project(act, 5, 3)
            act_norm(act, 4)
            act_split(act, half0[6] + 4)
            act_split(act, half0[6] + 5)
            act_ffn(act, 6, 4)
            act_norm(act, 5)
            act_split(act, half0[7] + 4)
            act_split(act, half0[7] + 5)
            act_ffn(act, 7, 5)
            act_norm(act, 6)
            act_split(act, half0[8] + 4)
            act_split(act, half0[8] + 5)
            act_hgrn(act)
            act_project(act, 9, 6)
            act_norm(act, 7)
            act_split(act, half0[10] + 4)
            act_split(act, half0[10] + 5)
            act_ffn(act, 10, 7)
            act_norm(act, 8)

        @block.vector
        def _(dve):
            dve_start(dve)
            dve.wait_ge(par_ready, 1)
            dve_norm(dve, 0)
            dve.wait_ge(const_landed, 16)
            dve.wait_ge(small_landed, 16 * N_SMALL_DMAS)
            dve_bias_rows(dve)
            for h in range(HALF_SLOTS):
                dve_split(dve, h)
            dve_first(dve)
            dve_project(dve, 1, 0, 0)
            dve_norm(dve, 1)
            dve_split(dve, half0[2] + 4)
            dve_split(dve, half0[2] + 5)
            dve_ffn(dve, 2, 1, 0)
            dve_norm(dve, 2)
            dve_split(dve, half0[3] + 4)
            dve_split(dve, half0[3] + 5)
            dve_ffn(dve, 3, 2, 1)
            dve_norm(dve, 3)
            dve_split(dve, half0[4] + 4)
            dve_split(dve, half0[4] + 5)
            dve_nsa(dve)
            dve_project(dve, 5, 3, 2)
            dve_norm(dve, 4)
            dve_split(dve, half0[6] + 4)
            dve_split(dve, half0[6] + 5)
            dve_ffn(dve, 6, 4, 3)
            dve_norm(dve, 5)
            dve_split(dve, half0[7] + 4)
            dve_split(dve, half0[7] + 5)
            dve_ffn(dve, 7, 5, 4)
            dve_norm(dve, 6)
            dve_split(dve, half0[8] + 4)
            dve_split(dve, half0[8] + 5)
            dve_hgrn(dve)
            dve_project(dve, 9, 6, 5)
            dve_norm(dve, 7)
            dve_split(dve, half0[10] + 4)
            dve_split(dve, half0[10] + 5)
            dve_ffn(dve, 10, 7, 6)
            dve_norm(dve, 8)
            dve_finish(dve)

        @block.tensor
        def _(pe):
            pe_start(pe)
            for b in range(4):
                pe_stats(pe, 0, b)
            pe_params(pe)
            pe_bias_rows(pe)
            pe_first(pe)
            pe_project(pe, 1, 0)
            pe_ffn(pe, 2, 1)
            pe_ffn(pe, 3, 2)
            pe_nsa(pe)
            pe_project(pe, 5, 3)
            pe_ffn(pe, 6, 4)
            pe_ffn(pe, 7, 5)
            pe_hgrn(pe)
            pe_project(pe, 9, 6)
            pe_ffn(pe, 10, 7)
            pe_finish(pe, True)


_INS = ["x", "ln1_g", "w_in", "pool_w", "pool_scale", "m_conv", "m_b_i", "m_b_f", "m_norm_g", "a_q_g", "a_k_g",
        "w_out", "ln2_g", "w_up", "ffn_conv", "w_down", "rel_bias_2", "ln_gain_2", "ln_bias_2", "ffn1_w_gate_2",
        "ffn1_w_up_2", "ffn1_w_down_2", "ffn2_w_gate_2", "ffn2_w_up_2", "ffn2_w_down_2", "nsa_w_in_2",
        "nsa_w_out_2", "nsa_cmp_pos_2", "nsa_cmp_w1_2", "nsa_cmp_w2_2", "hgrn_w_in_2", "hgrn_w_out_2",
        "hgrn_norm_gain_2", "hgrn_lb_2"]
STOP = 11


def kernel(**inputs):
    import concourse.bacc as bacc
    from concourse.bass_utils import run_bass_kernel_spmd

    nc = bacc.Bacc("TRN2", target_bir_lowering=False, num_devices=1)
    arrays, io = {}, {}
    for name in _INS:
        arrays[name] = np.ascontiguousarray(inputs[name])
    arrays["shape_constants"], const_at = shape_constants()
    arrays["distance_buckets"] = distance_buckets()
    for name, a in arrays.items():
        io[name] = nc.dram_tensor(name, a.shape, mybir.dt.from_np(a.dtype), kind="ExternalInput").ap()
    out = nc.dram_tensor("out", (1, T, D), F32, kind="ExternalOutput").ap()
    build_program(nc, io, const_at, out, STOP)
    result = run_bass_kernel_spmd(nc, [arrays], core_ids=[0])
    return result.results[0]["out"]
```

```python
import math
from contextlib import ExitStack

import numpy as np
import concourse.bass as bass
from concourse import mybir

F32 = mybir.dt.float32
F32R = mybir.dt.float32r
BF16 = mybir.dt.bfloat16
I32 = mybir.dt.int32
ACT = mybir.ActivationFunctionType
ALU = mybir.AluOpType
AX = mybir.AxisListType.X

P = 128
D = 1024
T = 256
KC = D // P
NT = T // P
D_FF = 2816
FFN_STEPS = D_FF // (2 * P)
M_HEADS = 4
A_HEADS = 8
DH = 64
N_HEADS = 16
N_GROUPS = 4
REL_BUCKETS = 32
REL_EXACT = REL_BUCKETS // 2
REL_MAX_DIST = 128
CMP_STRIDE = 16
CMP_LEN = 32
N_CMP = T // CMP_STRIDE - 1
H_HEADS = 8
LN_EPS = 1e-5
RMS_EPS = 1e-6
MASKED = -1e30
TINY = 1e-19
LARGE = 3e38
V_COLS = DH + N_GROUPS * 2 * DH
ALPHA = (2.0 * 2) ** 0.25
QK_SCALE = DH ** -0.5
POOL_WINDOWS = (2, 4, 8, 16)
PAD = 16
BIAS_COLS = P + T
LEVELS = (64, 32, 16, 8, 4, 2, 1)

RAW_SLOTS = 3
HALF_SLOTS = 6
ARENA = 16944
KEEP = 18


def shape_constants():
    i = np.arange(P)
    t = np.arange(T)
    parts = {}
    parts["ident"] = np.eye(P)
    parts["mean"] = np.full((P, P), 1.0 / D)
    parts["one"] = np.ones((P, 1))
    parts["flip"] = np.eye(P)[::-1]
    parts["causal"] = np.concatenate([np.zeros((P, P)), np.where(i[None, :] > i[:, None], MASKED, 0.0)], 1)
    parts["causal_rev"] = np.where(i[None, :] > P - 1 - i[:, None], MASKED, 0.0)
    parts["late"] = np.concatenate([np.where(i[None, :] < i[:, None], -MASKED, 0.0), np.zeros((P, P))], 1)
    inv = np.zeros((P, 2, T))
    for g, w in enumerate(POOL_WINDOWS):
        inv[64 * (g % 2):64 * (g % 2) + 64, g // 2] = 1.0 / np.minimum(t + 1, w)
    parts["inv_count"] = inv.reshape(P, -1)
    restart = np.ones((P, T))
    restart[:, ::P] = 0.0
    parts["restart"] = restart
    parts["ones"] = np.ones((P, T))
    valid = np.zeros((P, NT, N_CMP))
    for a in range(NT):
        valid[:, a] = (a * P + P - 1 - i)[:, None] >= CMP_STRIDE * np.arange(N_CMP)[None, :] + CMP_LEN - 1
    parts["cmp_valid"] = valid.reshape(P, -1)
    heads = np.zeros((P, 8))
    heads[np.arange(8 * N_CMP), np.arange(8 * N_CMP) // N_CMP] = 1.0
    parts["own_head"] = heads
    parts["levels"] = level_masks()
    parts["minus_half"] = np.full((P, 1), -0.5)
    at, cols = {}, 0
    for name, a in parts.items():
        at[name] = (cols, a.shape[1])
        cols += a.shape[1]
    return np.concatenate(list(parts.values()), 1).astype(np.float32), at


def level_masks():
    i = np.arange(P)
    levels = []
    for m in LEVELS:
        t = i[i // m % 2 == 1]
        levels.append((i[:, None] // (2 * m) == t[None, :] // (2 * m)) & (i[:, None] // m % 2 == 0))
    return np.concatenate(levels, 1)


def distance_buckets():
    def one_hot(dist):
        n = np.maximum(dist, 0)
        large = REL_EXACT + (np.log(np.maximum(n, 1) / REL_EXACT) / math.log(REL_MAX_DIST / REL_EXACT)
                             * (REL_BUCKETS - REL_EXACT)).astype(np.int64)
        b = np.where(n < REL_EXACT, n, np.minimum(large, REL_BUCKETS - 1))
        return np.eye(REL_BUCKETS)[b].T

    return one_hot(T - 1 - np.arange(BIAS_COLS)).astype(np.float32)


def build_program(nc, io, const_at, out):
    ctx = ExitStack()
    with ctx:
        def sb(name, shape, dt=F32):
            return ctx.enter_context(nc.sbuf_tensor(name, shape, dt))

        def sem(name):
            return ctx.enter_context(nc.semaphore(name))

        n_const = sum(n for _, n in const_at.values())
        consts = sb("consts", [P, n_const])
        raw = sb("raw", [P, RAW_SLOTS, 2048])
        whi = sb("whi", [P, HALF_SLOTS, 1024], F32R)
        wlo = sb("wlo", [P, HALF_SLOTS, 1024], F32R)
        xT = sb("xT", [P, KC, T])
        xc_at = nc.sbuf_base
        xc = sb("xc", [P, KC, T])
        sq_at = nc.sbuf_base
        sq = sb("sq", [P, KC, T])
        assert sq_at - xc_at == 4 * KC * T
        ahi = sb("ahi", [P, KC, T], F32R)
        alo = sb("alo", [P, KC, T], F32R)
        var = sb("var", [P, T])
        rstd = sb("rstd", [P, T])
        table_use = sb("table_use", [P, 1])
        ghi = sb("ghi", [P, 2, T], F32R)
        glo = sb("glo", [P, 2, T], F32R)
        ffn_buf = sb("ffn_buf", [P, 4, 2 * T])
        gate_act, conv_g, conv_u, gated = (ffn_buf[:, n, :].rearrange("p (a b) -> p a b", a=2) for n in range(4))
        zeros = sb("zeros", [P, 512], BF16)
        par = sb("par", [P, 316])
        arena_at = -(-nc.sbuf_base // 32) * 32
        arena = sb("arena", [P, ARENA])
        scratch = nc.dram_tensor("bias_rows", (N_HEADS, 384), F32, kind="Internal").ap()
        ps = ctx.enter_context(nc.psum_tensor("ps", [P, 8, 512], F32))

        def const(name, rows=P):
            at, n = const_at[name]
            return consts[0:rows, at:at + n]

        ident = const("ident")
        N_FIRST = const_at["one"][0] + 1

        def view(at, *shape, rows=P):
            n = int(np.prod(shape))
            assert at + n <= ARENA, (at, shape)
            v = arena[0:rows, at:at + n]
            if len(shape) == 2:
                v = v.rearrange("p (a b) -> p a b", a=shape[0])
            if len(shape) == 3:
                v = v.rearrange("p (a b c) -> p a b c", a=shape[0], b=shape[1])
            return at + n, v

        def split_view(at, name, *shape):
            assert at % 8 == 0 and at + int(np.prod(shape)) <= ARENA, (at, shape)
            return at + int(np.prod(shape)), nc.alloc_sbuf_tensor_at(name, [P, *shape], F32R, offset=arena_at + 4 * at)

        def bc(ap, axis, n):
            a = ap.unsqueeze(axis)
            shape = list(a.shape)
            shape[axis] = n
            return a.to_broadcast(shape)

        LN1, LN2, LNG, LNB = 0, 8, 16, 64
        MCONV, PSCALE, LB, AQ, AK, FCONV, CPOS = 112, 128, 130, 146, 147, 148, 280
        n_rows = (112, 124, 76)
        N_POOL_ROWS = 5

        def spare(tensor, at, *shape, rows=P):
            v = tensor.rearrange("p a b -> p (a b)")[0:rows, at:at + int(np.prod(shape))]
            return v if len(shape) == 1 else v.rearrange("p (a b) -> p a b", a=shape[0])

        at, qk_hi = split_view(0, "qk_hi", KC, T)
        at, qk_lo = split_view(at, "qk_lo", KC, T)
        at, av_hi = split_view(at, "av_hi", NT, 4, 3 * DH)
        at, av_lo = split_view(at, "av_lo", NT, 4, 3 * DH)
        at, z_qk = view(at, NT, 1024)
        at, m_v = view(at, NT, M_HEADS, DH + 1)
        at, m_o = view(at, NT, 256)
        startup = at
        at, conv_out = view(at, 4, T)
        at, decay = view(at, M_HEADS, 384)
        at, h_out = view(at, NT, 256)
        at, h_sq = view(at, NT, 256)
        at, att_score = view(at, 2, 384)
        at, att_prob = view(at, 3, 384)
        at, att_nmax = view(at, 2, 2)
        at, gates = view(at, NT, 8)
        at, ss = view(at, 32)
        at, rr = view(at, 32)
        at, a_sums = view(at, A_HEADS, 2)
        at, a_rsum = view(at, A_HEADS, 2)
        at, ucols = view(at, 16)
        at, den = view(at, NT, M_HEADS)
        at, m_ss = view(at, 8)
        at, m_rr = view(at, 8)
        at, gate_w = view(at, KC, 8)
        at, mng = view(at, 256)
        at, pool_w = view(at, 2, P)
        at, gate_bias = view(at, 2, rows=M_HEADS)
        i_g, f_g = (gate_act[0:M_HEADS, n, :] for n in range(2))
        f_abs, f_log = (conv_g[0:M_HEADS, n, :] for n in range(2))
        g_cum, u_g = (conv_u[0:M_HEADS, n, :] for n in range(2))
        m_cum, m_t = (gated[0:M_HEADS, n, :] for n in range(2))
        e_mt = f_abs
        conv_in = spare(xc, 0, 4, 3 + T)
        p_d = spare(xc, 4 * (3 + T), 2, T)
        p_in = spare(sq, 0, 2, PAD + T)
        p_2 = spare(sq, 2 * (PAD + T), 2, PAD + T)
        p_4 = spare(sq, 4 * (PAD + T), 2, PAD + T)
        p_8 = spare(sq, 6 * (PAD + T), 1, PAD + T)
        x_tok = spare(xc, 0, NT, D)
        out_tok = spare(sq, 0, NT, D)
        at, rows = view(startup, 3, P)
        at, hot = view(at, BIAS_COLS, rows=REL_BUCKETS)
        at, table = view(at, N_HEADS, rows=REL_BUCKETS)
        at, bias_row = view(at, BIAS_COLS, rows=N_HEADS)

        at, q_hi = split_view(0, "q_hi", KC, T)
        at, q_lo = split_view(at, "q_lo", KC, T)
        at, k_sel_hi = split_view(at, "k_sel_hi", 2, 2 * T)
        at, k_sel_lo = split_view(at, "k_sel_lo", 2, 2 * T)
        at, k_win_hi = split_view(at, "k_win_hi", 2, 2 * T)
        k_win_lo = (ghi, glo)
        at, v_sel_hi = split_view(at, "v_sel_hi", NT, V_COLS)
        at, v_win_hi = split_view(at, "v_win_hi", NT, V_COLS)
        v_sel_lo, v_win_lo = (nc.alloc_sbuf_tensor_at(name, [P, NT, V_COLS], F32R, offset=base)
                              for name, base in (("v_sel_lo", xc_at), ("v_win_lo", sq_at)))
        at, kc_hi = split_view(at, "kc_hi", N_GROUPS, 2 * N_CMP)
        at, kc_lo = split_view(at, "kc_lo", N_GROUPS, 2 * N_CMP)
        at, bias = view(at, N_HEADS, T)
        at, z_k = view(at, N_GROUPS + 1, T + 1)
        at, z_v = view(at, N_GROUPS + 1, T + 1)
        at, n_gates = view(at, NT, 48)
        at, n_sums = view(at, 2 * N_HEADS, 2)
        at, n_rsum = view(at, 2 * N_HEADS, 2)
        at, n_coef = view(at, 2 * N_HEADS, 2)
        at, n_nmax = view(at, 2, 2)
        at, hidT = view(at, 2, N_GROUPS * N_CMP)
        at, hid_bias = view(at, 2)
        hid_heads = spare(ffn_buf, 0, N_HEADS, N_CMP)
        at, c_max = view(at, NT, N_HEADS)
        at, c_sum = view(at, NT, N_HEADS)
        n_score, n_prob = spare(ffn_buf, 0, 2, 384), spare(ffn_buf, 768, 3, 384)
        c_score = z_k.rearrange("p a b -> p (a b)")[:, 0:480].rearrange("p (a b) -> p a b", a=NT)
        c_probT = z_k.rearrange("p a b -> p (a b)")[:, 480:992].rearrange("p (a b) -> p a b", a=2)
        c_val = z_v.rearrange("p a b -> p (a b)")[:, 0:1024].rearrange("p (a b) -> p a b", a=2)
        w1_k, w1_v = (spare(w, 0, 16, P) for w in (sq, xc))

        probT_hi, probT_lo = spare(ahi, 4 * T, 2, 4 * P), spare(alo, 4 * T, 2, 4 * P)

        at, r_q = view(0, H_HEADS, T)
        at, r_k = view(at, H_HEADS, T)
        at, r_b = view(at, H_HEADS, T)
        at, r_v = view(at, NT, D)
        at, r_g = view(at, NT, D)
        at, r_at = view(at, 2 * H_HEADS, P)
        at, r_cross = view(at, H_HEADS, P)
        at, r_o = view(at, NT, D)
        at, r_ss = view(at, 16)
        at, r_rr = view(at, 16)
        at, lb = view(at, 4, H_HEADS)
        at, r_gain = view(at, P)

        gate_w2 = sb("gate_w2", [P, KC, 48])
        w2_k = sb("w2_k", [P, 2, DH])
        w2_v = sb("w2_v", [P, DH])

        raw_landed = [sem(f"raw_landed{n}") for n in range(RAW_SLOTS)]
        ident_landed = sem("ident_landed")
        const_landed = sem("const_landed")
        x_landed = sem("x_landed")
        rows_landed = sem("rows_landed")
        pool_rows_landed = sem("pool_rows_landed")
        small_landed = sem("small_landed")
        hi_ready = sem("hi_ready")
        lo_ready = sem("lo_ready")
        half_done = sem("half_done")
        x_turned = sem("x_turned")
        x_ready = sem("x_ready")
        x_scaled = sem("x_scaled")
        par_turned = sem("par_turned")
        par_ready = sem("par_ready")
        zeros_ready = sem("zeros_ready")
        sq_ready = sem("sq_ready")
        xs_ready = sem("xs_ready")
        sqs_ready = sem("sqs_ready")
        stats_done = sem("stats_done")
        mean_sq_ready = sem("mean_sq_ready")
        std_ready = sem("std_ready")
        xg_ready = sem("xg_ready")
        ahi_ready = sem("ahi_ready")
        var_ready = sem("var_ready")
        xc_ready = sem("xc_ready")
        a_ready = sem("a_ready")
        a_pool_ready = sem("a_pool_ready")
        evac_done = sem("evac_done")
        mix_turned = sem("mix_turned")
        mix_hi = sem("mix_hi")
        mix_lo = sem("mix_lo")
        conv0_ready = sem("conv0_ready")
        convg_ready = sem("convg_ready")
        silu_ready = sem("silu_ready")
        g_ready = sem("g_ready")
        ffn_chain = sem("ffn_chain")
        y_ready = sem("y_ready")
        out_turned = sem("out_turned")
        out_ready = sem("out_ready")
        out_odd_ready = sem("out_odd_ready")
        stored = sem("stored")
        dve_chain = sem("dve_chain")
        act_chain = sem("act_chain")
        pool_chain = sem("pool_chain")
        counts = {"dve": 0, "act": 0, "pool": 0}

        def link(engine, semaphore, name, instruction):
            counts[name] += 1
            instruction.then_inc(semaphore, 1)
            engine.wait_ge(semaphore, counts[name])

        w_in, w_out = io["w_in"][0], io["w_out"][0]
        n_in, n_out = io["nsa_w_in_2"][0], io["nsa_w_out_2"][0]
        r_in, r_out = io["hgrn_w_in_2"][0], io["hgrn_w_out_2"][0]
        up0 = io["w_up"][0]
        A_COLS = [1288 + 256 * n for n in range(4)] + [256, 512, 2312, 2568, 0, 768, 1024]
        N_COLS = [1024, 1280, 0, 256, 512, 768, 1536, 1792, 2048, 2304]
        H_COLS = [1024 + 256 * n for n in range(4)] + [256 * n for n in range(4)] + \
                 [2048 + 256 * n for n in range(8)]
        O_COLS = [256 * n for n in range(4)]

        def ffn_mats(i, which):
            return tuple(io[f"ffn{which}_w_{m}_2"][i] for m in ("gate", "up", "down"))

        plan = [
            ("lin", w_in, A_COLS),
            ("lin", w_out, O_COLS),
            ("ffn", (up0[:, 0:D_FF], up0[:, D_FF:2 * D_FF], io["w_down"][0])),
            ("ffn", ffn_mats(0, 1)),
            ("lin", n_in, N_COLS),
            ("lin", n_out, O_COLS),
            ("ffn", ffn_mats(0, 2)),
            ("ffn", ffn_mats(1, 1)),
            ("lin", r_in, H_COLS),
            ("lin", r_out, O_COLS),
            ("ffn", ffn_mats(1, 2)),
        ]
        slab0 = [0]
        for e in plan:
            slab0.append(slab0[-1] + (len(e[2]) if e[0] == "lin" else 3 * FFN_STEPS))
        half0 = [2 * s for s in slab0]
        FFN_STEP = [(0, 0), (1, 0), (0, 1), (1, 1), (2, 0), (2, 1)]
        LAST_OF = (3, 4, 6)

        def stage_of(half):
            return max(n for n in range(len(plan)) if half0[n] <= half)

        def raw_freed(slab):
            n = stage_of(2 * slab)
            if plan[n][0] == "lin":
                return 2 * slab + 2
            j, m = divmod(slab - slab0[n], 3)
            return half0[n] + 6 * j + LAST_OF[m]

        def raw_half(kind, slot, matrix, x):
            if kind == "lin" or matrix < 2:
                return raw[:, slot, :].rearrange("p (k n) -> p k n", k=KC)[:, :, x * P:(x + 1) * P]
            return raw[:, slot, x * D:(x + 1) * D]

        def split_half(w, h, kind, matrix):
            v = w[:, h % HALF_SLOTS, :]
            return v.rearrange("p (k n) -> p k n", k=KC) if kind == "lin" or matrix < 2 else v

        def half_place(h):
            n = stage_of(h)
            if plan[n][0] == "lin":
                return "lin", 0, h % 2, h // 2
            j, s = divmod(h - half0[n], 6)
            m, x = FFN_STEP[s]
            return "ffn", m, x, slab0[n] + 3 * j + m

        n_halves = half0[-1]

        def act_split(act, h):
            if h >= n_halves:
                return
            kind, m, x, slab = half_place(h)
            act.wait_ge(raw_landed[slab % RAW_SLOTS], 16 * (slab // RAW_SLOTS + 1))
            if h >= HALF_SLOTS:
                act.wait_ge(half_done, h - HALF_SLOTS + 1)
            act.activation(split_half(whi, h, kind, m), raw_half(kind, slab % RAW_SLOTS, m, x),
                           ACT.Copy).then_inc(hi_ready, 1)

        def dve_split(dve, h):
            if h >= n_halves:
                return
            kind, m, x, slab = half_place(h)
            dve.wait_ge(hi_ready, h + 1)
            dve.tensor_tensor(split_half(wlo, h, kind, m), raw_half(kind, slab % RAW_SLOTS, m, x),
                              split_half(whi, h, kind, m).bitcast(F32), ALU.subtract).then_inc(lo_ready, 1)

        def act_split_next(act, n, j, s):
            m, x = FFN_STEP[s]
            slab = slab0[n] + 3 + m
            h = half0[n] + 6 + s
            act.wait_ge(raw_landed[slab % RAW_SLOTS], j * 16 + 16 * (slab // RAW_SLOTS + 1))
            act.wait_ge(half_done, j * 6 + (h - HALF_SLOTS + 1))
            act.activation(split_half(whi, h, "ffn", m), raw_half("ffn", slab % RAW_SLOTS, m, x),
                           ACT.Copy).then_inc(hi_ready, 1)

        def dve_split_next(dve, n, j, s):
            m, x = FFN_STEP[s]
            slab = slab0[n] + 3 + m
            h = half0[n] + 6 + s
            dve.wait_ge(hi_ready, j * 6 + (h + 1))
            dve.tensor_tensor(split_half(wlo, h, "ffn", m), raw_half("ffn", slab % RAW_SLOTS, m, x),
                              split_half(whi, h, "ffn", m).bitcast(F32), ALU.subtract).then_inc(lo_ready, 1)

        def three_pass(pe, dst, wh, wl, ah, al, first, last):
            pe.matmul(dst, wh, ah, start=first, stop=False, skip_group_check=True)
            pe.matmul(dst, wh, al, start=False, stop=False, skip_group_check=True)
            return pe.matmul(dst, wl, ah, start=False, stop=last, skip_group_check=True)

        def pe_halves_channels(pe, h, dsts, wait_chunk=None):
            for k in range(KC):
                if wait_chunk:
                    wait_chunk(k)
                for i, dst in enumerate(dsts):
                    wh, wl = (w[:, (h + i) % HALF_SLOTS, k * P:(k + 1) * P] for w in (whi, wlo))
                    last = three_pass(pe, dst, wh, wl, ahi[:, k, :], alo[:, k, :], k == 0, k == KC - 1)
                    if k == KC - 1:
                        last.then_inc(half_done, 1)

        def pe_half_channels(pe, h, dst):
            pe.wait_ge(lo_ready, h + 1)
            pe_halves_channels(pe, h, [dst])

        def pe_slab_tokens(pe, h, tiles, dsts, wait_chunk=None):
            s = h % HALF_SLOTS
            wh, wl = (w[:, s:s + 2, :].rearrange("p s (k n) -> p s k n", k=KC) for w in (whi, wlo))
            last = []
            for k in range(KC):
                if wait_chunk:
                    wait_chunk(k)
                for tile, dst in zip(tiles, dsts):
                    out2 = dst.rearrange("p (s n) -> p s n", s=2)
                    a_h, a_l = (a[:, k, tile * P:(tile + 1) * P] for a in (ahi, alo))
                    pe.matmul(out2, a_h, wh[:, :, k, :], start=k == 0, stop=False, skip_group_check=True)
                    pe.matmul(out2, a_l, wh[:, :, k, :], start=False, stop=False, skip_group_check=True)
                    ins = pe.matmul(out2, a_h, wl[:, :, k, :], start=False, stop=k == KC - 1, skip_group_check=True)
                    if k == KC - 1:
                        last.append(ins)
            return last

        def bank2(b):
            return ps[:, b, :].rearrange("p (a b) -> p a b", a=2)


        def x_count(p):
            return 4 + 8 * p

        PRE = [("rms", LN1, None, 4), ("rms", LN2, None, 2), ("none", None, None, 2),
               *(("ln", LNG + KC * i, LNB + KC * i, 2) for i in range(6))]

        def norm_index(p):
            return sum(PRE[n][0] != "none" for n in range(p))

        def x_pair(p, j):
            return j + 1 if p == 0 else x_count(p) - KC + 2 * j + 2

        def pe_stats(pe, p, j):
            kind, _, _, bank = PRE[p]
            ni = norm_index(p)
            if kind == "none":
                return
            if kind == "ln":
                pe.wait_ge(xs_ready, 4 * (ni - 2) + j + 1)
                pe.matmul(ps[:, bank, 0:T], const("mean"), xc[:, j, :], start=j == 0, stop=j == 3)
            pe.wait_ge(sqs_ready, 4 * ni + j + 1)
            last = pe.matmul(ps[:, bank + 1, 0:T], const("mean"), sq[:, 2 * j, :], start=j == 0, stop=j == 3)
            if j == 3:
                last.then_inc(stats_done, 1)

        def act_table(act, function):
            act.activation(table_use[:, :], const("one"), function)

        def act_squares(act, p, j):
            cs = slice(2 * j, 2 * j + 2)
            if j == 0 and PRE[p][0] != "none":
                act_table(act, ACT.Sqrt)
            act.wait_ge(x_ready, x_pair(p, j))
            if PRE[p][0] == "none":
                act.activation(ahi[:, cs, :], xT[:, cs, :], ACT.Copy).then_inc(ahi_ready, 2)
            else:
                act.activation(sq[:, cs, :], xT[:, cs, :], ACT.Square).then_inc(sq_ready, 1)

        def dve_sums(dve, p, j):
            kind = PRE[p][0]
            ni = norm_index(p)
            c = 2 * j
            dve.wait_ge(x_ready, x_pair(p, j))
            if kind == "none":
                dve.wait_ge(ahi_ready, KC * p + c + 2)
                dve.tensor_tensor(alo[:, c:c + 2, :], xT[:, c:c + 2, :], ahi[:, c:c + 2, :].bitcast(F32),
                                  ALU.subtract).then_inc(a_ready, 2)
                return
            if kind == "ln":
                dve.tensor_tensor(xc[:, j, :], xT[:, c, :], xT[:, c + 1, :], ALU.add).then_inc(xs_ready, 1)
            dve.wait_ge(sq_ready, 4 * ni + j + 1)
            dve.tensor_tensor(sq[:, c, :], sq[:, c, :], sq[:, c + 1, :], ALU.add).then_inc(sqs_ready, 1)

        def pool_tail(p, k):
            return PRE[p][0] == "ln" and k in (2, 4, 6)

        def a_counts(p, k):
            done = [(r, c) for r in range(min(p + 1, 8)) for c in range(KC) if r < p or c <= k]
            by_pool = sum(pool_tail(r, c) for r, c in done)
            return len(done) - by_pool, by_pool

        def wait_activations(engine, p, k=KC - 1):
            by_dve, by_pool = a_counts(p, k)
            engine.wait_ge(a_ready, by_dve)
            if by_pool:
                engine.wait_ge(a_pool_ready, by_pool)

        def dve_norm(dve, p):
            kind, gain, shift, bank = PRE[p]
            ni = norm_index(p)
            if kind == "none":
                return
            dve.wait_ge(stats_done, ni + 1)
            mean, square = ps[:, bank, 0:T], ps[:, bank + 1, 0:T]

            def centre(j):
                cs = slice(2 * j, 2 * j + 2)
                dve.tensor_tensor(xc[:, cs, :], xT[:, cs, :], bc(mean, 1, 2), ALU.subtract).then_inc(xc_ready, 1)

            if kind == "ln":
                dve.wait_ge(mean_sq_ready, ni - 1)
                link(dve, dve_chain, "dve", dve.scalar_tensor_tensor(var[:, :], var[:, :], -1.0, square, ALU.mult, ALU.add))
                dve.tensor_scalar(var[:, :], var[:, :], 0.0, LN_EPS, ALU.max, ALU.add).then_inc(var_ready, 1)
                centre(0)
            else:
                dve.tensor_scalar(var[:, :], square, RMS_EPS, None, ALU.add).then_inc(var_ready, 1)
            dve.wait_ge(std_ready, ni + 1)
            link(dve, dve_chain, "dve", dve.reciprocal(rstd[:, :], var[:, :]))

            if p == 0:
                dve.wait_ge(par_ready, 1)

            own = [k for k in range(KC) if p < 8 and not pool_tail(p, k)]

            def tail(k):
                dve.wait_ge(ahi_ready, KC * p + k + 1)
                hi = ahi[:, k, :].bitcast(F32)
                if kind == "ln":
                    ins = dve.scalar_tensor_tensor(alo[:, k, :], xc[:, k, :], par[:, shift + k:shift + k + 1], hi,
                                                   ALU.add, ALU.subtract)
                else:
                    ins = dve.tensor_tensor(alo[:, k, :], xc[:, k, :], hi, ALU.subtract)
                ins.then_inc(a_ready, 1)

            for k in range(KC):
                if kind == "ln" and k % 2 == 0:
                    dve.wait_ge(xc_ready, 4 * (ni - 2) + k // 2 + 1)
                dve.scalar_tensor_tensor(xc[:, k, :], (xc if kind == "ln" else xT)[:, k, :],
                                         par[:, gain + k:gain + k + 1], rstd[:, :], ALU.mult, ALU.mult).then_inc(xg_ready, 1)
                if kind == "ln" and k % 2 == 0 and k < KC - 2:
                    centre(k // 2 + 1)
                for c in own:
                    if min(c + (2 if kind != "ln" else 0 if c % 2 == 0 and c < KC - 2 else 1), KC - 1) == k:
                        tail(c)

        def act_norm(act, p):
            kind, _, shift, bank = PRE[p]
            ni = norm_index(p)
            if kind == "none":
                return
            if kind == "ln":
                act.wait_ge(stats_done, ni + 1)
                act.activation(var[:, :], ps[:, bank, 0:T], ACT.Square).then_inc(mean_sq_ready, 1)
            act.wait_ge(var_ready, ni + 1)
            act.activation(var[:, :], var[:, :], ACT.Sqrt).then_inc(std_ready, 1)
            if p == 0:
                act_start(act)
            for k in range(KC):
                act.wait_ge(xg_ready, KC * ni + k + 1)
                dst = ahi if p < 8 else xT
                if kind == "ln":
                    ins = act.activation(dst[:, k, :], xc[:, k, :], ACT.Identity, bias=par[:, shift + k:shift + k + 1])
                else:
                    ins = act.activation(dst[:, k, :], xc[:, k, :], ACT.Copy)
                ins.then_inc(ahi_ready, 1)

        def pool_norm(pool, p):
            kind, _, shift, _ = PRE[p]
            ni = norm_index(p)
            if kind == "none":
                wait_activations(pool, p)
                pool.tensor_scalar(xT[:, :, :], xT[:, :, :], ALPHA, None, ALU.mult).then_inc(x_scaled, 1)
            if kind == "ln" and p < 8:
                for k in [c for c in range(KC) if pool_tail(p, c)]:
                    pool.wait_ge(xg_ready, KC * ni + k + 1)
                    link(pool, pool_chain, "pool", pool.tensor_scalar(xT[:, k, :], xc[:, k, :],
                                                                      par[:, shift + k:shift + k + 1], None, ALU.add))
                    pool.wait_ge(ahi_ready, KC * p + k + 1)
                    pool.tensor_tensor(alo[:, k, :], xT[:, k, :], ahi[:, k, :].bitcast(F32),
                                       ALU.subtract).then_inc(a_pool_ready, 1)
                pool.wait_ge(xg_ready, KC * (ni + 1))
                for k in range(KC):
                    if pool_tail(p, k):
                        last = pool.tensor_scalar(xT[:, k, :], xT[:, k, :], ALPHA, None, ALU.mult)
                    else:
                        last = pool.tensor_scalar(xT[:, k, :], xc[:, k, :], par[:, shift + k:shift + k + 1], ALPHA,
                                                  ALU.add, ALU.mult)
                last.then_inc(x_scaled, 1)

        def mix_count(n):
            return 4 * ((1, 5, 9).index(n) + 1)

        def project_bank(n, s):
            return s if s < 2 and n != 9 else 4 + s % 4

        def pe_project(pe, n, p):
            pe.wait_ge(lo_ready, half0[n] + 2)
            pe_halves_channels(pe, half0[n], [ps[:, project_bank(n, s), 0:T] for s in range(2)],
                               lambda k: pe.wait_ge(mix_lo, mix_count(n) - (3 - k // 2 if n > 1 else 0)))
            for s in range(2, 8):
                if s >= 4:
                    pe.wait_ge(x_ready, x_count(p) + s - 3)
                pe_half_channels(pe, half0[n] + s, ps[:, project_bank(n, s), 0:T])
                if s in (3, 5, 7):
                    pe_stats(pe, p + 1, s // 2 - 1)
            pe_stats(pe, p + 1, 3)

        def act_project(act, n, p):
            for s in range(8):
                if s < 6:
                    act_split(act, half0[n] + s + HALF_SLOTS)
                if s % 2:
                    act_squares(act, p + 1, s // 2)

        def dve_project(dve, n, p, scaled):
            if scaled:
                dve.wait_ge(x_scaled, scaled)
            for s in range(8):
                dve.wait_ge(half_done, half0[n] + s + 1)
                dve.tensor_tensor(xT[:, s, :], xT[:, s, :], ps[:, project_bank(n, s), 0:T], ALU.add).then_inc(x_ready, 1)
                if s % 2:
                    dve_sums(dve, p + 1, s // 2)
                if s < 6:
                    dve_split(dve, half0[n] + s + HALF_SLOTS)

        def ffn_index(n):
            return (2, 3, 6, 7, 10).index(n)

        def pe_open_outputs(pe):
            for b in range(4):
                pe.matmul(ps[:, 4 + b, :], zeros[:, 0:P], zeros[:, :], start=True, stop=False, skip_group_check=True)

        def pe_keep_clock(pe):
            for _ in range(KEEP):
                pe.matmul(ps[:, 7, :], zeros[:, 0:P], zeros[:, :], start=True, stop=True)

        def pe_ffn(pe, n, p):
            f = ffn_index(n)
            if f == 0:
                pe.wait_ge(zeros_ready, 1)
            if PRE[p][0] == "none":
                pe.wait_ge(x_ready, x_count(p))
            else:
                pe_keep_clock(pe)
            pe_open_outputs(pe)

            def down(h, x, c):
                cols = slice(c * P, (c + 1) * P)
                return three_pass(pe, ps[:, 4 + c // 2, (c % 2) * T:(c % 2 + 1) * T],
                                  whi[:, h % HALF_SLOTS, cols], wlo[:, h % HALF_SLOTS, cols],
                                  ghi[:, x, :], glo[:, x, :], False, False)

            with pe.Fori(0, FFN_STEPS - 1) as j:
                for s in range(6):
                    h = half0[n] + s
                    m, x = FFN_STEP[s]
                    first = 1 if n == 2 else 2
                    if 0 < s < first:
                        continue
                    pe.wait_ge(lo_ready, j * 6 + (h + (first if s == 0 else 1)))
                    if s == 0:
                        pe_halves_channels(pe, h, [ps[:, i, 0:T] for i in range(first)],
                                           lambda k: wait_activations(pe, p, k))
                        continue
                    if m < 2:
                        pe_halves_channels(pe, h, [ps[:, 2 * x + m, 0:T]])
                        continue
                    pe.wait_ge(g_ready, j * 2 + (2 * FFN_STEPS * f + x + 1))
                    for c in range(KC):
                        last = down(h, x, c)
                    last.then_inc(half_done, 1)
            h = half0[n + 1] - 6
            for s in range(4):
                m, x = FFN_STEP[s]
                pe_half_channels(pe, h + s, ps[:, 2 * x + m, 0:T])
            pe.wait_ge(lo_ready, h + 6)
            pe.wait_ge(g_ready, 2 * FFN_STEPS * (f + 1))
            for i in range(4):
                for c in (2 * i, 2 * i + 1):
                    for x in range(2):
                        last = down(h + 4 + x, x, c)
                if i < 3:
                    last.then_inc(y_ready, 1)
                else:
                    last.then_inc(half_done, 2)
                if i >= 1:
                    pe_stats(pe, p + 1, i - 1)
            pe_stats(pe, p + 1, 3)

        def act_ffn(act, n, p):
            f = ffn_index(n)

            def step(j, splits):
                for s in range(6):
                    m, x = FFN_STEP[s]
                    if m < 2 and n == 2:
                        act.wait_ge(half_done, j * 6 + (half0[n] + s + 1))
                        conv = (conv_g, conv_u)[m]
                        tap = par[:, bass.ds(j * 2 + (FCONV + 88 + 22 * m + x), 1)]
                        act.activation(conv[:, x, :], ps[:, 2 * x + m, 0:T], ACT.Copy,
                                       scale=tap).then_inc(conv0_ready, 1)
                        if m == 1:
                            act.wait_ge(convg_ready, j * 2 + (x + 1))
                            act.activation(gate_act[:, x, :], conv_g[:, x, :], ACT.Silu).then_inc(silu_ready, 1)
                    elif m == 0:
                        act.wait_ge(half_done, j * 6 + (half0[n] + s + 1))
                        act.activation(gate_act[:, x, :], ps[:, 2 * x, 0:T], ACT.Silu).then_inc(silu_ready, 1)
                    splits(j, s)

            act_table(act, ACT.Silu)
            with act.Fori(0, FFN_STEPS - 1) as j:
                step(j, lambda j, s: act_split_next(act, n, j, s))
            step(FFN_STEPS - 1, lambda j, s: act_split(act, half0[n + 1] + s) if s < 4 else None)
            for i in range(4):
                act_squares(act, p + 1, i)

        def dve_ffn(dve, n, p, scaled):
            f = ffn_index(n)
            links = 5 if n == 2 else 2

            def step(j, splits):
                done = 0

                def chain(ins):
                    nonlocal done
                    done += 1
                    before = 0 if f == 0 else 2 * FFN_STEPS * (5 + 2 * (f - 1))
                    ins.then_inc(ffn_chain, 1)
                    dve.wait_ge(ffn_chain, j * (2 * links) + (before + done))

                for s in range(6):
                    m, x = FFN_STEP[s]
                    if m < 2 and n == 2:
                        conv = (conv_g, conv_u)[m]
                        dve.wait_ge(conv0_ready, j * 4 + (2 * x + m + 1))
                        for back in (1, 2):
                            tap = par[:, bass.ds(j * 2 + (FCONV + 44 * (2 - back) + 22 * m + x), 1)]
                            ins = dve.scalar_tensor_tensor(conv[:, x, back:T], ps[:, 2 * x + m, 0:T - back], tap,
                                                           conv[:, x, back:T], ALU.mult, ALU.add)
                            if m == 0 and back == 2:
                                ins.then_inc(convg_ready, 1)
                            else:
                                chain(ins)
                    if m == 1:
                        dve.wait_ge(half_done, j * 6 + (half0[n] + s + 1))
                        dve.wait_ge(silu_ready, j * 2 + (2 * FFN_STEPS * f + x + 1))
                        up = conv_u[:, x, :] if n == 2 else ps[:, 2 * x + 1, 0:T]
                        chain(dve.tensor_tensor(gated[:, x, :], gate_act[:, x, :], up, ALU.mult))
                        chain(dve.tensor_copy(ghi[:, x, :], gated[:, x, :]))
                        dve.tensor_tensor(glo[:, x, :], gated[:, x, :], ghi[:, x, :].bitcast(F32),
                                          ALU.subtract).then_inc(g_ready, 1)
                    if n == 2 and s == 2:
                        continue
                    if n == 2 and s == 3:
                        splits(j, 2)
                    splits(j, s)

            with dve.Fori(0, FFN_STEPS - 1) as j:
                step(j, lambda j, s: dve_split_next(dve, n, j, s))
            step(FFN_STEPS - 1, lambda j, s: dve_split(dve, half0[n + 1] + s) if s < 4 else None)
            if scaled:
                dve.wait_ge(x_scaled, scaled)
            for i in range(4):
                if i < 3:
                    dve.wait_ge(y_ready, 3 * f + i + 1)
                else:
                    dve.wait_ge(half_done, half0[n + 1])
                cs = slice(2 * i, 2 * i + 2)
                dve.scalar_tensor_tensor(xT[:, cs, :], bank2(4 + i), 0.5 if scaled else 1.0, xT[:, cs, :],
                                         ALU.mult, ALU.add).then_inc(x_ready, 2)
                dve_sums(dve, p + 1, i)

        gates_done = sem("gates_done")
        gates_evac = sem("gates_evac")
        nsa_gates_done = sem("nsa_gates_done")
        rows_done = sem("rows_done")
        rows_evac = sem("rows_evac")
        rows_stored = sem("rows_stored")
        bias_landed = sem("bias_landed")
        bias_ready = sem("bias_ready")

        def pe_start(pe):
            pe.wait_ge(ident_landed, 16)
            pe.wait_ge(x_landed, 16)
            for b in range(4):
                for c in range(2):
                    for a in range(NT):
                        last = pe.transpose(ps[:, b, c * T + a * P:c * T + (a + 1) * P],
                                            x_tok[:, a, (2 * b + c) * P:(2 * b + c + 1) * P], ident)
                last.then_inc(x_turned, 1)

        def pe_params(pe):
            pe.wait_ge(rows_landed, 16 * (len(row_sources) - N_POOL_ROWS + 4))
            pe.wait_ge(pool_rows_landed, 16 * N_POOL_ROWS)
            for g in range(3):
                last = pe.transpose(ps[:, 6, g * P:g * P + n_rows[g]], rows[0:n_rows[g], g, :],
                                    ident[0:n_rows[g], 0:n_rows[g]])
            last.then_inc(par_turned, 1)

        def pe_bias_rows(pe):
            pe.wait_ge(small_landed, 16 * N_SMALL_DMAS)
            pe.matmul(ps[0:N_HEADS, 7, 0:BIAS_COLS], table, hot, start=True, stop=True).then_inc(rows_done, 1)

        def act_start(act):
            act.wait_ge(par_turned, 1)
            at = 0
            for g in range(3):
                last = act.activation(par[:, at:at + n_rows[g]], ps[:, 6, g * P:g * P + n_rows[g]], ACT.Copy)
                at += n_rows[g]
            link(act, act_chain, "act", last)
            act.activation(par[:, AQ:AQ + 1], par[:, AQ:AQ + 1], ACT.Copy, scale=QK_SCALE).then_inc(par_ready, 1)
            act.wait_ge(par_ready, 1)

        def act_bias_rows(act):
            act.wait_ge(rows_done, 1)
            act.activation(bias_row, ps[0:N_HEADS, 7, 0:BIAS_COLS], ACT.Copy).then_inc(rows_evac, 1)

        def dve_start(dve):
            dve.memset(zeros[:, :], 0.0).then_inc(zeros_ready, 1)
            for b in range(4):
                dve.wait_ge(x_turned, b + 1)
                dve.tensor_copy(xT[:, 2 * b:2 * b + 2, :], bank2(b)).then_inc(x_ready, 1)
            for b in range(4):
                dve_sums(dve, 0, b)

        scores_done = sem("scores_done")
        max_ready = sem("max_ready")
        exp_done = sem("exp_done")
        probT_done = sem("probT_done")
        rsum_ready = sem("rsum_ready")
        scaled_ready = sem("scaled_ready")
        probT_zeros = sem("probT_zeros")
        pe_zeros = {0: 2, A_HEADS: 4}
        probT_hi_ready = sem("probT_hi_ready")
        probT_ready = sem("probT_ready")
        heads_done = sem("heads_done")

        def pe_attention(pe, u0, n, q, k, v, dst, opens, buf, between={}):
            prob = buf[1]

            def product(dst, w, a, first=True, last=True):
                return three_pass(pe, dst, w[0], w[1], a[0], a[1], first, last)

            def scores(i):
                u = u0 + i
                if u >= 2:
                    pe.wait_ge(max_ready, u - 1)
                for t in range(NT):
                    last = product(ps[:, u % 2, t * T:(t + 1) * T], q(i, t), k(i))
                last.then_inc(scores_done, 1)

            def turn(i):
                u = u0 + i
                pe.wait_ge(scaled_ready, u + 1)
                if u >= 2:
                    pe.wait_ge(probT_ready, u - 1)
                for m, block in enumerate((2, 0, 1)):
                    last = pe.transpose(ps[:, 2 + u % 2, m * P:(m + 1) * P], prob[:, u % 3, block * P:(block + 1) * P],
                                        ident)
                last.then_inc(probT_done, 1)

            def values(i):
                u = u0 + i
                pe.wait_ge(probT_ready, u + 1)
                for t in range(NT):
                    blocks = [x[:, u % 2, (1 - t) * T:(2 - t) * T] for x in (probT_hi, probT_lo)]
                    last = product(dst(i), v(i, t), blocks, first=t == 0 and opens(i), last=t == 1)
                last.then_inc(heads_done, 1)

            for i in range(n + 3):
                if i < n:
                    scores(i)
                if i in between:
                    between[i](pe)
                if 2 <= i < n + 2:
                    turn(i - 2)
                if i == 2:
                    pe.wait_ge(probT_zeros, pe_zeros[u0])
                if i >= 3:
                    values(i - 3)

        def dve_attention(dve, u0, n, add, buf, between={}):
            score, _, nmax, sums, rsum, _ = buf
            for i in range(n + 2):
                u = u0 + i
                if i < n:
                    s = score[:, u % 2, :]
                    dve.wait_ge(scores_done, u + 1)
                    if u >= 2:
                        dve.wait_ge(exp_done, u - 1)
                    for t, dst, keys in ((0, slice(0, P), slice(P, 2 * P)), (1, slice(P, 3 * P), slice(0, 2 * P))):
                        src = ps[:, u % 2, t * T:t * T + (t + 1) * P]
                        last = dve.tensor_tensor_reduce(s[:, dst], src, add(i)[:, keys], -1.0, LARGE, ALU.add, ALU.min,
                                                        nmax[:, u % 2, t:t + 1])
                    last.then_inc(max_ready, 1)
                if 1 <= i <= n:
                    dve.wait_ge(exp_done, u)
                    dve.reciprocal(rsum[:, i - 1, :], sums[:, i - 1, :]).then_inc(rsum_ready, 1)
                if i >= 2:
                    dve.wait_ge(probT_hi_ready, u - 1)
                    slot = (u - 2) % 2
                    dve.tensor_tensor(probT_lo[:, slot, P:4 * P], ps[:, 2 + slot, 0:3 * P],
                                      probT_hi[:, slot, P:4 * P].bitcast(F32), ALU.subtract).then_inc(probT_ready, 1)
                if i in between:
                    between[i](dve)

        def act_attention(act, u0, n, buf, between={}):
            score, prob, nmax, sums, _, _ = buf
            for i in range(n + 2):
                u = u0 + i
                if i >= 2:
                    slot = (u - 2) % 2
                    act.wait_ge(probT_done, u - 1)
                    if u >= 4:
                        act.wait_ge(heads_done, u - 3)
                    act.activation(probT_hi[:, slot, P:4 * P], ps[:, 2 + slot, 0:3 * P], ACT.Copy).then_inc(probT_hi_ready, 1)
                if i < n:
                    act.wait_ge(max_ready, u + 1)
                    if u >= 3:
                        act.wait_ge(probT_done, u - 2)
                    for t, cols in ((0, slice(0, P)), (1, slice(P, 3 * P))):
                        last = act.activation(prob[:, u % 3, cols], score[:, u % 2, cols], ACT.Exp, scale=-1.0,
                                              bias=nmax[:, u % 2, t:t + 1], accum_out=sums[:, i, t:t + 1])
                    last.then_inc(exp_done, 1)
                if i in between:
                    between[i](act)

        def pool_zeros(pool, stage):
            pool.wait_ge(half_done, half0[stage + 1])
            for x in (probT_hi, probT_lo):
                pool.memset(x[:, :, 0:P].bitcast(F32), 0.0).then_inc(probT_zeros, 1)

        def pool_attention(pool, u0, n, gate, buf, between={}):
            _, prob, _, _, rsum, coef = buf
            for i in range(n):
                u = u0 + i
                pool.wait_ge(rsum_ready, u + 1)
                co = rsum[:, i, :]
                if gate is not None:
                    co = coef[:, i, :]
                    link(pool, pool_chain, "pool", pool.tensor_tensor(co, rsum[:, i, :], gate(i), ALU.mult))
                for t, cols in ((0, slice(0, P)), (1, slice(P, 3 * P))):
                    p = prob[:, u % 3, cols]
                    last = pool.tensor_tensor(p, p, co[:, t:t + 1].to_broadcast([P, (t + 1) * P]), ALU.mult)
                last.then_inc(scaled_ready, 1)
                if i in between:
                    between[i](pool)

        a_bufs = (att_score, att_prob, att_nmax, a_sums, a_rsum, None)
        EV_A, EV_N, EV_H = 0, 22, 42
        token_tile = sem("token_tile")
        TT_A, TT_N, TT_H = 0, 8, 10
        pads_ready = sem("pads_ready")
        ones_ready = sem("ones_ready")
        gates_turned = sem("gates_turned")
        fabs_ready = sem("fabs_ready")
        softplus_ready = sem("softplus_ready")
        mt_ready = sem("mt_ready")
        emt_ready = sem("emt_ready")
        ucols_turned = sem("ucols_turned")
        ucols_read = sem("ucols_read")
        mcum_spread = sem("mcum_spread")
        decay_arg = sem("decay_arg")
        decay_ready = sem("decay_ready")
        qk_sq = sem("qk_sq")
        qk_var = sem("qk_var")
        qk_std = sem("qk_std")
        qk_normed = sem("qk_normed")
        qk_turned = sem("qk_turned")
        qk_hi_ready = sem("qk_hi_ready")
        qk_ready = sem("qk_ready")
        av_hi_ready = sem("av_hi_ready")
        conv_ready = sem("conv_ready")
        mqk_ready = sem("mqk_ready")
        mqk_done = sem("mqk_done")
        mw_ready = sem("mw_ready")
        num_done = sem("num_done")
        hc_ready = sem("hc_ready")
        hsq_ready = sem("hsq_ready")
        hvar_ready = sem("hvar_ready")
        hstd_ready = sem("hstd_ready")
        hm_ready = sem("hm_ready")
        pool_ready = sem("pool_ready")
        pool_done = sem("pool_done")
        po_ready = sem("po_ready")

        def pe_tile_tokens(pe, base, ev, o):
            pe.wait_ge(lo_ready, base + o + 2)
            for a in range(NT):
                if o + a >= 4:
                    pe.wait_ge(evac_done, ev + o + a - 3)
                last, = pe_slab_tokens(pe, base + o, [a], [ps[:, (o + a) % 4, 0:T]])
                if a == 0:
                    last.then_inc(token_tile, 1)
                else:
                    last.then_inc(half_done, 2)

        def pe_tile_channels(pe, base, ev, o):
            if o >= 4:
                pe.wait_ge(evac_done, ev + o - 3)
            pe_half_channels(pe, base + o, ps[:, o % 4, 0:T])

        def pe_first_tiles(pe, base, n, norm):
            pe_keep_clock(pe)
            pe.wait_ge(lo_ready, base + n)
            pe_halves_channels(pe, base, [ps[:, i, 0:T] for i in range(n)],
                               lambda k: wait_activations(pe, norm, k))

        def pe_first(pe):
            for o in range(0, 22, 2):
                if o == 2:
                    pe_bias_rows(pe)
                    for a in range(NT):
                        for k in range(KC):
                            last = pe.matmul(ps[:, 6, a * 8:(a + 1) * 8], xc[:, k, a * P:(a + 1) * P], gate_w[:, k, :],
                                             start=k == 0, stop=k == KC - 1)
                    last.then_inc(gates_done, 1)
                if o == 4:
                    pe.wait_ge(gates_evac, 1)
                    for m in range(2):
                        for a in range(NT):
                            last = pe.transpose(ps[0:M_HEADS, 7, m * T + a * P:m * T + (a + 1) * P],
                                                gates[:, a, 4 * m:4 * m + 4], ident)
                    last.then_inc(gates_turned, 1)
                if o == 12:
                    pe.wait_ge(mt_ready, 1)
                    pe.wait_ge(emt_ready, 1)
                    for m, row in enumerate((u_g, e_mt)):
                        for a in range(NT):
                            last = pe.transpose(ps[:, 6, 8 * m + 4 * a:8 * m + 4 * a + 4], row[:, a * P:(a + 1) * P],
                                                ident[0:M_HEADS, 0:M_HEADS])
                    last.then_inc(ucols_turned, 1)
                if o == 14:
                    pe.wait_ge(ucols_read, 1)
                    for h in range(M_HEADS):
                        last = pe.matmul(ps[:, 7 - h // 2, (h % 2) * T:(h % 2 + 1) * T],
                                         ident[0:M_HEADS, h:h + 1].to_broadcast([M_HEADS, P]), m_cum,
                                         start=True, stop=True)
                    last.then_inc(mcum_spread, 1)
                if o in (16, 18):
                    m = (o - 16) // 2
                    pe.wait_ge(qk_normed, 1)
                    if m:
                        pe.wait_ge(decay_arg, 1)
                    for c in range(4):
                        for a in range(NT):
                            last = pe.transpose(ps[:, 4 + 2 * m + c // 2, (c % 2) * T + a * P:(c % 2) * T + (a + 1) * P],
                                                z_qk[:, a, (4 * m + c) * P:(4 * m + c + 1) * P], ident)
                    last.then_inc(qk_turned, 1)
                if o == 0:
                    pe.wait_ge(zeros_ready, 1)
                    pe_keep_clock(pe)
                    pe.wait_ge(lo_ready, half0[0] + 2)
                    first, last = pe_slab_tokens(pe, half0[0], range(NT), [ps[:, a, 0:T] for a in range(NT)],
                                                 lambda k: wait_activations(pe, 0, k))
                    first.then_inc(token_tile, 1)
                    last.then_inc(half_done, 2)
                elif 8 <= o < 12 or o == 16:
                    pe_tile_channels(pe, half0[0], EV_A, o)
                    pe_tile_channels(pe, half0[0], EV_A, o + 1)
                else:
                    pe_tile_tokens(pe, half0[0], EV_A, o)
            pe.wait_ge(evac_done, EV_A + 22)
            pe.wait_ge(mqk_ready, 1)
            for h in range(M_HEADS):
                lo = DH * (h % 2)
                q, k = conv_out[lo:lo + DH, h // 2, :], conv_out[lo:lo + DH, 2 + h // 2, :]
                pe.matmul(ps[:, h, 0:T], k[:, 0:P], q, start=True, stop=True)
                pe.matmul(ps[:, h, T:T + P], k[:, P:T], q[:, P:T], start=True, stop=True).then_inc(mqk_done, 1)
            pe.wait_ge(pool_ready, 1)
            pe.wait_ge(qk_ready, 2)
            for c in range(2):
                last = pe.matmul(ps[:, 4, c * T:(c + 1) * T], pool_w[:, c, :], p_d[:, c, :], start=True, stop=True)
            last.then_inc(pool_done, 1)

            def numerators(pe):
                pe.wait_ge(ones_ready, 1)
                pe.wait_ge(decay_arg, 1)
                for h in range(M_HEADS):
                    pe.wait_ge(mw_ready, h + 1)
                    col = slice(h * (DH + 1), (h + 1) * (DH + 1))
                    pe.matmul(ps[:, 6, col], decay[:, h, 0:P], m_v[:, 0, h, :], start=True, stop=True)
                    pe.matmul(ps[:, 7, col], decay[:, h, P:T], m_v[:, 0, h, :], start=True, stop=False)
                    last = pe.matmul(ps[:, 7, col], decay[:, h, T:T + P], m_v[:, 1, h, :], start=False, stop=True)
                last.then_inc(num_done, 1)

            def outputs_free(pe):
                pe.wait_ge(po_ready, 1)

            def head_rows(i):
                return slice(DH * (i % 2), DH * (i % 2) + DH)

            pe.wait_ge(mw_ready, M_HEADS)
            pe_attention(pe, 0, A_HEADS,
                         lambda i, t: [x[head_rows(i), i // 2, t * P:(t + 1) * P] for x in (qk_hi, qk_lo)],
                         lambda i: [x[head_rows(i), 4 + i // 2, :] for x in (qk_hi, qk_lo)],
                         lambda i, t: [x[:, t, i // 2, DH * (i % 2):DH * (i % 2) + 2 * DH] for x in (av_hi, av_lo)],
                         lambda i: bank2(4 + i // 4)[:, i // 2 % 2, :], lambda i: i % 2 == 0, a_bufs,
                         {1: numerators, 2: outputs_free})
            pe.wait_ge(hm_ready, 1)
            for c in range(2):
                for a in range(NT):
                    last = pe.transpose(ps[:, 6, c * T + a * P:c * T + (a + 1) * P], h_out[:, a, c * P:(c + 1) * P], ident)
            last.then_inc(mix_turned, 1)

        def act_mix(act, count, src, cs, turned):
            act.wait_ge(mix_turned, turned)
            act.activation(ahi[:, cs:cs + 2, :], src, ACT.Copy).then_inc(mix_hi, 1)

        def dve_mix(dve, count, src, cs):
            dve.wait_ge(mix_hi, count)
            dve.tensor_tensor(alo[:, cs:cs + 2, :], src, ahi[:, cs:cs + 2, :].bitcast(F32), ALU.subtract).then_inc(mix_lo, 1)

        def head_cols(v, o):
            n = 2 * (o // 2 - 6)
            return v[:, o % 2, n:n + 2, :].rearrange("p n (b d) -> p n b d", d=DH)[:, :, 0:3:2, :]

        def act_first(act):
            for o in range(22):
                slab, x = o // 2, o % 2
                channels = slab in (4, 5, 8)
                src = ps[:, o % 4, 0:T]
                if channels or x == 1:
                    act.wait_ge(half_done, half0[0] + o + 1)
                else:
                    act.wait_ge(token_tile, TT_A + {0: 1, 1: 2, 2: 3, 3: 4, 6: 5, 7: 6, 9: 7, 10: 8}[slab])
                if slab < 4:
                    act.activation(z_qk[:, x, 256 * slab:256 * slab + 256], src, ACT.Copy).then_inc(evac_done, 1)
                elif slab < 6:
                    if o == 8:
                        act.wait_ge(pads_ready, 2)
                    act.activation(conv_in[:, o - 8, 3:3 + T], src, ACT.Copy).then_inc(evac_done, 1)
                elif slab < 8:
                    act.activation(head_cols(av_hi, o), src.rearrange("p (n b d) -> p n b d", n=2, b=2),
                                   ACT.Copy).then_inc(av_hi_ready, 1)
                elif slab == 8:
                    if x == 0:
                        act.wait_ge(evac_done, EV_A + 16)
                        act.wait_ge(pads_ready, 3)
                    act.activation(p_in[:, x, PAD:PAD + T], src, ACT.Copy).then_inc(evac_done, 1)
                elif slab == 9:
                    act.activation(m_v[:, x, :, 0:DH], src.rearrange("p (h d) -> p h d", h=M_HEADS),
                                   ACT.Copy).then_inc(evac_done, 1)
                else:
                    act.activation(m_o[:, x, :], src, ACT.Sigmoid).then_inc(evac_done, 1)
                act_split(act, half0[0] + o + HALF_SLOTS)
                if o == 2:
                    act_bias_rows(act)
                    act.wait_ge(gates_done, 1)
                    act.activation(gates[:, :, :], ps[:, 6, 0:16].rearrange("p (a b) -> p a b", a=NT),
                                   ACT.Copy).then_inc(gates_evac, 1)
                if o == 6:
                    act.wait_ge(fabs_ready, 1)
                    link(act, act_chain, "act", act.activation(f_abs, f_abs, ACT.Exp, scale=-1.0))
                    act.activation(f_abs, f_abs, ACT.Ln, bias=1.0).then_inc(softplus_ready, 1)
                if o == 8:
                    act.wait_ge(mt_ready, 1)
                    act.activation(e_mt, m_t, ACT.Exp, scale=-1.0).then_inc(emt_ready, 1)
                if o in (17, 19):
                    m = (o - 17) // 2
                    act.wait_ge(qk_turned, m + 1)
                    act.activation(qk_hi[:, 4 * m:4 * m + 4, :], ps[:, 4 + 2 * m:6 + 2 * m, :].rearrange("p a (b c) -> p (a b) c", b=2),
                                   ACT.Copy, scale=par[:, AQ + m:AQ + m + 1]).then_inc(qk_hi_ready, 1)
                if o == 16:
                    act.wait_ge(conv_ready, 1)
                    act.activation(conv_out, conv_out, ACT.Silu).then_inc(mqk_ready, 1)
            act.wait_ge(decay_arg, 1)
            act.activation(decay, decay, ACT.Exp, scale=-1.0).then_inc(decay_ready, 1)
            act.wait_ge(pool_done, 1)
            for c in range(2):
                last = act.activation(p_d[:, c, :], ps[:, 4, c * T:(c + 1) * T], ACT.Copy,
                                      scale=par[:, PSCALE + c:PSCALE + c + 1])
            last.then_inc(po_ready, 1)
            act.wait_ge(po_ready, 1)
            act.activation(ahi[:, 0:2, :], p_d, ACT.Copy).then_inc(mix_hi, 1)

            def head_squares(act):
                act.wait_ge(hc_ready, 1)
                act.activation(h_sq, h_out, ACT.Square).then_inc(hsq_ready, 1)

            act_attention(act, 0, A_HEADS, a_bufs, {4: head_squares})
            act.wait_ge(heads_done, A_HEADS)
            for b in range(2):
                act.activation(ahi[:, 4 + 2 * b:6 + 2 * b, :], bank2(4 + b), ACT.Copy).then_inc(mix_hi, 1)
            act_mix(act, 4, bank2(6), 2, 1)

        def dve_first(dve):
            def chain(ins):
                link(dve, dve_chain, "dve", ins)

            for o in range(22):
                if 12 <= o < 16:
                    dve.wait_ge(av_hi_ready, o - 11)
                    dve.tensor_tensor(head_cols(av_lo, o), ps[:, o % 4, 0:T].rearrange("p (n b d) -> p n b d", n=2, b=2),
                                      head_cols(av_hi, o).bitcast(F32), ALU.subtract).then_inc(evac_done, 1)
                dve_split(dve, half0[0] + o + HALF_SLOTS)
                if o in (17, 19):
                    m = (o - 17) // 2
                    dve.wait_ge(qk_hi_ready, m + 1)
                    dve.scalar_tensor_tensor(qk_lo[:, 4 * m:4 * m + 4, :],
                                             ps[:, 4 + 2 * m:6 + 2 * m, :].rearrange("p a (b c) -> p (a b) c", b=2),
                                             par[:, AQ + m:AQ + m + 1], qk_hi[:, 4 * m:4 * m + 4, :].bitcast(F32),
                                             ALU.mult, ALU.subtract).then_inc(qk_ready, 1)
                if o == 4:
                    dve.wait_ge(const_landed, 16)
                    dve.wait_ge(small_landed, 16 * N_SMALL_DMAS)
                    dve.wait_ge(gates_turned, 1)
                    dve.tensor_scalar(i_g, ps[0:M_HEADS, 7, 0:T], gate_bias[:, 0:1], None, ALU.add)
                    chain(dve.tensor_scalar(f_g, ps[0:M_HEADS, 7, T:2 * T], gate_bias[:, 1:2], None, ALU.add))
                    dve.scalar_tensor_tensor(f_abs, f_g, -1.0, f_g, ALU.mult, ALU.max).then_inc(fabs_ready, 1)
                if o == 6:
                    dve.wait_ge(softplus_ready, 1)
                    chain(dve.scalar_tensor_tensor(f_log, f_g, 0.0, f_abs, ALU.min, ALU.subtract))
                    chain(dve.tensor_tensor_scan(g_cum, const("ones", M_HEADS), f_log, 0.0, ALU.mult, ALU.add))
                    chain(dve.tensor_tensor(u_g, i_g, g_cum, ALU.subtract))
                    chain(dve.tensor_tensor_scan(m_cum, const("ones", M_HEADS), u_g, 0.0, ALU.mult, ALU.max))
                    dve.tensor_tensor(m_t, g_cum, m_cum, ALU.add).then_inc(mt_ready, 1)
                if o == 11:
                    dve.wait_ge(rows_stored, 16)
                    dve.wait_ge(ucols_turned, 1)
                    dve.tensor_copy(ucols, ps[:, 6, 0:16]).then_inc(ucols_read, 1)
                if o == 8:
                    dve.wait_ge(qk_sq, 1)
                    chain(dve.tensor_reduce(ss, sq[:, :, :].rearrange("p a b -> p (a b)").rearrange("p (g d) -> p g d", d=DH),
                                            AX, ALU.add))
                    dve.tensor_scalar(ss, ss, 1.0 / DH, RMS_EPS, ALU.mult, ALU.add).then_inc(qk_var, 1)
                if o == 12:
                    dve.wait_ge(qk_std, 1)
                    z = z_qk.rearrange("p a (g d) -> p (a g) d", d=DH)
                    dve.tensor_tensor(z, z, bc(rr, 2, DH), ALU.mult).then_inc(qk_normed, 1)
                if o == 14:
                    dve.wait_ge(mcum_spread, 1)
                    dve.wait_ge(ucols_read, 1)
                    for h in range(M_HEADS):
                        m = ps[:, 7 - h // 2, (h % 2) * T:(h % 2 + 1) * T]
                        dve.scalar_tensor_tensor(decay[:, h, 0:T], m, ucols[:, h:h + 1], const("late"),
                                                 ALU.subtract, ALU.max)
                        last = dve.scalar_tensor_tensor(decay[:, h, T:T + P], m[:, P:T], ucols[:, 4 + h:5 + h],
                                                        const("late")[:, 0:P], ALU.subtract, ALU.max)
                    last.then_inc(decay_arg, 1)
                if o == 15:
                    dve.wait_ge(pads_ready, 2)
                    dve.wait_ge(evac_done, EV_A + 12)
                    for j in range(4):
                        for c in range(4):
                            x = conv_in[:, c, j:j + T]
                            tap = par[:, MCONV + 4 * j + c:MCONV + 4 * j + c + 1]
                            if j == 0:
                                last = dve.tensor_scalar(conv_out[:, c, :], x, tap, None, ALU.mult)
                            else:
                                last = dve.scalar_tensor_tensor(conv_out[:, c, :], x, tap, conv_out[:, c, :],
                                                                ALU.mult, ALU.add)
                        if j < 3:
                            chain(last)
                    last.then_inc(conv_ready, 1)
            dve.wait_ge(decay_ready, 1)
            for h in range(M_HEADS):
                dve.wait_ge(mqk_done, h + 1)
                dve.scalar_tensor_tensor(decay[:, h, :], ps[:, h, 0:384], QK_SCALE, decay[:, h, :],
                                         ALU.mult, ALU.mult).then_inc(mw_ready, 1)
            dve.wait_ge(evac_done, EV_A + 22)
            chain(dve.tensor_tensor(m_o, m_o, bc(mng, 1, NT), ALU.mult))
            num = [ps[:, 6 + a, 0:M_HEADS * (DH + 1)].rearrange("p (h e) -> p h e", h=M_HEADS) for a in range(NT)]

            def normalise(dve):
                dve.wait_ge(num_done, 1)
                least = ucols[:, 8:16].rearrange("p (a h) -> p a h", a=NT)
                for a in range(NT):
                    last = dve.scalar_tensor_tensor(den[:, a, :], num[a][:, :, DH], -1.0, least[:, a, :], ALU.mult, ALU.max)
                chain(last)
                for a in range(NT):
                    last = dve.tensor_tensor(den[:, a, :], num[a][:, :, DH], den[:, a, :], ALU.max)
                chain(last)
                chain(dve.reciprocal(den, den))
                for a in range(NT):
                    last = dve.tensor_tensor(h_out[:, a, :].rearrange("p (h d) -> p h d", d=DH), num[a][:, :, 0:DH],
                                             bc(den[:, a, :], 2, DH), ALU.mult)
                last.then_inc(hc_ready, 1)

            def variance(dve):
                dve.wait_ge(hsq_ready, 1)
                chain(dve.tensor_reduce(m_ss, h_sq.rearrange("p a (h d) -> p (a h) d", d=DH), AX, ALU.add))
                dve.tensor_scalar(m_ss, m_ss, 1.0 / DH, RMS_EPS, ALU.mult, ALU.add).then_inc(hvar_ready, 1)

            def scale_heads(dve):
                dve.wait_ge(hc_ready, 1)
                chain(dve.tensor_tensor(h_out, h_out, m_o, ALU.mult))
                dve.wait_ge(hstd_ready, 1)
                hh = h_out.rearrange("p a (h d) -> p (a h) d", d=DH)
                dve.tensor_tensor(hh, hh, bc(m_rr, 2, DH), ALU.mult).then_inc(hm_ready, 1)

            dve_attention(dve, 0, A_HEADS, lambda i: const("causal"), a_bufs,
                          {2: normalise, 4: variance, 6: scale_heads})
            dve_mix(dve, 1, p_d, 0)
            dve_mix(dve, 2, bank2(4), 4)
            dve_mix(dve, 3, bank2(5), 6)
            dve_mix(dve, 4, bank2(6), 2)

        def pool_first(pool):
            def chain(ins):
                link(pool, pool_chain, "pool", ins)

            pool.wait_ge(gates_done, 1)
            wait_activations(pool, 0)
            pool.memset(conv_in[:, :, 0:3], 0.0).then_inc(pads_ready, 1)
            pool.wait_ge(evac_done, EV_A + 8)
            z = z_qk.rearrange("p a b -> p (a b)")
            pool.tensor_tensor(sq[:, :, :].rearrange("p a b -> p (a b)"), z, z, ALU.mult).then_inc(qk_sq, 1)
            pool.wait_ge(const_landed, 16)
            pool.wait_ge(qk_var, 1)
            pool.tensor_tensor(rr, ss, const("minus_half").to_broadcast([P, 2 * NT * A_HEADS]), ALU.pow).then_inc(qk_std, 1)
            pool.memset(p_in[:, :, 0:PAD], 0.0).then_inc(pads_ready, 1)
            pool.wait_ge(pads_ready, 3)
            pool.wait_ge(evac_done, EV_A + 18)
            n = PAD + T
            chain(pool.tensor_tensor(p_2[:, :, 1:n], p_in[:, :, 1:n], p_in[:, :, 0:n - 1], ALU.add))
            chain(pool.tensor_tensor(p_4[:, :, 3:n], p_2[:, :, 3:n], p_2[:, :, 1:n - 2], ALU.add))
            chain(pool.tensor_tensor(p_8[:, 0, 7:n], p_4[:, 1, 7:n], p_4[:, 1, 3:n - 4], ALU.add))
            p_16 = p_2[64:128, 0, :]
            chain(pool.tensor_tensor(p_16[:, 15:n], p_8[64:128, 0, 15:n], p_8[64:128, 0, 7:n - 8], ALU.add))
            inv = const("inv_count").rearrange("p (a b) -> p a b", a=2)
            pool.tensor_tensor(p_d[0:64, 0, :], p_2[0:64, 0, PAD:n], inv[0:64, 0, :], ALU.mult)
            pool.tensor_tensor(p_d[64:128, 0, :], p_4[64:128, 0, PAD:n], inv[64:128, 0, :], ALU.mult)
            pool.tensor_tensor(p_d[0:64, 1, :], p_8[0:64, 0, PAD:n], inv[0:64, 1, :], ALU.mult)
            chain(pool.tensor_tensor(p_d[64:128, 1, :], p_16[:, PAD:n], inv[64:128, 1, :], ALU.mult))
            pool.tensor_tensor(p_d, p_d, p_in[:, :, PAD:n], ALU.subtract).then_inc(pool_ready, 1)
            pool_zeros(pool, 0)

            def head_rstd(pool):
                pool.wait_ge(hvar_ready, 1)
                pool.tensor_tensor(m_rr, m_ss, const("minus_half").to_broadcast([P, NT * M_HEADS]), ALU.pow).then_inc(hstd_ready, 1)

            pool_attention(pool, 0, A_HEADS, None, a_bufs, {4: head_rstd})

        def pe_finish(pe):
            for c in range(KC):
                pe.wait_ge(ahi_ready, KC * 8 + c + 1)
                for a in range(NT):
                    last = pe.transpose(ps[:, 4 + 2 * a + c // 4, (c % 4) * P:(c % 4 + 1) * P],
                                        xT[:, c, a * P:(a + 1) * P], ident)
                if c % 4 == 3:
                    last.then_inc(out_turned, 1)

        def act_finish(act):
            for b in range(2):
                act.wait_ge(out_turned, b + 1)
                act.activation(out_tok[:, 1, b * 512:(b + 1) * 512], ps[:, 6 + b, :], ACT.Copy).then_inc(out_odd_ready, 1)

        def dve_finish(dve):
            for b in range(2):
                dve.wait_ge(out_turned, b + 1)
                dve.tensor_copy(out_tok[:, 0, b * 512:(b + 1) * 512], ps[:, 4 + b, :]).then_inc(out_ready, 1)

        dup_landed = [sem(f"dup_landed{m}") for m in range(4)]
        w1_landed = sem("w1_landed")
        n_gates_raw = sem("n_gates_raw")
        n_gates_turned = sem("n_gates_turned")
        n_gates_ready = sem("n_gates_ready")
        hid_done = sem("hid_done")
        n_hi_ready = sem("n_hi_ready")
        n_zeros_ready = sem("n_zeros_ready")
        pos_ready = sem("pos_ready")
        hid_ready = sem("hid_ready")
        hid_spread = sem("hid_spread")
        kc_done = sem("kc_done")
        kc_hi_ready = sem("kc_hi_ready")
        kc_ready = sem("kc_ready")
        vc_done = sem("vc_done")
        vc_ready = sem("vc_ready")
        c_scores_done = sem("c_scores_done")
        c_scores_read = sem("c_scores_read")
        c_arg_ready = sem("c_arg_ready")
        c_exp_ready = sem("c_exp_ready")
        c_prob_ready = sem("c_prob_ready")
        c_turned = sem("c_turned")
        c_probT_ready = sem("c_probT_ready")
        n_bufs = (n_score, n_prob, n_nmax, n_sums, n_rsum, n_coef)
        k_sel = [[x[:, n, :] for n in range(2)] for x in (k_sel_hi, k_sel_lo)]
        k_win = [[k_win_hi[:, n, :] for n in range(2)], [x.rearrange("p a b -> p (a b)") for x in k_win_lo]]
        Q_TILE, KS_TILE = 4, 12

        def pool_load_nsa(pool):
            pool.wait_ge(x_ready, x_count(1))
            pool.wait_ge(rows_stored, 16)
            shifted = bass.AP(tensor=scratch.tensor, offset=scratch.offset, ap=[[1, P], [BIAS_COLS, N_HEADS], [1, T]])
            pool.dma_start(bias, shifted).then_inc(bias_landed, 16)
            pool.memset(kc_hi[:, :, :].bitcast(F32), 0.0)
            for v in (v_sel_hi, v_win_hi):
                pool.memset(v[:, :, :].bitcast(F32), 0.0)
            pool.memset(kc_lo[:, :, :].bitcast(F32), 0.0).then_inc(n_zeros_ready, 1)
            for z, dst in enumerate((z_k, z_v)):
                link(pool, pool_chain, "pool", pool.memset(dst[:, N_GROUPS, :], 0.0))
                pool.tensor_copy(dst[:, N_GROUPS, 1:1 + CMP_LEN:2],
                                 par[:, CPOS + 16 * z:CPOS + 16 * z + CMP_LEN // 2]).then_inc(pos_ready, 1)
            pool.wait_ge(bias_landed, 16)
            pool.tensor_tensor(bias[:, :, P:T], bias[:, :, P:T], bc(const("causal_rev"), 1, N_HEADS),
                               ALU.add).then_inc(bias_ready, 1)

        def pool_nsa(pool):
            pool_norm(pool, 3)
            wait_activations(pool, 3)
            pool.wait_ge(x_scaled, 2)
            for z, dst in enumerate((w1_k, w1_v)):
                pool.dma_start(dst, io["nsa_cmp_w1_2"][0, z].rearrange("l d e -> (l d) e").rearrange("(m p) e -> p m e", p=P)) \
                    .then_inc(w1_landed, 16)
            for z, dst in enumerate((z_k, z_v)):
                pool.wait_ge(evac_done, EV_N + 2 * z + 2)
                pool.dma_start(dst[64:128, 0:N_GROUPS:2, 0:T], dst[0:64, 0:N_GROUPS:2, 1:1 + T]).then_inc(dup_landed[z], 16)
                pool.dma_start(dst[0:64, 1:N_GROUPS:2, 1:1 + T], dst[64:128, 1:N_GROUPS:2, 0:T]).then_inc(dup_landed[z], 16)
            pool.wait_ge(hid_done, 2)
            for v in (v_sel_lo, v_win_lo):
                last = pool.memset(v[:, :, :].bitcast(F32), 0.0)
            last.then_inc(n_zeros_ready, 1)
            for b, keys in enumerate(((k_sel_hi[:, 0, :], k_sel_hi[:, 1, :]), (k_sel_lo[:, 0, :], k_sel_lo[:, 1, :]),
                                      (k_win_hi[:, 0, :], k_win_hi[:, 1, :]), [x.rearrange("p a b -> p (a b)") for x in k_win_lo])):
                if b % 2 == 0:
                    pool.wait_ge(evac_done, EV_N + KS_TILE + 2 * b + 2)
                pool.dma_start(keys[1][0:64, :], keys[0][64:128, :]).then_inc(dup_landed[2 + b // 2], 16)
                pool.dma_start(keys[1][64:128, :], keys[0][0:64, :]).then_inc(dup_landed[2 + b // 2], 16)
            pool_zeros(pool, 4)
            pool_attention(pool, A_HEADS, 2 * N_HEADS,
                           lambda i: n_gates[:, :, 3 * (i % N_HEADS) + i // N_HEADS + 1], n_bufs)

        def chunk_bank(c):
            return bank2(4 + c // 2)[:, c % 2, :]

        def pe_nsa(pe):
            for o in range(0, 20, 2):
                if o == 4:
                    pe.wait_ge(x_scaled, 2)
                    for a in range(NT):
                        for k in range(KC):
                            last = pe.matmul(ps[:, 4, a * 48:(a + 1) * 48], xT[:, k, a * P:(a + 1) * P],
                                             gate_w2[:, k, :], start=k == 0, stop=k == KC - 1)
                    last.then_inc(nsa_gates_done, 1)
                if o == 8:
                    pe.wait_ge(n_gates_raw, 1)
                    pe.matmul(ps[:, 5, 0:96], const("flip"), n_gates.rearrange("p a b -> p (a b)"), start=True,
                              stop=True).then_inc(n_gates_turned, 1)
                if o == 8:
                    pe.wait_ge(w1_landed, 32)
                    pe.wait_ge(pos_ready, 2)
                    for z, (src, w1) in enumerate(((z_k, w1_k), (z_v, w1_v))):
                        pe.wait_ge(dup_landed[z], 32)
                        for m in range(CMP_LEN // 2):
                            blocks = src[:, :, 1 + 2 * m:2 + 2 * m + CMP_STRIDE * (N_CMP - 1):CMP_STRIDE]
                            last = pe.matmul(ps[:, 6, z * P:z * P + 75].rearrange("p (g n) -> p g n", n=N_CMP),
                                             w1[:, m, :], blocks, start=m == 0, stop=m == CMP_LEN // 2 - 1)
                        last.then_inc(hid_done, 1)
                if o == 12:
                    pe.wait_ge(hid_ready, 2)
                    pe.matmul(ps[:, 7, 0:60], w2_k[:, :, :].rearrange("p a b -> p (a b)"), hidT[:, 0, :],
                              start=True, stop=True).then_inc(kc_done, 1)
                    pe.wait_ge(hid_spread, 1)
                    for half in range(2):
                        last = pe.matmul(ps[0:8 * N_CMP, 6, half * DH:(half + 1) * DH],
                                         hid_heads[:, half * 8:half * 8 + 8, :].rearrange("p a b -> p (a b)"),
                                         w2_v[:, :], start=True, stop=True)
                    last.then_inc(vc_done, 1)
                if o == 14:
                    pe.wait_ge(evac_done, EV_N + Q_TILE + KC)
                    pe.wait_ge(kc_ready, 2)
                    for a in range(NT):
                        for c in range(KC):
                            q, k = ([x[:, c, a * P:(a + 1) * P] for x in (q_hi, q_lo)],
                                    [x[:, c // 2, :] for x in (kc_hi, kc_lo)])
                            last = three_pass(pe, ps[:, 4, a * 240 + c * 30:a * 240 + (c + 1) * 30],
                                              q[0], q[1], k[0], k[1], True, True)
                    last.then_inc(c_scores_done, 1)
                if o == 0:
                    pe_first_tiles(pe, half0[4], 2, 3)
                elif o in (14, 18):
                    pe_tile_tokens(pe, half0[4], EV_N, o)
                else:
                    pe_tile_channels(pe, half0[4], EV_N, o)
                    pe_tile_channels(pe, half0[4], EV_N, o + 1)
            pe.wait_ge(evac_done, EV_N + 20)
            pe.wait_ge(dup_landed[2], 64)

            def queries(i, t):
                c = i // 2 % KC
                return [x[DH * (i % 2):DH * (i % 2) + DH, c, t * P:(t + 1) * P] for x in (q_hi, q_lo)]

            def head_keys(i):
                g, h = i % N_HEADS // 4, i % 2
                return [k[(g + h) % 2][DH * h:DH * h + DH, g // 2 * T:(g // 2 + 1) * T]
                        for k in (k_sel, k_win)[i // N_HEADS]]

            def head_values(i, t):
                at = 2 * DH * (i % N_HEADS // 4) + DH * (1 - i % 2)
                return [v[:, t, at:at + 2 * DH] for v in ((v_sel_hi, v_sel_lo), (v_win_hi, v_win_lo))[i // N_HEADS]]

            def turn_compressed(pe):
                pe.wait_ge(c_prob_ready, 1)
                for a in range(NT):
                    for half in range(2):
                        last = pe.transpose(ps[0:8 * N_CMP, 5, (2 * half + a) * P:(2 * half + a + 1) * P],
                                            c_score[:, a, half * 120:(half + 1) * 120], ident)
                last.then_inc(c_turned, 1)

            def compressed(pe):
                pe.wait_ge(c_probT_ready, 1)
                pe.wait_ge(vc_ready, 1)
                pe.wait_ge(c_scores_read, 1)
                pe_open_outputs(pe)
                for c in range(KC):
                    pe.matmul(chunk_bank(c), c_val[0:8 * N_CMP, c // 4, (c % 4) * P:(c % 4 + 1) * P],
                              c_probT[0:8 * N_CMP, c // 4, :], start=False, stop=False, skip_group_check=True)

            def window_keys(pe):
                pe.wait_ge(dup_landed[3], 64)

            pe_attention(pe, A_HEADS, 2 * N_HEADS, queries, head_keys, head_values, lambda i: chunk_bank(i // 2 % KC),
                         lambda i: False, n_bufs, {0: turn_compressed, 1: compressed, N_HEADS - 1: window_keys})

        def pe_turn_mix(pe):
            for a in range(NT):
                pe.wait_ge(r_o_ready, a + 1)
                for c in range(KC):
                    dst = ps[:, c // 2, (c % 2) * T + a * P:(c % 2) * T + (a + 1) * P]
                    last = pe.transpose(dst, r_o[:, a, c * P:(c + 1) * P], ident)
                    if a == NT - 1 and c % 2:
                        last.then_inc(mix_turned, 1)

        def turned(b, reverse):
            if not reverse:
                return bank2(b)
            return ps[:, 4 + b, :].rearrange("p (c a n) -> p c a n", c=2, a=NT)[:, :, :, ::-1]

        def by_tile(v, reverse):
            return v.rearrange("p c (a n) -> p c a n", a=NT) if reverse else v

        def act_mix_all(act, before, reverse=False):
            for b in range(4):
                if reverse:
                    act.wait_ge(heads_done, A_HEADS + 2 * N_HEADS)
                else:
                    act.wait_ge(mix_turned, before + b + 1)
                act.activation(by_tile(ahi[:, 2 * b:2 * b + 2, :], reverse), turned(b, reverse), ACT.Copy).then_inc(mix_hi, 1)

        def dve_mix_all(dve, before, reverse=False):
            for b in range(4):
                cs = slice(2 * b, 2 * b + 2)
                dve.wait_ge(mix_hi, before + b + 1)
                dve.tensor_tensor(by_tile(alo[:, cs, :], reverse), turned(b, reverse),
                                  by_tile(ahi[:, cs, :].bitcast(F32), reverse), ALU.subtract).then_inc(mix_lo, 1)

        def group_cols(v):
            return v[:, DH:].rearrange("p (g b d) -> p g b d", b=2, d=DH)[:, :, 0, :]

        def act_nsa(act):
            for o in range(20):
                slab, x = o // 2, o % 2
                src = ps[:, o % 4, 0:T]
                if slab in (7, 9) and x == 0:
                    act.wait_ge(token_tile, TT_N + (slab - 5) // 2)
                else:
                    act.wait_ge(half_done, half0[4] + o + 1)
                if slab < 2:
                    dst = (z_k, z_v)[slab]
                    act.activation(dst[0:64, 2 * x, 1:1 + T], src[0:64, :], ACT.Copy)
                    act.activation(dst[64:128, 2 * x + 1, 0:T], src[64:128, :], ACT.Copy).then_inc(evac_done, 1)
                elif slab < 6:
                    act.activation(q_hi[:, o - 4, :].rearrange("p (a n) -> p a n", a=NT),
                                   src.rearrange("p (a n) -> p a n", a=NT)[:, :, ::-1], ACT.Copy,
                                   scale=QK_SCALE).then_inc(n_hi_ready, 1)
                elif slab in (7, 9):
                    act.wait_ge(n_zeros_ready, 2)
                    act.activation(group_cols((v_sel_hi if slab == 7 else v_win_hi)[:, x, :]),
                                   src.rearrange("p (g d) -> p g d", d=DH), ACT.Copy).then_inc(n_hi_ready, 1)
                else:
                    act.activation((k_sel if slab == 6 else k_win)[0][0][:, x * T:(x + 1) * T], src,
                                   ACT.Copy).then_inc(n_hi_ready, 1)
                act_split(act, half0[4] + o + HALF_SLOTS)
                if o == 4:
                    act.wait_ge(nsa_gates_done, 1)
                    act.activation(n_gates, ps[:, 4, 0:96].rearrange("p (a b) -> p a b", a=NT), ACT.Copy,
                                   scale=1.0 / ALPHA).then_inc(n_gates_raw, 1)
                if o == 7:
                    act.wait_ge(n_gates_turned, 1)
                    act.activation(n_gates, ps[:, 5, 0:96].rearrange("p (a b) -> p a b", a=NT),
                                   ACT.Sigmoid).then_inc(n_gates_ready, 1)
                if o == 9:
                    act_table(act, ACT.Gelu_apprx_tanh)
                    act.wait_ge(hid_done, 2)
                    link(act, act_chain, "act", act.activation(hid_bias, ps[:, 6, 60:61 + P:P], ACT.Copy))
                    for z in range(2):
                        act.activation(hidT[:, z, :], ps[:, 6, z * P:z * P + 60], ACT.Gelu_apprx_tanh,
                                       bias=hid_bias[:, z:z + 1]).then_inc(hid_ready, 1)
                    act_table(act, ACT.Exp)
                if o == 12:
                    act.wait_ge(kc_done, 1)
                    act.wait_ge(n_zeros_ready, 1)
                    for h in range(2):
                        rows = slice(DH * h, DH * h + DH)
                        act.activation(kc_hi[rows, :, h * N_CMP:(h + 1) * N_CMP],
                                       ps[rows, 7, 0:60].rearrange("p (g n) -> p g n", g=N_GROUPS),
                                       ACT.Copy).then_inc(kc_hi_ready, 1)
                if o == 15:
                    act.wait_ge(c_arg_ready, 1)
                    act.activation(c_score, c_score, ACT.Exp).then_inc(c_exp_ready, 1)
                if o == 19:
                    act.wait_ge(c_turned, 1)
                    act.activation(c_probT[0:8 * N_CMP, :, :], ps[0:8 * N_CMP, 5, :].rearrange("p (a b) -> p a b", a=2),
                                   ACT.Copy).then_inc(c_probT_ready, 1)
            act_attention(act, A_HEADS, 2 * N_HEADS, n_bufs)
            act_mix_all(act, 0, reverse=True)

        def dve_nsa(dve):
            def chain(ins):
                link(dve, dve_chain, "dve", ins)

            by_head = c_score.rearrange("p a (h n) -> p (a h) n", n=N_CMP)
            c_m, c_s = (x.rearrange("p a h -> p (a h)") for x in (c_max, c_sum))
            score = c_score.rearrange("p a (h n) -> p a h n", n=N_CMP)
            for o in range(20):
                slab, x = o // 2, o % 2
                src = ps[:, o % 4, 0:T]
                if slab >= 2:
                    dve.wait_ge(n_hi_ready, o - 3)
                    if slab < 6:
                        hi, lo = (v[:, o - 4, :].rearrange("p (a n) -> p a n", a=NT) for v in (q_hi, q_lo))
                        dve.scalar_tensor_tensor(lo, src.rearrange("p (a n) -> p a n", a=NT)[:, :, ::-1], QK_SCALE,
                                                 hi.bitcast(F32), ALU.mult, ALU.subtract).then_inc(evac_done, 1)
                    elif slab in (7, 9):
                        hi, lo = (group_cols(v[:, x, :])
                                  for v in ((v_sel_hi, v_sel_lo) if slab == 7 else (v_win_hi, v_win_lo)))
                        dve.tensor_tensor(lo, src.rearrange("p (g d) -> p g d", d=DH), hi.bitcast(F32),
                                          ALU.subtract).then_inc(evac_done, 1)
                    else:
                        hi, lo = (v[0][:, x * T:(x + 1) * T] for v in (k_sel if slab == 6 else k_win))
                        dve.tensor_tensor(lo, src, hi.bitcast(F32), ALU.subtract).then_inc(evac_done, 1)
                dve_split(dve, half0[4] + o + HALF_SLOTS)
                if o == 9:
                    dve.wait_ge(hid_ready, 2)
                    dve.tensor_copy(hid_heads.rearrange("p (g q) n -> p g q n", g=N_GROUPS),
                                    bc(hidT[:, 1, :].rearrange("p (g n) -> p g n", g=N_GROUPS), 2, 4)).then_inc(hid_spread, 1)
                if o == 12:
                    for h in range(2):
                        rows, cols = slice(DH * h, DH * h + DH), slice(h * N_CMP, (h + 1) * N_CMP)
                        dve.wait_ge(kc_hi_ready, 2)
                        dve.tensor_tensor(kc_lo[rows, :, cols], ps[rows, 7, 0:60].rearrange("p (g n) -> p g n", g=N_GROUPS),
                                          kc_hi[rows, :, cols].bitcast(F32), ALU.subtract).then_inc(kc_ready, 1)
                    dve.wait_ge(vc_done, 1)
                    for half in range(2):
                        last = dve.tensor_tensor(c_val[0:120, half, :].rearrange("p (h d) -> p h d", d=DH),
                                                 bc(ps[0:120, 6, half * DH:(half + 1) * DH], 1, 8),
                                                 bc(const("own_head", 120), 2, DH), ALU.mult)
                    last.then_inc(vc_ready, 1)
                if o == 14:
                    first = P // CMP_STRIDE - 1
                    dve.memset(score[:, 0, :, first:], MASKED)
                    dve.wait_ge(bias_ready, 1)
                    dve.wait_ge(c_scores_done, 1)
                    raw_score = ps[:, 4, 0:480].rearrange("p (a h n) -> p a h n", a=NT, n=N_CMP)
                    dve.tensor_tensor(score[:, 0, :, 0:first], raw_score[:, 0, :, 0:first],
                                      bias[:, :, P + CMP_LEN - 1:T:CMP_STRIDE], ALU.add)
                    dve.tensor_tensor(score[:, 1, :, :], raw_score[:, 1, :, :], bias[:, :, CMP_LEN - 1:T:CMP_STRIDE],
                                      ALU.add).then_inc(c_scores_read, 1)
                    dve.wait_ge(c_scores_read, 1)
                    chain(dve.tensor_reduce(c_m, by_head, AX, ALU.max))
                    dve.tensor_tensor(by_head, by_head, bc(c_m, 2, N_CMP), ALU.subtract).then_inc(c_arg_ready, 1)
                if o == 16:
                    dve.wait_ge(c_exp_ready, 1)
                    chain(dve.tensor_reduce(c_s, by_head, AX, ALU.add))
                    for a in range(NT):
                        last = dve.tensor_tensor(score[:, a, :, :], score[:, a, :, :],
                                                 bc(const("cmp_valid")[:, a * N_CMP:(a + 1) * N_CMP], 1, N_HEADS), ALU.mult)
                    chain(last)
                    chain(dve.reciprocal(c_s, c_s))
                    dve.wait_ge(n_gates_ready, 1)
                    chain(dve.tensor_tensor(c_sum, c_sum, n_gates.rearrange("p a (h b) -> p a h b", b=3)[:, :, :, 0],
                                            ALU.mult))
                    dve.tensor_tensor(by_head, by_head, bc(c_s, 2, N_CMP), ALU.mult).then_inc(c_prob_ready, 1)
            dve_attention(dve, A_HEADS, 2 * N_HEADS, lambda i: bias[:, i % N_HEADS, :], n_bufs)
            dve_mix_all(dve, 4, reverse=True)

        N_LEVELS = len(LEVELS)
        r_gain_landed = sem("r_gain_landed")
        lb_arg = sem("lb_arg")
        lb_exp = sem("lb_exp")
        f_ready = sem("f_ready")
        logf_ready = sem("logf_ready")
        k_ready = sem("k_ready")
        level_arg = sem("level_arg")
        level_exp = sem("level_exp")
        level_ready = sem("level_ready")
        level_scored = sem("level_scored")
        level_placed = sem("level_placed")
        diag_done = sem("diag_done")
        diag_ready = sem("diag_ready")
        cross_ready = sem("cross_ready")
        r_out_done = sem("r_out_done")
        r_sq_ready = sem("r_sq_ready")
        r_var_ready = sem("r_var_ready")
        r_std_ready = sem("r_std_ready")
        r_silu_ready = sem("r_silu_ready")
        r_gate_ready = sem("r_gate_ready")
        r_o_ready = sem("r_o_ready")
        level_buf = (xc, sq)

        def halves(v, m):
            return v.rearrange("p a b -> p (a b)").rearrange("p (n b m) -> p n b m", b=2, m=m)

        def tiles(v):
            return v.rearrange("p a b -> p (a b)").rearrange("p (i n) -> p i n", n=P)

        def level_bank(u):
            b = 4 + 2 * (u % 2)
            return ps[:, b:b + 2, :]

        def pool_hgrn(pool):
            pool.wait_ge(x_ready, x_count(4))
            pool.dma_start(r_gain, spread(io["hgrn_norm_gain_2"][0], P)).then_inc(r_gain_landed, 16)
            pool_norm(pool, 6)
            pool.wait_ge(evac_done, EV_H + 16)
            pool.wait_ge(k_ready, 1)
            for u in range(N_LEVELS + 1):
                pool.wait_ge(level_exp, u + 1)
                m = LEVELS[u] if u < N_LEVELS else P
                y, k, q = (halves(v, m) for v in (level_buf[u % 2][:, :, :], r_k, r_q))
                pool.tensor_tensor(y[:, :, 0, :], y[:, :, 0, :], k[:, :, 0, :], ALU.mult)
                pool.tensor_tensor(y[:, :, 1, :], y[:, :, 1, :], q[:, :, 1, :], ALU.mult).then_inc(level_ready, 1)
            pool.wait_ge(r_silu_ready, 1)
            pool.wait_ge(r_gain_landed, 16)
            g = r_g.rearrange("p a (h d) -> p (a h) d", d=P)
            pool.tensor_tensor(g, g, bc(r_gain, 1, NT * H_HEADS), ALU.mult).then_inc(r_gate_ready, 1)

        def pe_hgrn(pe):

            def level(u):
                pe.wait_ge(level_ready, u + 1)
                if u < 2:
                    pe.wait_ge(diag_ready, 1)
                else:
                    pe.wait_ge(level_placed, u - 1)
                y = tiles(level_buf[u % 2][:, :, :])
                for i in range(2 * H_HEADS):
                    odd = y[:, i, :].rearrange("p (n b m) -> p n b m", b=2, m=LEVELS[u])[:, :, 1, :]
                    dst = level_bank(u)[:, i // 8, (i % 8) * 64:(i % 8 + 1) * 64]
                    last = pe.matmul(dst.rearrange("p (n m) -> p n m", m=LEVELS[u]), y[:, i, :], odd, start=True, stop=True)
                last.then_inc(level_scored, 1)

            for o in range(0, 32, 2):
                if o == 0:
                    pe_first_tiles(pe, half0[8], 2, 6)
                elif o < 16:
                    pe_tile_channels(pe, half0[8], EV_H, o)
                    pe_tile_channels(pe, half0[8], EV_H, o + 1)
                else:
                    pe_tile_tokens(pe, half0[8], EV_H, o)
                if o == 16:
                    pe.wait_ge(evac_done, EV_H + 16)
                    pe.wait_ge(k_ready, 1)
                    for i in range(2 * H_HEADS):
                        last = pe.matmul(ps[:, 4 + i // 4, (i % 4) * P:(i % 4 + 1) * P], tiles(r_k)[:, i, :],
                                         tiles(r_q)[:, i, :], start=True, stop=True)
                    last.then_inc(diag_done, 1)
                if o >= 18:
                    level((o - 18) // 2)
            pe.wait_ge(level_ready, N_LEVELS + 1)
            pe.wait_ge(level_placed, N_LEVELS - 1)
            y = level_buf[N_LEVELS % 2]
            for h in range(H_HEADS):
                last = pe.matmul(level_bank(N_LEVELS)[:, h // 4, (h % 4) * P:(h % 4 + 1) * P], y[:, h, 0:P], y[:, h, P:T],
                                 start=True, stop=True)
            last.then_inc(level_scored, 1)
            pe.wait_ge(level_placed, N_LEVELS)
            pe.wait_ge(evac_done, EV_H + 24)
            for a in range(NT):
                if a == 1:
                    pe.wait_ge(cross_ready, 1)
                for h in range(H_HEADS):
                    dst = ps[:, 4 + 2 * a + h // 4, (h % 4) * P:(h % 4 + 1) * P]
                    cols = slice(h * P, (h + 1) * P)
                    if a == 1:
                        pe.matmul(dst, r_cross[:, h, :], r_v[:, 0, cols], start=True, stop=False)
                    last = pe.matmul(dst, r_at[:, 2 * h + a, :], r_v[:, a, cols], start=a == 0, stop=True)
                last.then_inc(r_out_done, 1)
            pe.wait_ge(evac_done, EV_H + 32)
            pe_turn_mix(pe)

        def act_hgrn(act):
            act.wait_ge(lb_arg, 1)
            act.activation(lb[:, 0:2, :], lb[:, 0:2, :], ACT.Exp).then_inc(lb_exp, 1)

            def exps(u):
                act.wait_ge(level_arg, u + 1)
                buf = level_buf[u % 2][:, :, :]
                act.activation(buf, buf, ACT.Exp).then_inc(level_exp, 1)

            for o in range(32):
                slab, x = o // 2, o % 2
                src = ps[:, o % 4, 0:T]
                if slab >= 8 and x == 0:
                    act.wait_ge(token_tile, TT_H + slab - 7)
                else:
                    act.wait_ge(half_done, half0[8] + o + 1)
                if slab < 4:
                    act.activation(r_k[:, o, :], src, ACT.Sigmoid, scale=-1.0)
                    act.activation(r_b[:, o, :], src, ACT.Sigmoid).then_inc(evac_done, 1)
                elif slab < 8:
                    act.activation(r_q[:, o - 8, :], src, ACT.Silu).then_inc(evac_done, 1)
                else:
                    act.activation((r_v if slab < 12 else r_g)[:, x, 256 * (slab % 4):256 * (slab % 4 + 1)], src,
                                   ACT.Copy).then_inc(evac_done, 1)
                act_split(act, half0[8] + o + HALF_SLOTS)
                if o == 7:
                    act.wait_ge(f_ready, 1)
                    for h in range(H_HEADS):
                        act.activation(r_b[:, h, :], r_b[:, h, :], ACT.Ln, scale=lb[:, 3, h:h + 1],
                                       bias=lb[:, 2, h:h + 1]).then_inc(logf_ready, 1)
                if o == 15:
                    exps(0)
                    exps(1)
                if 19 <= o < 31 and o % 2:
                    exps((o - 19) // 2 + 2)
            act.wait_ge(evac_done, EV_H + 32)
            act.activation(r_g, r_g, ACT.Silu).then_inc(r_silu_ready, 1)
            act_table(act, ACT.Sqrt)
            act.wait_ge(level_scored, N_LEVELS + 1)
            act.activation(r_cross.rearrange("p (b h) n -> p b (h n)", b=2), level_bank(N_LEVELS), ACT.Copy).then_inc(cross_ready, 1)
            for a in range(NT):
                act.wait_ge(r_out_done, a + 1)
                act.activation(xc[:, 4 * a:4 * a + 4, :].rearrange("p a b -> p (a b)"),
                               ps[:, 4 + 2 * a:6 + 2 * a, :].rearrange("p a b -> p (a b)"), ACT.Square).then_inc(r_sq_ready, 1)
                act.wait_ge(r_var_ready, a + 1)
                act.activation(r_rr[:, 8 * a:8 * a + 8], r_ss[:, 8 * a:8 * a + 8], ACT.Sqrt).then_inc(r_std_ready, 1)
            act_mix_all(act, 1)

        def dve_hgrn(dve):
            def chain(ins):
                link(dve, dve_chain, "dve", ins)

            raw0, raw1 = par[:, LB:LB + 8], par[:, LB + 8:LB + 16]
            e0, e1, low, top = (lb[:, n, :] for n in range(4))
            chain(dve.tensor_tensor(low, raw0, raw1, ALU.max))
            dve.tensor_tensor(e0, raw0, low, ALU.subtract)
            dve.tensor_tensor(e1, raw1, low, ALU.subtract).then_inc(lb_arg, 1)
            dve.wait_ge(lb_exp, 1)
            chain(dve.tensor_tensor(top, e0, e1, ALU.add))
            chain(dve.reciprocal(top, top))
            dve.tensor_tensor(e0, e0, top, ALU.mult)
            chain(dve.tensor_tensor(e1, e1, top, ALU.mult))
            chain(dve.tensor_tensor(low, e0, e1, ALU.add))
            chain(dve.tensor_tensor(low, low, e0, ALU.subtract))
            chain(dve.tensor_scalar(top, low, -1.0, 1.0, ALU.mult, ALU.add))

            def args(u):
                if u == 0:
                    dve.wait_ge(x_scaled, 5)
                if u >= 2:
                    dve.wait_ge(level_scored, u - 1)
                m = LEVELS[u] if u < N_LEVELS else P
                e, b = (halves(v, m) for v in (level_buf[u % 2][:, :, :], r_b))
                ref = b[:, :, 0, m - 1:m].to_broadcast([P, H_HEADS * T // (2 * m), m])
                dve.tensor_tensor(e[:, :, 0, :], ref, b[:, :, 0, :], ALU.subtract)
                if u < N_LEVELS:
                    dve.tensor_tensor(e[:, :, 1, :], b[:, :, 1, :], ref, ALU.subtract).then_inc(level_arg, 1)
                else:
                    dve.tensor_copy(e[:, :, 1, :], b[:, :, 1, :]).then_inc(level_arg, 1)

            def place(u):
                dve.wait_ge(level_scored, u + 1)
                if u:
                    dve.wait_ge(level_placed, u)
                m = LEVELS[u]
                mask = const("levels")[:, u * 64:(u + 1) * 64].bitcast(I32)
                mask = bc(mask, 1, 2 * H_HEADS).rearrange("p a (n m) -> p a n m", m=m)
                dst = r_at.rearrange("p a (n b m) -> p a n b m", b=2, m=m)[:, :, :, 1, :]
                src = level_bank(u).rearrange("p b (i n m) -> p (b i) n m", n=64 // m, m=m)
                dve.copy_predicated(dst, mask, src).then_inc(level_placed, 1)

            for o in range(32):
                dve_split(dve, half0[8] + o + HALF_SLOTS)
                if o >= 19 and o % 2:
                    u = (o - 19) // 2
                    if u + 2 <= N_LEVELS:
                        args(u + 2)
                    place(u)
                if o == 7:
                    dve.wait_ge(evac_done, EV_H + 8)
                    dve.tensor_scalar(r_b, r_b, TINY, None, ALU.max).then_inc(f_ready, 1)
                    dve.tensor_tensor(r_k, r_k, bc(top, 2, T), ALU.mult).then_inc(k_ready, 1)
                if o == 9:
                    for h in range(H_HEADS):
                        dve.wait_ge(logf_ready, h + 1)
                        last = dve.tensor_tensor_scan(r_b[:, h, :], const("restart"), r_b[:, h, :], 0.0, ALU.mult, ALU.add)
                    chain(last)
                if o in (10, 11):
                    args(o - 10)
                if o == 17:
                    dve.wait_ge(diag_done, 1)
                    dve.tensor_tensor(r_at, ps[:, 4:8, :].rearrange("p b (i n) -> p (b i) n", n=P),
                                      bc(ident, 1, 2 * H_HEADS), ALU.mult).then_inc(diag_ready, 1)
                    dve.wait_ge(diag_ready, 1)
            for a in range(NT):
                dve.wait_ge(r_sq_ready, a + 1)
                cols = slice(8 * a, 8 * a + 8)
                chain(dve.tensor_reduce(r_ss[:, cols], xc[:, 4 * a:4 * a + 4, :].rearrange("p a b -> p (a b)")
                                        .rearrange("p (h d) -> p h d", d=P), AX, ALU.add))
                dve.tensor_scalar(r_ss[:, cols], r_ss[:, cols], 1.0 / P, RMS_EPS, ALU.mult, ALU.add).then_inc(r_var_ready, 1)
                dve.wait_ge(r_std_ready, a + 1)
                chain(dve.reciprocal(r_rr[:, cols], r_rr[:, cols]))
                chain(dve.tensor_tensor(r_o[:, a, :].rearrange("p (h d) -> p h d", d=P),
                                        ps[:, 4 + 2 * a:6 + 2 * a, :].rearrange("p b (h d) -> p (b h) d", d=P),
                                        bc(r_rr[:, cols], 2, P), ALU.mult))
                if a == 0:
                    dve.wait_ge(r_gate_ready, 1)
                dve.tensor_tensor(r_o[:, a, :], r_o[:, a, :], r_g[:, a, :], ALU.mult).then_inc(r_o_ready, 1)
            dve_mix_all(dve, 8)

        block = ctx.enter_context(nc.Block())

        @block.sync
        def _(sp):
            def load(slab, matrix, ap):
                dst = raw[:, slab % RAW_SLOTS, :]
                if matrix < 2:
                    dst = dst.rearrange("p (k n) -> p k n", k=KC)
                    src = ap.rearrange("(k p) n -> p k n", p=P)
                else:
                    dst = dst.rearrange("p (c n) -> p c n", c=2)
                    src = ap.rearrange("(c p) n -> p c n", p=P)
                sp.dma_start(dst, src).then_inc(raw_landed[slab % RAW_SLOTS], 16)

            sp.dma_start(x_tok, io["x"][0].rearrange("(a p) d -> p a d", p=P)).then_inc(x_landed, 16)
            sp.dma_start(consts[:, 0:N_FIRST], io["shape_constants"][:, 0:N_FIRST]).then_inc(ident_landed, 16)
            for n, e in enumerate(plan):
                if e[0] == "lin":
                    for i, col in enumerate(e[2]):
                        slab = slab0[n] + i
                        if slab == 1:
                            sp.wait_ge(pool_rows_landed, 16 * N_POOL_ROWS)
                        if slab >= RAW_SLOTS:
                            sp.wait_ge(lo_ready, raw_freed(slab - RAW_SLOTS))
                        load(slab, 0, e[1][:, col:col + 256])
                    continue
                for m in range(3):
                    sp.wait_ge(lo_ready, raw_freed(slab0[n] + m - RAW_SLOTS))
                    w = e[1][m]
                    load(slab0[n] + m, m, w[:, 0:256] if m < 2 else w[0:256, :])
                with sp.Fori(1, FFN_STEPS) as j:
                    for m in range(3):
                        sp.wait_ge(lo_ready, j * 6 + (half0[n] - 6 + LAST_OF[m]))
                        w = e[1][m]
                        load(slab0[n] + m, m, w[:, bass.ds(j * 256, 256)] if m < 2 else w[bass.ds(j * 256, 256), :])
            for b in range(2):
                sp.wait_ge(out_ready, b + 1)
                sp.wait_ge(out_odd_ready, b + 1)
                cols = slice(b * D // 2, (b + 1) * D // 2)
                sp.dma_start(out[0][:, cols].rearrange("(a p) d -> p a d", p=P), out_tok[:, :, cols]).then_inc(stored, 16)
            sp.wait_ge(stored, 32)

        row_sources = [
            (0, 0, io["ln1_g"].rearrange("a (k p) -> (a k) p", p=P)),
            (0, LN2, io["ln2_g"].rearrange("a (k p) -> (a k) p", p=P)),
            (0, LNG, io["ln_gain_2"].rearrange("i j (k p) -> (i j k) p", p=P)),
            (0, LNB, io["ln_bias_2"].rearrange("i j (k p) -> (i j k) p", p=P)),
            (1, 0, io["m_conv"].rearrange("a j (c p) -> (a j c) p", p=P)),
            (1, PSCALE - MCONV, io["pool_scale"].rearrange("a (c p) -> (a c) p", p=P)),
            (1, LB - MCONV, io["hgrn_lb_2"].rearrange("i (k p) -> (i k) p", p=P)),
            (1, FCONV - MCONV, io["ffn_conv"][0, 0:2].rearrange("j (c p) -> (j c) p", p=P)),
            (2, 0, io["ffn_conv"][0, 2:3].rearrange("j (c p) -> (j c) p", p=P)),
            (2, CPOS - FCONV - 88, io["nsa_cmp_pos_2"][0].rearrange("z (l q) d -> (z l) (q d)", q=2)),
        ]
        N_SMALL_DMAS = 14

        def spread(ap, n):
            return bass.AP(tensor=ap.tensor, offset=ap.offset, ap=[[0, P], [1, n]])

        @block.gpsimd
        def _(pool):
            for g, row, src in row_sources[:N_POOL_ROWS]:
                pool.dma_start(rows[row:row + src.shape[0], g, :], src).then_inc(pool_rows_landed, 16)
            pool.memset(m_v[:, :, :, DH:DH + 1], 1.0).then_inc(ones_ready, 1)
            for x in (av_hi, av_lo):
                pool.memset(x[:, :, :, DH:2 * DH].bitcast(F32), 0.0)
            pool.memset(pool_w, 0.0).then_inc(pads_ready, 1)
            pool.wait_ge(pads_ready, 1)
            small = [(gate_w, w_in[:, 1280:1288].rearrange("(k p) n -> p k n", p=P)),
                     (hot, io["distance_buckets"]), (table, io["rel_bias_2"]),
                     (gate_w2[:, :, :], n_in[:, 2560:2608].rearrange("(k p) n -> p k n", p=P)),
                     (w2_k[:, 0, :], io["nsa_cmp_w2_2"][0, 0]), (w2_k[:, 1, :], io["nsa_cmp_w2_2"][0, 0]),
                     (w2_v[:, :], io["nsa_cmp_w2_2"][0, 1]),
                     (mng, spread(io["m_norm_g"][0], 256)),
                     (gate_bias[:, 0:1], io["m_b_i"].rearrange("a h -> h a")),
                     (gate_bias[:, 1:2], io["m_b_f"].rearrange("a h -> h a"))]
            small += [(pool_w[64 * (g % 2):64 * (g % 2) + 64, g // 2, 64 * (g % 2):64 * (g % 2) + 64],
                       io["pool_w"][0, g]) for g in range(4)]
            for dst, src in small:
                pool.dma_start(dst, src).then_inc(small_landed, 16)
            assert len(small) == N_SMALL_DMAS
            pool.wait_ge(rows_evac, 1)
            pool.dma_start(scratch, bias_row).then_inc(rows_stored, 16)
            pool_first(pool)
            pool_norm(pool, 2)
            pool_load_nsa(pool)
            pool_nsa(pool)
            pool_norm(pool, 4)
            pool_norm(pool, 5)
            pool_hgrn(pool)
            pool_norm(pool, 7)
            pool_norm(pool, 8)
            pool.wait_ge(rows_stored, 16)

        @block.scalar
        def _(act):
            for g, row, src in row_sources[N_POOL_ROWS:]:
                act.dma_start(rows[row:row + src.shape[0], g, :], src).then_inc(rows_landed, 16)
            for n, name in ((AQ, "a_q_g"), (AK, "a_k_g")):
                for twice in range(2):
                    act.dma_start(rows[n - MCONV:n - MCONV + 1, 1, twice * DH:(twice + 1) * DH],
                                   io[name]).then_inc(rows_landed, 16)
            act.dma_start(consts[:, N_FIRST:], io["shape_constants"][:, N_FIRST:]).then_inc(const_landed, 16)
            act.wait_ge(ident_landed, 16)
            for b in range(4):
                act_squares(act, 0, b)
            for h in range(2):
                act_split(act, h)
            act_norm(act, 0)
            for h in range(2, HALF_SLOTS):
                act_split(act, h)
            act_first(act)
            act_project(act, 1, 0)
            act_norm(act, 1)
            act_split(act, half0[2] + 4)
            act_split(act, half0[2] + 5)
            act_ffn(act, 2, 1)
            act_norm(act, 2)
            act_split(act, half0[3] + 4)
            act_split(act, half0[3] + 5)
            act_ffn(act, 3, 2)
            act_norm(act, 3)
            act_split(act, half0[4] + 4)
            act_split(act, half0[4] + 5)
            act_nsa(act)
            act_project(act, 5, 3)
            act_norm(act, 4)
            act_split(act, half0[6] + 4)
            act_split(act, half0[6] + 5)
            act_ffn(act, 6, 4)
            act_norm(act, 5)
            act_split(act, half0[7] + 4)
            act_split(act, half0[7] + 5)
            act_ffn(act, 7, 5)
            act_norm(act, 6)
            act_split(act, half0[8] + 4)
            act_split(act, half0[8] + 5)
            act_hgrn(act)
            act_project(act, 9, 6)
            act_norm(act, 7)
            act_split(act, half0[10] + 4)
            act_split(act, half0[10] + 5)
            act_ffn(act, 10, 7)
            act_norm(act, 8)
            act_finish(act)

        @block.vector
        def _(dve):
            dve_start(dve)
            for h in range(2):
                dve_split(dve, h)
            dve_norm(dve, 0)
            for h in range(2, HALF_SLOTS):
                dve_split(dve, h)
            dve_first(dve)
            dve_project(dve, 1, 0, 0)
            dve_norm(dve, 1)
            dve_split(dve, half0[2] + 4)
            dve_split(dve, half0[2] + 5)
            dve_ffn(dve, 2, 1, 0)
            dve_norm(dve, 2)
            dve_split(dve, half0[3] + 4)
            dve_split(dve, half0[3] + 5)
            dve_ffn(dve, 3, 2, 1)
            dve_norm(dve, 3)
            dve_split(dve, half0[4] + 4)
            dve_split(dve, half0[4] + 5)
            dve_nsa(dve)
            dve_project(dve, 5, 3, 2)
            dve_norm(dve, 4)
            dve_split(dve, half0[6] + 4)
            dve_split(dve, half0[6] + 5)
            dve_ffn(dve, 6, 4, 3)
            dve_norm(dve, 5)
            dve_split(dve, half0[7] + 4)
            dve_split(dve, half0[7] + 5)
            dve_ffn(dve, 7, 5, 4)
            dve_norm(dve, 6)
            dve_split(dve, half0[8] + 4)
            dve_split(dve, half0[8] + 5)
            dve_hgrn(dve)
            dve_project(dve, 9, 6, 5)
            dve_norm(dve, 7)
            dve_split(dve, half0[10] + 4)
            dve_split(dve, half0[10] + 5)
            dve_ffn(dve, 10, 7, 6)
            dve_norm(dve, 8)
            dve_finish(dve)

        @block.tensor
        def _(pe):
            pe_start(pe)
            for b in range(4):
                pe_stats(pe, 0, b)
            pe_params(pe)
            pe_first(pe)
            pe_project(pe, 1, 0)
            pe_ffn(pe, 2, 1)
            pe_ffn(pe, 3, 2)
            pe_nsa(pe)
            pe_project(pe, 5, 3)
            pe_ffn(pe, 6, 4)
            pe_ffn(pe, 7, 5)
            pe_hgrn(pe)
            pe_project(pe, 9, 6)
            pe_ffn(pe, 10, 7)
            pe_finish(pe)


_INS = ["x", "ln1_g", "w_in", "pool_w", "pool_scale", "m_conv", "m_b_i", "m_b_f", "m_norm_g", "a_q_g", "a_k_g",
        "w_out", "ln2_g", "w_up", "ffn_conv", "w_down", "rel_bias_2", "ln_gain_2", "ln_bias_2", "ffn1_w_gate_2",
        "ffn1_w_up_2", "ffn1_w_down_2", "ffn2_w_gate_2", "ffn2_w_up_2", "ffn2_w_down_2", "nsa_w_in_2",
        "nsa_w_out_2", "nsa_cmp_pos_2", "nsa_cmp_w1_2", "nsa_cmp_w2_2", "hgrn_w_in_2", "hgrn_w_out_2",
        "hgrn_norm_gain_2", "hgrn_lb_2"]


def kernel(**inputs):
    import concourse.bacc as bacc
    from concourse.bass_utils import run_bass_kernel_spmd

    nc = bacc.Bacc("TRN2", target_bir_lowering=False, num_devices=1)
    arrays, io = {}, {}
    for name in _INS:
        arrays[name] = np.ascontiguousarray(inputs[name])
    arrays["shape_constants"], const_at = shape_constants()
    arrays["distance_buckets"] = distance_buckets()
    for name, a in arrays.items():
        io[name] = nc.dram_tensor(name, a.shape, mybir.dt.from_np(a.dtype), kind="ExternalInput").ap()
    out = nc.dram_tensor("out", (1, T, D), F32, kind="ExternalOutput").ap()
    build_program(nc, io, const_at, out)
    result = run_bass_kernel_spmd(nc, [arrays], core_ids=[0])
    return result.results[0]["out"]
```
